# Optimizing a Trainium2 kernel written in Bass

```python
import math
import jax
import jax.numpy as jnp
from jax import lax
import numpy as np

D_MODEL = 1024
BATCH = 1
SEQ = 1024
DEPTH = 1
DEC_BATCH = 8
DEC_SEQ = 1
PAST_LEN = 4096
PAGE_SIZE = 128

N_META = 16
SSD_HEADS = 8
SSD_HEAD_DIM = 64
SSD_WIDTH = SSD_HEADS * SSD_HEAD_DIM
SSD_GROUPS = 2
D_STATE = 64
CONV_W = 4
CONV_DIM = SSD_WIDTH + 2 * SSD_GROUPS * D_STATE
SSD_CHUNK = 128
MLA_HEADS = 8
QK_NOPE = 64
QK_ROPE = 32
QK_DIM = QK_NOPE + QK_ROPE
V_DIM = 64
MLA_WIDTH = MLA_HEADS * V_DIM
Q_LORA = 384
KV_LORA = 256
ROPE_THETA = 10000.0
Q_BLOCK = 128
ATTN_SCALE = QK_DIM ** -0.5
D_FF = -(-8 * D_MODEL // (3 * 256)) * 256
EPS = 1e-6
IN_COLS = SSD_WIDTH + CONV_DIM + SSD_HEADS + Q_LORA + KV_LORA + QK_ROPE
IN_SPLITS = (SSD_WIDTH, SSD_WIDTH + CONV_DIM, SSD_WIDTH + CONV_DIM + SSD_HEADS,
             SSD_WIDTH + CONV_DIM + SSD_HEADS + Q_LORA, IN_COLS - QK_ROPE)

kernel_name = 'hybrid_ssd_mla_meta_decoder_step'

def rmsnorm(x, g):
    xf = x.astype(jnp.float32)
    r = lax.rsqrt(jnp.mean(xf * xf, axis=-1, keepdims=True) + EPS)
    return (xf * r * g.astype(jnp.float32)).astype(x.dtype)

def rope_angles(pos):
    inv = ROPE_THETA ** (-jnp.arange(QK_ROPE // 2, dtype=jnp.float32) * (2.0 / QK_ROPE))
    ang = pos.astype(jnp.float32)[:, None] * inv[None, :]
    return jnp.cos(ang), jnp.sin(ang)

def apply_rope(x, cos, sin):
    xf = x.astype(jnp.float32)
    x1, x2 = xf[..., :QK_ROPE // 2], xf[..., QK_ROPE // 2:]
    return jnp.concatenate([x1 * cos - x2 * sin, x1 * sin + x2 * cos], axis=-1).astype(x.dtype)

def head_gain(g_nope, g_rope):
    return jnp.concatenate([g_nope, g_rope, g_rope], axis=-1)

def project(x, g, w):
    return jnp.split(rmsnorm(x, g) @ w, IN_SPLITS, axis=-1)

def causal_conv(xpad, w, b):
    L = xpad.shape[1] - (CONV_W - 1)
    out = b
    for k in range(CONV_W):
        out = out + xpad[:, k:k + L] * w[k]
    return out

def ssd_scan(x, dt, A, Bm, Cm, h0, chunk):
    b, l, h, p = x.shape
    n = Bm.shape[-1]
    c = l // chunk
    rep = h // Bm.shape[2]
    Bh = jnp.repeat(Bm.astype(jnp.float32), rep, axis=2).reshape(b, c, chunk, h, n)
    Ch = jnp.repeat(Cm.astype(jnp.float32), rep, axis=2).reshape(b, c, chunk, h, n)
    xf = x.astype(jnp.float32).reshape(b, c, chunk, h, p)
    dtc = dt.reshape(b, c, chunk, h)
    acs = jnp.cumsum(dtc * A, axis=2)
    seg = acs[:, :, :, None, :] - acs[:, :, None, :, :]
    causal = jnp.tril(jnp.ones((chunk, chunk), dtype=bool))[None, None, :, :, None]
    Lmat = jnp.exp(jnp.where(causal, seg, -jnp.inf))
    scores = jnp.einsum('bcihn,bcjhn->bcijh', Ch, Bh) * Lmat * dtc[:, :, None, :, :]
    y_diag = jnp.einsum('bcijh,bcjhp->bcihp', scores, xf)
    decay = jnp.exp(acs[:, :, -1:, :] - acs)
    states = jnp.einsum('bcjhn,bcjh,bcjhp->bchpn', Bh, decay * dtc, xf)
    chunk_decay = jnp.exp(acs[:, :, -1, :])

    def step(hc, inp):
        st, dec = inp
        return hc * dec[:, :, None, None] + st, hc

    h_final, h_in = lax.scan(step, h0.astype(jnp.float32),
                             (jnp.transpose(states, (1, 0, 2, 3, 4)), jnp.transpose(chunk_decay, (1, 0, 2))))
    h_in = jnp.transpose(h_in, (1, 0, 2, 3, 4))
    y_off = jnp.einsum('bcihn,bchpn,bcih->bcihp', Ch, h_in, jnp.exp(acs))
    return (y_diag + y_off).reshape(b, l, h, p), h_final

def ssd_branch(z, xpad, dt_raw, h0, segments, conv_w, conv_b, dt_bias, a_log, d_skip, norm_g):
    xa = jax.nn.silu(causal_conv(xpad, conv_w, conv_b))
    b, t = xa.shape[:2]
    gn = SSD_GROUPS * D_STATE
    xs = xa[..., :SSD_WIDTH].reshape(b, t, SSD_HEADS, SSD_HEAD_DIM)
    Bm = xa[..., SSD_WIDTH:SSD_WIDTH + gn].reshape(b, t, SSD_GROUPS, D_STATE)
    Cm = xa[..., SSD_WIDTH + gn:].reshape(b, t, SSD_GROUPS, D_STATE)
    dt = jax.nn.softplus(dt_raw.astype(jnp.float32) + dt_bias.astype(jnp.float32))
    A = -jnp.exp(a_log.astype(jnp.float32))
    ys = []
    h = h0.astype(jnp.float32)
    start = 0
    for length, chunk in segments:
        sl = slice(start, start + length)
        y, h = ssd_scan(xs[:, sl], dt[:, sl], A, Bm[:, sl], Cm[:, sl], h, chunk)
        ys.append(y)
        start += length
    y = jnp.concatenate(ys, axis=1)
    y = y + d_skip.astype(jnp.float32)[:, None] * xs.astype(jnp.float32)
    y = y.reshape(b, t, SSD_WIDTH) * jax.nn.silu(z.astype(jnp.float32))
    yg = y.reshape(b, t, SSD_GROUPS, SSD_WIDTH // SSD_GROUPS)
    yg = yg * lax.rsqrt(jnp.mean(yg * yg, axis=-1, keepdims=True) + EPS)
    out = (yg.reshape(b, t, SSD_WIDTH) * norm_g.astype(jnp.float32)).astype(z.dtype)
    return out, h, xpad[:, -(CONV_W - 1):]

def mla_queries(c_q, g_qn, w_uq, cos, sin, gq):
    b, t = c_q.shape[:2]
    q = (rmsnorm(c_q, g_qn) @ w_uq).reshape(b, t, MLA_HEADS, QK_DIM)
    q = jnp.concatenate([q[..., :QK_NOPE], apply_rope(q[..., QK_NOPE:], cos, sin)], axis=-1)
    return rmsnorm(q, gq)

def mla_keys_values(lat, kr, w_ukv, gk):
    b, t = lat.shape[:2]
    kv = (lat @ w_ukv).reshape(b, t, MLA_HEADS, QK_NOPE + V_DIM)
    kr_h = jnp.broadcast_to(kr[:, :, None, :], (b, t, MLA_HEADS, QK_ROPE)).astype(kv.dtype)
    k = jnp.concatenate([kv[..., :QK_NOPE], kr_h], axis=-1)
    return rmsnorm(k, gk), kv[..., QK_NOPE:]

def block_causal_attention(q, k, v):
    b, t, h, _ = q.shape
    nb = -(-t // Q_BLOCK)
    tp = nb * Q_BLOCK
    pad = ((0, 0), (0, tp - t), (0, 0), (0, 0))
    qp, kp, vp = jnp.pad(q, pad), jnp.pad(k, pad), jnp.pad(v, pad)
    kpos = jnp.arange(tp)

    def blk(start):
        qb = lax.dynamic_slice_in_dim(qp, start, Q_BLOCK, axis=1)
        s = jnp.einsum('bqhd,bkhd->bhqk', qb, kp).astype(jnp.float32) * ATTN_SCALE
        qpos = start + jnp.arange(Q_BLOCK)
        s = jnp.where(kpos[None, :] <= qpos[:, None], s, -jnp.inf)
        p = jax.nn.softmax(s, axis=-1)
        return jnp.einsum('bhqk,bkhd->bqhd', p.astype(vp.dtype), vp)

    o = lax.map(blk, jnp.arange(nb) * Q_BLOCK)
    return jnp.transpose(o, (1, 0, 2, 3, 4)).reshape(b, tp, h, V_DIM)[:, :t]

def paged_attention(q, k_new, v_new, lat_pool, kr_pool, layer, page_table, w_ukv, gk):
    b, s, h, _ = q.shape
    qf = q.astype(jnp.float32)

    def update(carry, k, v, mask):
        m, l, acc = carry
        sc = jnp.einsum('bshd,bkhd->bhsk', qf, k.astype(jnp.float32)) * ATTN_SCALE
        if mask is not None:
            sc = jnp.where(mask, sc, -jnp.inf)
        m_new = jnp.maximum(m, jnp.max(sc, axis=-1))
        p = jnp.exp(sc - m_new[..., None])
        corr = jnp.exp(m - m_new)
        acc = acc * corr[..., None] + jnp.einsum('bhsk,bkhd->bhsd', p, v.astype(jnp.float32))
        return m_new, l * corr + jnp.sum(p, axis=-1), acc

    def page_step(carry, pids):
        k, v = mla_keys_values(lat_pool[layer, pids], kr_pool[layer, pids], w_ukv, gk)
        return update(carry, k, v, None), None

    init = (jnp.full((b, h, s), -jnp.inf, jnp.float32), jnp.zeros((b, h, s), jnp.float32),
            jnp.zeros((b, h, s, V_DIM), jnp.float32))
    carry, _ = lax.scan(page_step, init, page_table.T)
    causal = jnp.tril(jnp.ones((s, s), dtype=bool))[None, None]
    m, l, acc = update(carry, k_new, v_new, causal)
    o = acc / l[..., None]
    return jnp.transpose(o, (0, 2, 1, 3)).astype(q.dtype)

def finish_layer(x, ssd_out, att, mla_out_g, w_out, ffn_norm_g, w_gate, w_up, w_down):
    b, t = x.shape[:2]
    mla_out = rmsnorm(att.reshape(b, t, MLA_WIDTH), mla_out_g)
    h = x + jnp.concatenate([ssd_out, mla_out], axis=-1) @ w_out
    n = rmsnorm(h, ffn_norm_g)
    return h + (jax.nn.silu(n @ w_gate) * (n @ w_up)) @ w_down

def setup_inputs(seed: int = 0) -> dict:
    key = jax.random.key(seed)
    ks = jax.random.split(key, 32)

    def nrm(i, shape, scale):
        return jax.random.normal(ks[i], shape, jnp.float32) * scale

    def gain(i, shape):
        return 1.0 + nrm(i, shape, 0.02)

    L = DEPTH
    n_pages = PAST_LEN // PAGE_SIZE
    n_used = DEC_BATCH * n_pages
    n_pool = n_used + max(1, n_used // 4)
    page_table = jax.random.permutation(ks[0], n_pool)[:n_used].reshape(DEC_BATCH, n_pages).astype(jnp.int32)
    dt0 = jnp.exp(jax.random.uniform(ks[1], (L, SSD_HEADS), jnp.float32,
                                     minval=math.log(1e-3), maxval=math.log(1e-1)))
    dt_bias = dt0 + jnp.log(-jnp.expm1(-dt0))
    a_log = jnp.log(jax.random.uniform(ks[2], (L, SSD_HEADS), jnp.float32, minval=1.0, maxval=16.0))
    mix = SSD_WIDTH + MLA_WIDTH
    return {
        'x_prompt': nrm(3, (BATCH, SEQ, D_MODEL), 1.0),
        'x_sample': nrm(4, (DEC_BATCH, DEC_SEQ, D_MODEL), 1.0),
        'cache_kv_latent': nrm(5, (L, n_pool, PAGE_SIZE, KV_LORA), 1.0),
        'cache_k_rope': nrm(6, (L, n_pool, PAGE_SIZE, QK_ROPE), 1.0),
        'state_conv': nrm(7, (L, DEC_BATCH, CONV_W - 1, CONV_DIM), 1.0),
        'state_ssm': nrm(8, (L, DEC_BATCH, SSD_HEADS, SSD_HEAD_DIM, D_STATE), 0.1),
        'page_table': page_table,
        'meta_tokens': nrm(9, (N_META, D_MODEL), 1.0),
        'attn_norm_g': gain(10, (L, D_MODEL)),
        'w_in': nrm(11, (L, D_MODEL, IN_COLS), D_MODEL ** -0.5),
        'conv_w': nrm(12, (L, CONV_W, CONV_DIM), CONV_W ** -0.5),
        'conv_b': nrm(13, (L, CONV_DIM), 0.02),
        'dt_bias': dt_bias,
        'a_log': a_log,
        'd_skip': gain(14, (L, SSD_HEADS)),
        'ssd_norm_g': gain(15, (L, SSD_WIDTH)),
        'q_norm_g': gain(16, (L, Q_LORA)),
        'w_uq': nrm(17, (L, Q_LORA, MLA_HEADS * QK_DIM), Q_LORA ** -0.5),
        'kv_norm_g': gain(18, (L, KV_LORA)),
        'w_ukv': nrm(19, (L, KV_LORA, MLA_HEADS * (QK_NOPE + V_DIM)), KV_LORA ** -0.5),
        'q_head_g_nope': gain(20, (L, QK_NOPE)),
        'q_head_g_rope': gain(21, (L, QK_ROPE // 2)),
        'k_head_g_nope': gain(22, (L, QK_NOPE)),
        'k_head_g_rope': gain(23, (L, QK_ROPE // 2)),
        'mla_out_g': gain(24, (L, MLA_WIDTH)),
        'w_out': nrm(25, (L, mix, D_MODEL), mix ** -0.5),
        'ffn_norm_g': gain(26, (L, D_MODEL)),
        'w_gate': nrm(27, (L, D_MODEL, D_FF), D_MODEL ** -0.5),
        'w_up': nrm(28, (L, D_MODEL, D_FF), D_MODEL ** -0.5),
        'w_down': nrm(29, (L, D_FF, D_MODEL), D_FF ** -0.5),
    }

def reference(x_prompt, x_sample, cache_kv_latent, cache_k_rope, state_conv, state_ssm, page_table,
              meta_tokens, attn_norm_g, w_in, conv_w, conv_b, dt_bias, a_log, d_skip, ssd_norm_g,
              q_norm_g, w_uq, kv_norm_g, w_ukv, q_head_g_nope, q_head_g_rope, k_head_g_nope,
              k_head_g_rope, mla_out_g, w_out, ffn_norm_g, w_gate, w_up, w_down):
    b = x_prompt.shape[0]
    hp = jnp.concatenate([jnp.broadcast_to(meta_tokens[None].astype(x_prompt.dtype), (b, N_META, D_MODEL)),
                          x_prompt], axis=1)
    hs = x_sample
    t = hp.shape[1]
    s = hs.shape[1]
    past = page_table.shape[1] * cache_kv_latent.shape[2]
    cos_p, sin_p = rope_angles(jnp.arange(t))
    cos_s, sin_s = rope_angles(past + jnp.arange(s))
    lat_p_l, kr_p_l, conv_p_l, ssm_p_l = [], [], [], []
    lat_s_l, kr_s_l, conv_s_l, ssm_s_l = [], [], [], []
    for l in range(DEPTH):
        gq = head_gain(q_head_g_nope[l], q_head_g_rope[l])
        gk = head_gain(k_head_g_nope[l], k_head_g_rope[l])
        ssd_w = (conv_w[l], conv_b[l], dt_bias[l], a_log[l], d_skip[l], ssd_norm_g[l])
        ffn_w = (mla_out_g[l], w_out[l], ffn_norm_g[l], w_gate[l], w_up[l], w_down[l])

        z, xbc, dt_raw, c_q, c_kv, kr_raw = project(hp, attn_norm_g[l], w_in[l])
        xpad = jnp.concatenate([jnp.zeros((b, CONV_W - 1, CONV_DIM), xbc.dtype), xbc], axis=1)
        h0 = jnp.zeros((b, SSD_HEADS, SSD_HEAD_DIM, D_STATE), jnp.float32)
        ssd_p, h_p, conv_p = ssd_branch(z, xpad, dt_raw, h0, ((N_META, N_META), (t - N_META, SSD_CHUNK)), *ssd_w)
        lat_p = rmsnorm(c_kv, kv_norm_g[l])
        kr_p = apply_rope(kr_raw, cos_p[None], sin_p[None])
        q = mla_queries(c_q, q_norm_g[l], w_uq[l], cos_p[None, :, None], sin_p[None, :, None], gq)
        k, v = mla_keys_values(lat_p, kr_p, w_ukv[l], gk)
        att_p = block_causal_attention(q, k, v)
        hp = finish_layer(hp, ssd_p, att_p, *ffn_w)

        z, xbc, dt_raw, c_q, c_kv, kr_raw = project(hs, attn_norm_g[l], w_in[l])
        xpad = jnp.concatenate([state_conv[l].astype(xbc.dtype), xbc], axis=1)
        ssd_s, h_s, conv_s = ssd_branch(z, xpad, dt_raw, state_ssm[l], ((s, s),), *ssd_w)
        lat_s = rmsnorm(c_kv, kv_norm_g[l])
        kr_s = apply_rope(kr_raw, cos_s[None], sin_s[None])
        q = mla_queries(c_q, q_norm_g[l], w_uq[l], cos_s[None, :, None], sin_s[None, :, None], gq)
        k, v = mla_keys_values(lat_s, kr_s, w_ukv[l], gk)
        att_s = paged_attention(q, k, v, cache_kv_latent, cache_k_rope, l, page_table, w_ukv[l], gk)
        hs = finish_layer(hs, ssd_s, att_s, *ffn_w)

        lat_p_l.append(lat_p)
        kr_p_l.append(kr_p)
        conv_p_l.append(conv_p)
        ssm_p_l.append(h_p.astype(x_prompt.dtype))
        lat_s_l.append(lat_s)
        kr_s_l.append(kr_s)
        conv_s_l.append(conv_s)
        ssm_s_l.append(h_s.astype(state_ssm.dtype))

    y_prompt = hp[:, N_META:]
    y_sample = hs
    return (y_prompt, y_sample,
            jnp.stack(lat_p_l), jnp.stack(kr_p_l), jnp.stack(conv_p_l), jnp.stack(ssm_p_l),
            jnp.stack(lat_s_l), jnp.stack(kr_s_l), jnp.stack(conv_s_l), jnp.stack(ssm_s_l))


_drawn_inputs = setup_inputs


def setup_inputs(seed=0):
    import zlib

    import numpy as np

    out = dict(_drawn_inputs(seed))
    spreads = {}
    factors = {'d_skip': 5.622,
     'ssd_norm_g': 4.692,
     'q_norm_g': 5.393,
     'kv_norm_g': 2.828,
     'q_head_g_nope': 5.968,
     'q_head_g_rope': 8.0,
     'k_head_g_nope': 7.156,
     'k_head_g_rope': 8.0,
     'mla_out_g': 5.331,
     'ffn_norm_g': 5.0}
    for name, (base, spread) in spreads.items():
        noise = np.random.default_rng([zlib.crc32(name.encode()), seed]).standard_normal(out[name].shape)
        drawn = base * np.exp(spread * noise) if base else spread * noise
        out[name] = jnp.asarray(drawn.astype(out[name].dtype))
    for name, factor in factors.items():
        out[name] = (out[name] * factor).astype(out[name].dtype)
    return out
```

```python
from contextlib import ExitStack

import concourse.bass as bass
from concourse import mybir

F32 = mybir.dt.float32
I32 = mybir.dt.int32
ALU = mybir.AluOpType
ACT = mybir.ActivationFunctionType
AXX = mybir.AxisListType.X
RMAX = bass.bass_isa.ReduceOp.max
ds = bass.ds

P = 128
D = 1024
KD = D // P
META = 16
SEQ = 1024
T = META + SEQ
NS = 8
TOK = T + NS
NT = SEQ // P
ODD = META + NS
SH, SP_, SN, SG = 8, 64, 64, 2
SW = SH * SP_
CONV = SW + 2 * SG * SN
CT = CONV // P
H, NOPE, ROPE, VD = 8, 64, 32, 64
HALF = ROPE // 2
QK = NOPE + ROPE
QL, KL = 384, 256
FF = 2816
IN = SW + CONV + SH + QL + KL + ROPE
C_XBC, C_DT, C_KV = SW, SW + CONV, SW + CONV + SH + QL
N_DQ, N_KV = SH + QL, KL + ROPE
PAGE, NPG = 128, 32
LATW = KL + ROPE
EPS = 1e-6
SCALE = QK ** -0.5
NEG = -1e30
N_SMALLS = 21
N_ODD_STORES = 7
POOL_TWO, ACT_TWO, DVE_TWO = 16, 2, 24


class Steps:

    def __init__(self, sem, name):
        self.sem, self.name, self.base, self.n, self.loop = sem, name, 0, 0, None

    def begin(self, i, per, first=0):
        self.loop, self.start = (i, per), self.n - first * per
        self.n, self.first = self.start, first

    def end(self, times):
        assert self.n - self.start == self.loop[1], (self.name, self.n - self.start)
        self.n = self.start + self.loop[1] * (self.first + times)
        self.loop = None

    def value(self):
        if self.loop is None:
            return self.n
        i, per = self.loop
        return i * per + self.n

    def __call__(self, eng, ins):
        ins.then_inc(self.sem, 1)
        self.n += 1
        eng.wait_ge(self.sem, self.value())


def bc(ap, n, axis):
    shape = list(ap.shape)
    shape.insert(axis, n)
    return ap.unsqueeze(axis).to_broadcast(shape)


def by_head(ap, width):
    return ap.rearrange("p (h d) -> p h d", d=width)



def tiles_block(nc, a, s):
    ctx = ExitStack()
    sb = lambda name, shape: ctx.enter_context(nc.sbuf_tensor("t_" + name, shape, F32))
    sems = []

    def sem(name):
        sems.append(nc.alloc_semaphore("t_" + name))
        return sems[-1]


    ps = ctx.enter_context(nc.psum_tensor("t_ps", [P, 8, 512], F32))
    w_in = sb("w_in", [P, KD, IN])
    w_uq = sb("w_uq", [P, QL // P, H * QK])
    w_ukv = sb("w_ukv", [P, KL // P, H * (NOPE + VD)])
    attn_g = sb("attn_g", [P, KD])
    qn_g = sb("qn_g", [P, QL // P])
    kvn_g = sb("kvn_g", [P, KL])
    conv_w = sb("conv_w", [P, CT, 4])
    conv_b = sb("conv_b", [P, CT])
    dt_b = sb("dt_b", [P, SH])
    neg_a = sb("neg_a", [P, SH])
    d_skip = sb("d_skip", [P, SH])
    gqk = sb("gqk", [QK, 1])
    gk = sb("gk", [QK, 1])
    cs = sb("cs", [P, NT + 1, 2 * HALF])
    ident = sb("ident", [P, P])
    upper = sb("upper", [P, P])
    ones = sb("ones", [P, P])
    mhalf = sb("mhalf", [P, 2 * H])
    eps = sb("eps", [P, 2 * H])
    cs_now = sb("cs_now", [P, 2 * HALF])
    state = sb("state", [P, 4 * SP_])
    stout = sb("stout", [P, 2, P])

    x = [sb(f"x{i}", [P, D]) for i in range(2)]
    xT = sb("xT", [P, KD, P])
    raw = [sb(f"raw{i}", [P, CT, 3 + P]) for i in range(2)]
    z = [sb(f"z{i}", [P, SW]) for i in range(2)]
    dq = [sb(f"dq{i}", [P, N_DQ]) for i in range(2)]
    kv = [sb(f"kv{i}", [P, N_KV]) for i in range(2)]
    junk = sb("junk", [P, D])
    junk_cl = sb("junk_cl", [P, QL + KL])
    junk_kr = sb("junk_kr", [P, ROPE])
    junk_y = sb("junk_y", [P, SW])
    stx = sb("stx", [P, 8])
    stc = sb("stc", [P, 4])
    sty = sb("sty", [P, 4])
    stq = sb("stq", [P, 5 * H])
    conv = sb("conv", [P, CT, P])
    ex = sb("ex", [P, CT, P])
    zex = sb("zex", [P, SW])
    xs = sb("xs", [P, SW])
    bn = sb("bn", [P, 2 * P])
    cz = sb("cz", [P, SG, P])
    gmask = sb("gmask", [P, SG, P])
    dts = sb("dts", [P, 14, SH])
    ud = sb("ud", [P, SH, P])
    seg = sb("seg", [P, SH, P])
    cbm = sb("cbm", [P, SG, P])
    xdt = sb("xdt", [P, SW])
    xw = sb("xw", [P, SW])
    dx = sb("dx", [P, SW])
    y = sb("y", [P, SW])
    ys = sb("ys", [P, SW])
    cq = sb("cq", [P, QL])
    lat = sb("lat", [P, KL])
    kr = sb("kr", [P, ROPE])
    krt = sb("krt", [P, 4, HALF])
    clT = sb("clT", [P, 5, P])
    q = sb("q", [P, H, QK])
    qsq = sb("qsq", [P, H, QK])
    k = sb("k", [P, H, QK])
    ksq = sb("ksq", [P, H, NOPE])
    v = sb("v", [P, SW])
    rp = sb("rp", [P, 4, H, HALF])
    qT = sb("qT", [QK, H, P])
    kT = sb("kT", [QK, H, P])
    sconv = sb("sconv", [3 * NS, CONV])
    sT = sb("sT", [P, CT, 3 * NS])
    rawn = sb("rawn", [ODD, CONV])
    rawl = sb("rawl", [3, CONV])

    V, AV, U, W, LN, W1, DT, DTA, ACS, EACS, DIN, DEC, DLAST = range(13)

    weights = [sem(f"weights{i}") for i in range(KD)]
    smalls = sem("smalls")
    up_weights = sem("up_weights")
    names = """consts a_exp folded up_folded x_squared x_rstd x_normed xT_ready0 xT_ready1 xT_copied0 xT_copied1
    xbc_ready0 xbc_ready1 xbc_copied0 xbc_copied1 z_ready z_copied dq_ready dq_copied kv_ready kv_copied
    halo_done conv_done conv_exp conv_silu z_exp z_silu dt_in dt_exp dt_w dt_ln dt_done ud_ready
    cl_squared cl_rstd cl_normed clT_ready0 clT_ready1 clT_copied0 clT_copied1
    xs_ready bT_ready xs_copied bn_copied acs_ready acs_copied bc_ready bc_taken cb_ready cb_taken
    seg_done seg_exp last_exp decay_in decay_exp cz_ready att_ready xdt_ready xw_ready dx_ready
    yd_ready yo_ready st_ready yd_taken yo_taken st_taken state_done
    q_ready kvu_ready q_copied kn_squared v_copied kn_taken kr_done kr_squared q_roped q_squared qk_sums qk_rstd
    q_normed k_normed qT_ready0 qT_ready1 kT_ready0 kT_ready1 qT_copied0 qT_copied1 kT_copied0 kT_copied1
    y_done y_squared y_rstd y_normed
    sconv_ready sconv_copied rawn_ready rawn_copied rawl_ready rawl_copied stout_ready stout_copied""".split()
    S = {n: sem(n) for n in names}
    x_loaded = [sem(f"x_loaded{i}") for i in range(2)]
    sample_loaded = sem("sample_loaded")
    stored = {n: sem("stored_" + n) for n in "ys lat kr qT kT v odd".split()}
    last_stored = sem("last_stored")
    act_steps = Steps(sem("act_steps"), "act")
    dve_steps = Steps(sem("dve_steps"), "dve")
    pool_steps = Steps(sem("pool_steps"), "pool")

    def out(ins, name):
        ins.then_inc(S[name], 1)


    def rows(t):
        return ODD if isinstance(t, int) and t == 0 else P

    def after(eng, name, n):
        if not (isinstance(n, int) and n <= 0):
            eng.wait_ge(S[name], n)

    def free(eng, name, t):
        if not (isinstance(t, int) and t <= 0):
            eng.wait_ge(stored[name], t * 16 + 16)

    block = ctx.enter_context(nc.Block())

    @block.sync
    def _(sp):
        def data(name, n):
            sp.wait_ge(S[name], n)
            sp.wait_ge(S["consts"], 1)

        def load_x(t, c, p):
            if isinstance(t, int) and t == 0:
                sp.dma_start(x[0][0:META, :], a["meta_tokens"]).then_inc(x_loaded[0], 16)
                sp.dma_start(x[0][META:ODD, :], a["x_sample"].rearrange("b s d -> (b s) d")).then_inc(sample_loaded, 16)
                return
            row = sp.snap((t - 1) * P)
            if not (isinstance(t, int) and t == 1):
                data("xT_ready1", t - 1)
            sp.dma_start(x[p][:, :], a["x_prompt"][0, ds(row, P), :]).then_inc(x_loaded[p], 16)

        def store(t):
            if isinstance(t, int) and t == 0:
                pieces = [(0, META, 0, True), (META, ODD, T, False)]
            else:
                at = sp.snap(META + (t - 1) * P)
                pieces = [(0, P, at, True)]
            data("cl_normed", t + 1)
            for lo, hi, at, prompt in pieces:
                dst = a["kv_latent_prompt"][0, 0, ds(at, hi - lo), :] if prompt else a["kv_latent_sample"][0, :, 0, :]
                sp.dma_start(dst, lat[lo:hi, :]).then_inc(stored["lat"], 16)
            data("kr_done", t + 1)
            for lo, hi, at, prompt in pieces:
                dst = a["k_rope_prompt"][0, 0, ds(at, hi - lo), :] if prompt else a["k_rope_sample"][0, :, 0, :]
                sp.dma_start(dst, kr[lo:hi, :]).then_inc(stored["kr"], 16)
            data("v_copied", t + 1)
            for lo, hi, at, _ in pieces:
                sp.dma_start(s["v"][ds(at, hi - lo), :], v[lo:hi, :]).then_inc(stored["v"], 16)
            data("qT_copied1", t + 1)
            data("y_normed", t + 1)
            for lo, hi, at, _ in pieces[:1]:
                sp.dma_start(s["ys"][ds(at, hi - lo), :], ys[lo:hi, :]).then_inc(stored["ys"], 16)
            for lo, hi, at, _ in pieces:
                sp.dma_start(s["qT"][:, :, ds(at, hi - lo)].rearrange("h d t -> d h t"),
                             qT[:, :, lo:hi]).then_inc(stored["qT"], 16)
            data("kT_copied1", t + 1)
            for lo, hi, at, _ in pieces:
                sp.dma_start(s["kT"][:, :, ds(at, hi - lo)].rearrange("h d t -> d h t"),
                             kT[:, :, lo:hi]).then_inc(stored["kT"], 16)

        load_x(0, 0, 0)
        load_x(1, 0, 1)
        for kd in range(KD):
            sp.dma_start(w_in[:, kd, :], a["w_in"][0, kd * P:(kd + 1) * P, :]).then_inc(weights[kd], 16)
        sp.dma_start(w_uq[:, :, :], a["w_uq"][0].rearrange("(k p) n -> p k n", p=P)).then_inc(up_weights, 16)
        sp.dma_start(w_ukv[:, :, :], a["w_ukv"][0].rearrange("(k p) n -> p k n", p=P)).then_inc(up_weights, 16)
        load_x(2, 1, 0)
        sp.wait_ge(S["z_silu"], 1)
        sp.dma_start(s["s_z"], z[0][META:ODD, :]).then_inc(stored["odd"], 16)
        sp.wait_ge(S["xs_copied"], 1)
        sp.dma_start(s["s_x"], xs[META:ODD, :]).then_inc(stored["odd"], 16)
        sp.wait_ge(S["bn_copied"], 1)
        sp.dma_start(s["s_bc"], bn[META:ODD, :]).then_inc(stored["odd"], 16)
        sp.wait_ge(S["dt_done"], 1)
        sp.dma_start(s["s_dt"], dts[META:ODD, DT, :]).then_inc(stored["odd"], 16)
        sp.dma_start(s["s_dta"], dts[META:ODD, DTA, :]).then_inc(stored["odd"], 16)
        sp.wait_ge(S["rawn_copied"], 1)
        sp.dma_start(a["conv_sample"][0, :, 0:2, :], a["state_conv"][0, :, 1:3, :]).then_inc(last_stored, 16)
        sp.dma_start(a["conv_sample"][0, :, 2, :], rawn[META:ODD, :]).then_inc(last_stored, 16)
        sp.wait_ge(S["q_normed"], 1)
        sp.dma_start(s["s_q"], q[META:ODD, :, :]).then_inc(stored["odd"], 16)
        sp.wait_ge(S["k_normed"], 1)
        sp.wait_ge(S["kn_taken"], 1)
        sp.dma_start(s["s_k"], k[META:ODD, :, :]).then_inc(stored["odd"], 16)
        store(0)
        with sp.Fori(0, 3) as i:
            load_x(i * 2 + 3, i + 1, 1)
            store(i * 2 + 1)
            load_x(i * 2 + 4, i + 2, 0)
            store(i * 2 + 2)
        store(7)
        store(8)
        sp.wait_ge(S["rawl_copied"], 1)
        sp.dma_start(a["conv_prompt"][0, 0, :, :], rawl[:, :]).then_inc(last_stored, 16)
        sp.wait_ge(S["stout_copied"], 1)
        for b2 in range(2):
            for g in range(SG):
                h0 = g * 4 + b2 * 2
                sp.dma_start(a["ssm_prompt"][0, 0, h0:h0 + 2, :, :].rearrange("h p n -> (h p) n"),
                             stout[:, b2, g * SN:(g + 1) * SN]).then_inc(last_stored, 16)
        sp.wait_ge(last_stored, 16 * 7)
        sp.wait_ge(stored["odd"], 16 * N_ODD_STORES)
        sp.wait_ge(stored["ys"], 16 * (NT + 1))
        for n in ("lat", "kr", "qT", "kT", "v"):
            sp.wait_ge(stored[n], 16 * (NT + 2))

    @block.gpsimd
    def _(pool):
        def rstd(dst, src):
            pool_steps(pool, pool.tensor_tensor(out=src, in0=src, in1=eps[0:src.shape[0], 0:src.shape[1]], op=ALU.add))
            return pool.tensor_tensor(out=dst, in0=src, in1=mhalf[0:src.shape[0], 0:src.shape[1]], op=ALU.pow)

        def norm_x(t):
            R = rows(t)
            after(pool, "x_squared", t + 1)
            out(rstd(stx[0:R, 2:3], stx[0:R, 0:1]), "x_rstd")

        pool_steps(pool, pool.memset(ident[:, :], 0.0))
        pool_steps(pool, pool.affine_select(out=ident[:, :], in_=ident[:, :], compare_op=ALU.not_equal, fill=1.0,
                                            base=0, pattern=[[-1, P]], channel_multiplier=1))
        pool_steps(pool, pool.memset(upper[:, :], 1.0))
        pool.affine_select(out=upper[:, :], in_=upper[:, :], compare_op=ALU.is_ge, fill=0.0, base=0,
                           pattern=[[1, P]], channel_multiplier=-1)
        pool.memset(ones[:, :], 1.0)
        pool.memset(mhalf[:, :], -0.5)
        pool.memset(eps[:, :], EPS)
        pool_steps(pool, pool.memset(gmask[:, :, :], 0.0))
        pool_steps(pool, pool.memset(gmask[0:SN, 0, :], 1.0))
        pool_steps(pool, pool.memset(gmask[SN:P, 1, :], 1.0))
        pool.memset(state[:, :], 0.0)
        pool_steps(pool, pool.memset(raw[0][:, :, 0:3], 0.0))
        out(pool.memset(junk[:, :], 0.0), "consts")
        norm_x(0)
        norm_x(1)

        def rope(dst, src, tmp, t, R, heads):
            c, sn = cs_now[0:R, 0:HALF], cs_now[0:R, HALF:2 * HALF]
            if heads:
                c, sn = bc(c, H, 1), bc(sn, H, 1)
                x1, x2, d1, d2 = src[:, :, 0:HALF], src[:, :, HALF:ROPE], dst[:, :, 0:HALF], dst[:, :, HALF:ROPE]
            else:
                x1, x2, d1, d2 = src[:, 0:HALF], src[:, HALF:ROPE], dst[:, 0:HALF], dst[:, HALF:ROPE]
            pool.tensor_tensor(out=tmp[0], in0=x1, in1=c, op=ALU.mult)
            pool.tensor_tensor(out=tmp[1], in0=x2, in1=sn, op=ALU.mult)
            pool.tensor_tensor(out=tmp[2], in0=x1, in1=sn, op=ALU.mult)
            pool_steps(pool, pool.tensor_tensor(out=tmp[3], in0=x2, in1=c, op=ALU.mult))
            pool.tensor_tensor(out=d1, in0=tmp[0], in1=tmp[1], op=ALU.subtract)
            return pool.tensor_tensor(out=d2, in0=tmp[2], in1=tmp[3], op=ALU.add)

        def iteration(t, p, ahead):
            R = rows(t)
            C = META if R == ODD else P
            pool.wait_ge(S["cl_squared"], t + 1)
            out(rstd(stc[0:R, 2:4], stc[0:R, 0:2]), "cl_rstd")
            pool.wait_ge(S["conv_silu"], t + 1)
            out(pool.tensor_tensor(out=cz[:, :, 0:R], in0=bc(conv[:, CT - 1, 0:R], SG, 1), in1=gmask[:, :, 0:R],
                                   op=ALU.mult), "cz_ready")
            pool_steps(pool, pool.tensor_copy(cs_now[:, :], cs[:, ds(t, 1), :].rearrange("p o d -> p (o d)")))
            free(pool, "kr", t)
            pool.wait_ge(S["kv_copied"], t + 1)
            out(rope(kr[0:R, :], kv[p][0:R, KL:N_KV], [krt[0:R, j, :] for j in range(4)], t, R, False), "kr_done")
            pool.wait_ge(S["dt_done"], t + 1)
            out(pool.tensor_tensor(out=ud[0:C, :, 0:C], in0=bc(upper[0:C, 0:C], SH, 1),
                                   in1=bc(dts[0:C, DTA, :], C, 2), op=ALU.mult), "ud_ready")
            pool.wait_ge(S["xs_copied"], t + 1)
            out(pool.tensor_tensor(out=by_head(dx[0:C, :], SP_), in0=by_head(xs[0:C, :], SP_),
                                   in1=bc(d_skip[0:C, :], SP_, 2), op=ALU.mult), "dx_ready")
            pool.wait_ge(S["decay_exp"], t + 1)
            pool.wait_ge(S["xdt_ready"], t + 1)
            out(pool.tensor_tensor(out=by_head(xw[0:C, :], SP_), in0=by_head(xdt[0:C, :], SP_),
                                   in1=bc(dts[0:C, DEC, :], SP_, 2), op=ALU.mult), "xw_ready")
            pool.wait_ge(S["seg_exp"], t + 1)
            pool.wait_ge(S["cb_taken"], t + 1)
            for g in range(SG):
                ins = pool.tensor_tensor(out=seg[0:C, 4 * g:4 * g + 4, 0:C], in0=seg[0:C, 4 * g:4 * g + 4, 0:C],
                                         in1=bc(cbm[0:C, g, 0:C], 4, 1), op=ALU.mult)
            out(ins, "att_ready")
            if ahead:
                norm_x(t + 2)
            pool.wait_ge(S["q_copied"], t + 1)
            out(rope(q[0:R, :, NOPE:QK], q[0:R, :, NOPE:QK], [rp[0:R, j, :, :] for j in range(4)], t, R, True), "q_roped")
            pool.wait_ge(S["qk_sums"], t + 1)
            pool.wait_ge(S["kr_squared"], t + 1)
            pool_steps(pool, pool.tensor_tensor(out=stq[0:R, H:2 * H], in0=stq[0:R, H:2 * H],
                                                in1=stq[0:R, 4 * H:4 * H + 1].to_broadcast([R, H]), op=ALU.add))
            out(rstd(stq[0:R, 2 * H:4 * H], stq[0:R, 0:2 * H]), "qk_rstd")
            pool.wait_ge(S["qk_rstd"], t + 1)
            out(pool.tensor_tensor(out=q[0:R, :, :], in0=q[0:R, :, :], in1=bc(stq[0:R, 2 * H:3 * H], QK, 2),
                                   op=ALU.mult), "q_normed")
            out(pool.tensor_tensor(out=k[0:R, :, NOPE:QK], in0=bc(kr[0:R, :], H, 1),
                                   in1=bc(stq[0:R, 3 * H:4 * H], ROPE, 2), op=ALU.mult), "k_normed")
            pool.wait_ge(S["y_squared"], t + 1)
            out(rstd(sty[0:C, 2:4], sty[0:C, 0:2]), "y_rstd")

        iteration(0, 0, True)
        with pool.Fori(0, 3) as i:
            pool_steps.begin(i, POOL_TWO)
            iteration(i * 2 + 1, 1, True)
            iteration(i * 2 + 2, 0, True)
            pool_steps.end(3)
        iteration(7, 1, False)
        iteration(8, 0, False)

    @block.scalar
    def _(act):
        def load_small(dst, src):
            act.dma_start(dst, src).then_inc(smalls, 16)

        load_small(attn_g[:, :], a["attn_norm_g"].rearrange("o (k p) -> p (o k)", p=P))
        load_small(qn_g[:, :], a["q_norm_g"].rearrange("o (k p) -> p (o k)", p=P))
        load_small(kvn_g[:, :], a["kv_norm_g"].to_broadcast([P, KL]))
        load_small(neg_a[:, :], a["a_log"].to_broadcast([P, SH]))
        load_small(dt_b[:, :], a["dt_bias"].to_broadcast([P, SH]))
        load_small(d_skip[:, :], a["d_skip"].to_broadcast([P, SH]))
        for j in range(CT):
            load_small(conv_w[:, j, :], a["conv_w"][0, :, j * P:(j + 1) * P].rearrange("k p -> p k"))
        load_small(conv_b[:, :], a["conv_b"].rearrange("o (c p) -> p (o c)", p=P))
        for dst, name in ((gqk, "q"), (gk, "k")):
            load_small(dst[0:NOPE, :], a[name + "_head_g_nope"].rearrange("o d -> d o"))
            for j in range(2):
                load_small(dst[NOPE + j * HALF:NOPE + (j + 1) * HALF, :], a[name + "_head_g_rope"].rearrange("o d -> d o"))
        load_small(cs[:, :, :], a["rope_table"])
        load_small(sconv[:, :], a["state_conv"][0].rearrange("b k c -> (b k) c"))

        def copy(dst, src, name):
            out(act.activation(dst, src, ACT.Copy), name)

        def square_x(t, c, p):
            R = rows(t)
            act.wait_ge(x_loaded[p], 16 * (c + 1))
            if R == ODD:
                act.wait_ge(sample_loaded, 16)
                act.wait_ge(S["consts"], 1)
            after(act, "x_normed", t)
            out(act.activation(junk[0:R, :], x[p][0:R, :], ACT.Square, scale=D ** -0.5,
                               accum_out=stx[0:R, 0:1]), "x_squared")

        def copy_xT(t):
            R = rows(t)
            after(act, "kv_ready", t)
            for j in range(2):
                act.wait_ge(S[f"xT_ready{j}"], t + 1)
                copy(xT[:, 4 * j:4 * j + 4, 0:R], ps[:, j, 0:4 * R].rearrange("p (k r) -> p k r", r=R), f"xT_copied{j}")

        def copy_xbc(t, p):
            R = rows(t)
            after(act, "halo_done", t)
            act.wait_ge(S["xbc_ready0"], t + 1)
            copy(raw[p][:, 0:4, 3:3 + R], ps[:, 2, 0:4 * R].rearrange("p (k r) -> p k r", r=R), "xbc_copied0")
            act.wait_ge(S["xbc_ready1"], t + 1)
            copy(raw[p][:, 4:6, 3:3 + R], ps[:, 3, 0:2 * R].rearrange("p (k r) -> p k r", r=R), "xbc_copied1")
            act.wait_ge(S["z_ready"], t + 1)
            after(act, "y_done", t - 1)
            copy(z[p][0:R, :], ps[0:R, 0, :], "z_copied")

        def copy_rest(t, p):
            R = rows(t)
            act.wait_ge(S["dq_ready"], t + 1)
            copy(dq[p][0:R, :], ps[0:R, 1, 0:N_DQ], "dq_copied")
            act.wait_ge(S["kv_ready"], t + 1)
            copy(kv[p][0:R, :], ps[0:R, 2, 0:N_KV], "kv_copied")

        act.wait_ge(smalls, 16 * N_SMALLS)
        out(act.activation(neg_a[:, :], neg_a[:, :], ACT.Exp), "a_exp")
        square_x(0, 0, 0)
        square_x(1, 0, 1)
        copy_xT(0)
        copy_xbc(0, 0)
        copy_rest(0, 0)
        act.wait_ge(S["sconv_ready"], 1)
        copy(sT[:, :, :], ps[:, 4, 0:CT * 3 * NS].rearrange("p (c r) -> p c r", c=CT), "sconv_copied")
        act.wait_ge(S["rawn_ready"], 1)
        act.activation(rawn[:, 0:4 * P], ps[0:ODD, 6, :], ACT.Copy)
        copy(rawn[:, 4 * P:], ps[0:ODD, 7, 0:2 * P], "rawn_copied")

        def iteration(t, c, p, ahead, after_it):
            R = rows(t)
            C = META if R == ODD else P
            if after_it:
                copy_xT(t + 1)
            act.wait_ge(S["dt_in"], t + 1)
            act_steps(act, act.activation(dts[0:R, AV, :], dts[0:R, V, :], ACT.Abs))
            out(act.activation(dts[0:R, U, :], dts[0:R, AV, :], ACT.Exp, scale=-1.0), "dt_exp")
            act.activation(junk_cl[0:R, 0:QL], dq[p][0:R, SH:N_DQ], ACT.Square, scale=QL ** -0.5, accum_out=stc[0:R, 0:1])
            out(act.activation(junk_cl[0:R, QL:QL + KL], kv[p][0:R, 0:KL], ACT.Square, scale=KL ** -0.5,
                               accum_out=stc[0:R, 1:2]), "cl_squared")
            act.wait_ge(S["conv_done"], t + 1)
            out(act.activation(ex[:, :, 0:R], conv[:, :, 0:R], ACT.Exp, scale=-1.0), "conv_exp")
            out(act.activation(zex[0:R, :], z[p][0:R, :], ACT.Exp, scale=-1.0), "z_exp")
            act.wait_ge(S["dt_w"], t + 1)
            out(act.activation(dts[0:R, LN, :], dts[0:R, W, :], ACT.Ln), "dt_ln")
            if after_it:
                copy_xbc(t + 1, 1 - p)
            act.wait_ge(S["clT_ready0"], t + 1)
            copy(clT[:, 0:4, 0:R], ps[:, 4, 0:4 * R].rearrange("p (k r) -> p k r", r=R), "clT_copied0")
            act.wait_ge(S["xs_ready"], t + 1)
            copy(xs[0:R, :], ps[0:R, 6, :], "xs_copied")
            act.wait_ge(S["bT_ready"], t + 1)
            copy(clT[:, 4, 0:R], ps[:, 5, 0:R], "clT_copied1")
            nb = 2 if R == ODD else 1
            copy(bn[0:R, 0:nb * P], ps[0:R, 5, P:(1 + nb) * P], "bn_copied")
            act.wait_ge(S["acs_ready"], t + 1)
            act.activation(dts[0:C, EACS, :], ps[0:C, 7, 0:SH], ACT.Exp)
            copy(dts[0:C, ACS, :], ps[0:C, 7, 0:SH], "acs_copied")
            act.wait_ge(S["bc_ready"], t + 1)
            last = ps[:, 6:8, 0:4 * C].rearrange("p b (h i) -> p b h i", i=C)[:, :, :, C - 1]
            out(act.activation(dts[:, DLAST, :].rearrange("p (b h) -> p b h", b=2), last, ACT.Exp), "last_exp")
            act.wait_ge(S["decay_in"], t + 1)
            out(act.activation(dts[0:C, DEC, :], dts[0:C, DIN, :], ACT.Exp), "decay_exp")
            act.wait_ge(S["seg_done"], t + 1)
            out(act.activation(seg[0:C, :, 0:C], seg[0:C, :, 0:C], ACT.Exp), "seg_exp")
            if ahead:
                square_x(t + 2, c + 1, p)
            if after_it:
                copy_rest(t + 1, 1 - p)
            act.wait_ge(S["q_ready"], t + 1)
            copy(q[0:R, :, :].rearrange("p (b h) d -> p b (h d)", b=2), ps[0:R, 4:6, 0:4 * QK], "q_copied")
            act.wait_ge(S["kvu_ready"], t + 1)
            up = ps[0:R, 6:8, :].rearrange("p b (h d) -> p b h d", d=NOPE + VD)
            out(act.activation(ksq[0:R, :, :].rearrange("p (b h) d -> p b h d", b=2), up[:, :, :, 0:NOPE],
                               ACT.Square, scale=QK ** -0.5), "kn_squared")
            free(act, "v", t)
            copy(v[0:R, :].rearrange("p (b h d) -> p b h d", b=2, d=VD), up[:, :, :, NOPE:NOPE + VD], "v_copied")
            act.wait_ge(S["kr_done"], t + 1)
            out(act.activation(junk_kr[0:R, :], kr[0:R, :], ACT.Square, scale=QK ** -0.5,
                               accum_out=stq[0:R, 4 * H:4 * H + 1]), "kr_squared")
            act.wait_ge(S["q_roped"], t + 1)
            out(act.activation(qsq[0:R, :, :], q[0:R, :, :], ACT.Square, scale=QK ** -0.5), "q_squared")
            act.wait_ge(S["y_done"], t + 1)
            for g in range(SG):
                w = SW // SG
                ins = act.activation(junk_y[0:C, g * w:(g + 1) * w], y[0:C, g * w:(g + 1) * w], ACT.Square,
                                     scale=w ** -0.5, accum_out=sty[0:C, g:g + 1])
            out(ins, "y_squared")
            free(act, "kT", t)
            for j, b in ((0, 5), (1, 4)):
                act.wait_ge(S[f"kT_ready{j}"], t + 1)
                copy(kT[:, 4 * j:4 * j + 4, 0:R], ps[0:QK, b, 0:4 * R].rearrange("p (h r) -> p h r", r=R), f"kT_copied{j}")

        iteration(0, 0, 0, True, True)
        act.wait_ge(stored["odd"], 16 * N_ODD_STORES)
        with act.Fori(0, 3) as i:
            act_steps.begin(i, ACT_TWO)
            iteration(i * 2 + 1, i, 1, True, True)
            iteration(i * 2 + 2, i + 1, 0, True, True)
            act_steps.end(3)
        iteration(7, 3, 1, False, True)
        iteration(8, 4, 0, False, False)
        act.wait_ge(S["rawl_ready"], 1)
        act.activation(rawl[:, 0:4 * P], ps[0:3, 6, :], ACT.Copy)
        copy(rawl[:, 4 * P:], ps[0:3, 7, 0:2 * P], "rawl_copied")
        act.wait_ge(S["stout_ready"], 1)
        copy(stout[:, :, :], ps[:, 5, 0:2 * P].rearrange("p (b n) -> p b n", b=2), "stout_copied")

    @block.vector
    def _(dve):
        def add_one_reciprocal(ap):
            dve_steps(dve, dve.tensor_scalar(ap, ap, 1.0, None, ALU.add))
            dve_steps(dve, dve.reciprocal(ap, ap))

        def norm_x(t, p):
            R = rows(t)
            dve.wait_ge(S["x_rstd"], t + 1)
            out(dve.tensor_scalar(x[p][0:R, :], x[p][0:R, :], stx[0:R, 2:3], None, ALU.mult), "x_normed")

        dve.wait_ge(smalls, 16 * N_SMALLS)
        norm_x(0, 0)
        for kd in range(KD):
            dve.wait_ge(weights[kd], 16)
            out(dve.tensor_scalar(w_in[:, kd, :], w_in[:, kd, :], attn_g[:, kd:kd + 1], None, ALU.mult), "folded")
        norm_x(1, 1)
        dve.wait_ge(up_weights, 32)
        for kd in range(QL // P):
            ins = dve.tensor_scalar(w_uq[:, kd, :], w_uq[:, kd, :], qn_g[:, kd:kd + 1], None, ALU.mult)
        out(ins, "up_folded")
        dve_steps(dve, dve.tensor_tensor(out=gqk[:, :], in0=gqk[:, :], in1=gk[:, :], op=ALU.mult))
        dve.wait_ge(S["sconv_copied"], 1)
        dve.wait_ge(S["a_exp"], 1)
        dve.wait_ge(S["consts"], 1)

        def iteration(t, p, ahead):
            R = rows(t)
            odd = R == ODD
            C = META if odd else P
            if not odd:
                out(dve.tensor_copy(raw[p][:, :, 0:3], raw[1 - p][:, :, P:P + 3]), "halo_done")
                dve.wait_ge(S["halo_done"], t + 1)
            dve.wait_ge(S["dq_copied"], t + 1)
            out(dve.tensor_tensor(out=dts[0:R, V, :], in0=dq[p][0:R, 0:SH], in1=dt_b[0:R, :], op=ALU.add), "dt_in")
            dve.wait_ge(S["xbc_copied1"], t + 1)
            for kk in range(4):
                for j in range(CT):
                    parts = [(0, C, raw[p][:, j, kk:kk + C])]
                    if odd:
                        own = raw[p][:, j, 3 + META:3 + ODD] if kk == 3 else sT[:, j, :].rearrange("p (b k) -> p b k", k=3)[:, :, kk]
                        parts.append((META, ODD, own))
                    for lo, hi, src in parts:
                        o = conv[:, j, lo:hi]
                        if kk == 0:
                            ins = dve.tensor_scalar(o, src, conv_w[:, j, 0:1], conv_b[:, j:j + 1], ALU.mult, ALU.add)
                        else:
                            ins = dve.scalar_tensor_tensor(out=o, in0=src, scalar=conv_w[:, j, kk:kk + 1], in1=o,
                                                           op0=ALU.mult, op1=ALU.add)
                if kk < 3:
                    dve_steps(dve, ins)
            out(ins, "conv_done")
            if odd:
                out(dve.tensor_copy(raw[0][:, :, P:P + 3], raw[0][:, :, META:META + 3]), "halo_done")
            dve.wait_ge(S["dt_exp"], t + 1)
            dve_steps(dve, dve.tensor_scalar(dts[0:R, W, :], dts[0:R, U, :], 1.0, None, ALU.add))
            out(dve.scalar_tensor_tensor(out=dts[0:R, W1, :], in0=dts[0:R, W, :], scalar=-1.0, in1=dts[0:R, U, :],
                                         op0=ALU.add, op1=ALU.subtract), "dt_w")
            dve.wait_ge(S["conv_exp"], t + 1)
            add_one_reciprocal(ex[:, :, 0:R])
            out(dve.tensor_tensor(out=conv[:, :, 0:R], in0=conv[:, :, 0:R], in1=ex[:, :, 0:R], op=ALU.mult), "conv_silu")
            dve.wait_ge(S["cl_rstd"], t + 1)
            free(dve, "lat", t)
            dve.tensor_scalar(cq[0:R, :], dq[p][0:R, SH:N_DQ], stc[0:R, 2:3], None, ALU.mult)
            out(dve.scalar_tensor_tensor(out=lat[0:R, :], in0=kv[p][0:R, 0:KL], scalar=stc[0:R, 3:4], in1=kvn_g[0:R, :],
                                         op0=ALU.mult, op1=ALU.mult), "cl_normed")
            dve.wait_ge(S["dt_ln"], t + 1)
            dve.wait_ge(S["dt_w"], t + 1)
            dve.tensor_tensor(out=dts[0:R, LN, :], in0=dts[0:R, LN, :], in1=dts[0:R, W1, :], op=ALU.subtract)
            dve_steps(dve, dve.tensor_scalar(dts[0:R, V, :], dts[0:R, V, :], 0.0, None, ALU.max))
            dve_steps(dve, dve.tensor_tensor(out=dts[0:R, DT, :], in0=dts[0:R, V, :], in1=dts[0:R, LN, :], op=ALU.add))
            out(dve.scalar_tensor_tensor(out=dts[0:R, DTA, :], in0=dts[0:R, DT, :], scalar=-1.0, in1=neg_a[0:R, :],
                                         op0=ALU.mult, op1=ALU.mult), "dt_done")
            dve.wait_ge(S["z_exp"], t + 1)
            add_one_reciprocal(zex[0:R, :])
            out(dve.tensor_tensor(out=z[p][0:R, :], in0=z[p][0:R, :], in1=zex[0:R, :], op=ALU.mult), "z_silu")
            dve.wait_ge(S["xs_copied"], t + 1)
            out(dve.tensor_tensor(out=by_head(xdt[0:C, :], SP_), in0=by_head(ps[0:C, 6, :], SP_),
                                  in1=bc(dts[0:C, DT, :], SP_, 2), op=ALU.mult), "xdt_ready")
            dve.wait_ge(S["last_exp"], t + 1)
            every = ps[0:C, 6:8, 0:4 * C].rearrange("p b (h i) -> p b h i", i=C)
            out(dve.tensor_tensor(out=dts[0:C, DIN, :].rearrange("p (b h) -> p b h", b=2), in0=every[:, :, :, C - 1],
                                  in1=dts[0:C, ACS, :].rearrange("p (b h) -> p b h", b=2), op=ALU.subtract), "decay_in")
            for h in range(SH):
                ins = dve.tensor_scalar(seg[0:C, h, 0:C], every[:, h // 4, h % 4, :], dts[0:C, ACS, h:h + 1], 0.0,
                                        ALU.subtract, ALU.min)
            out(ins, "seg_done")
            dve.wait_ge(S["cb_ready"], t + 1)
            out(dve.tensor_tensor(out=cbm[0:C, :, 0:C], in0=ps[0:C, 5, 2 * P:2 * P + 2 * C].rearrange("p (g i) -> p g i", g=SG),
                                  in1=bc(upper[0:C, 0:C], SG, 1), op=ALU.mult), "cb_taken")
            if ahead:
                norm_x(t + 2, p)
            dve.wait_ge(S["kn_squared"], t + 1)
            dve.tensor_reduce(stq[0:R, H:2 * H], ksq[0:R, :, :], AXX, ALU.add)
            dve.wait_ge(S["q_squared"], t + 1)
            out(dve.tensor_reduce(stq[0:R, 0:H], qsq[0:R, :, :], AXX, ALU.add), "qk_sums")
            dve.wait_ge(S["yo_ready"], t + 1)
            out(dve.tensor_tensor(out=by_head(y[0:C, :], SP_), in0=by_head(ps[0:C, 5, :], SP_),
                                  in1=bc(dts[0:C, EACS, :], SP_, 2), op=ALU.mult), "yo_taken")
            dve.wait_ge(S["yo_taken"], t + 1)
            dve.wait_ge(S["yd_ready"], t + 1)
            out(dve.tensor_tensor(out=y[0:C, :], in0=y[0:C, :], in1=ps[0:C, 4, :], op=ALU.add), "yd_taken")
            dve.wait_ge(S["yd_taken"], t + 1)
            dve.wait_ge(S["dx_ready"], t + 1)
            dve_steps(dve, dve.tensor_tensor(out=y[0:C, :], in0=y[0:C, :], in1=dx[0:C, :], op=ALU.add))
            out(dve.tensor_tensor(out=y[0:C, :], in0=y[0:C, :], in1=z[p][0:C, :], op=ALU.mult), "y_done")
            dve.wait_ge(S["qk_rstd"], t + 1)
            dve.wait_ge(S["v_copied"], t + 1)
            out(dve.tensor_tensor(out=k[0:R, :, 0:NOPE].rearrange("p (b h) d -> p b h d", b=2),
                                  in0=ps[0:R, 6:8, :].rearrange("p b (h d) -> p b h d", d=NOPE + VD)[:, :, :, 0:NOPE],
                                  in1=bc(stq[0:R, 3 * H:4 * H].rearrange("p (b h) -> p b h", b=2), NOPE, 3),
                                  op=ALU.mult), "kn_taken")
            dve.wait_ge(S["st_ready"], t + 1)
            dve.wait_ge(S["last_exp"], t + 1)
            half = [slice(0, SN), slice(SN, P)]
            for g in range(SG):
                ins = dve.tensor_tensor(out=by_head(state[half[g], :], SP_), in0=by_head(state[half[g], :], SP_),
                                        in1=bc(dts[half[g], DLAST, 4 * g:4 * g + 4], SP_, 2), op=ALU.mult)
            dve_steps(dve, ins)
            for g in range(SG):
                ins = dve.tensor_tensor(out=state[half[g], :], in0=state[half[g], :],
                                        in1=ps[half[g], 4, 256 * g:256 * (g + 1)], op=ALU.add)
            out(ins, "state_done")
            free(dve, "qT", t)
            for j, b in ((0, 7), (1, 6)):
                dve.wait_ge(S[f"qT_ready{j}"], t + 1)
                out(dve.tensor_scalar(qT[:, 4 * j:4 * j + 4, 0:R], ps[0:QK, b, 0:4 * R].rearrange("p (h r) -> p h r", r=R),
                                      gqk[:, 0:1], None, ALU.mult), f"qT_copied{j}")
            dve.wait_ge(S["y_rstd"], t + 1)
            if not odd:
                dve.wait_ge(stored["ys"], t * 16)
            for g in range(SG):
                w = SW // SG
                ins = dve.tensor_scalar(ys[0:C, g * w:(g + 1) * w], y[0:C, g * w:(g + 1) * w], sty[0:C, 2 + g:3 + g],
                                        None, ALU.mult)
            out(ins, "y_normed")

        iteration(0, 0, True)
        dve.wait_ge(stored["odd"], 16 * N_ODD_STORES)
        with dve.Fori(0, 3) as i:
            dve_steps.begin(i, DVE_TWO)
            iteration(i * 2 + 1, 1, True)
            iteration(i * 2 + 2, 0, True)
            dve_steps.end(3)
        iteration(7, 1, False)
        iteration(8, 0, False)

    @block.tensor
    def _(pe):
        def product(dst, lhsT, rhs, name):
            for n, (l, r) in enumerate(zip(lhsT, rhs)):
                ins = pe.matmul(dst, l, r, start=(n == 0), stop=(n == len(lhsT) - 1))
            if name:
                out(ins, name)

        def turn(dst, srcs, name):
            for d, src in zip(dst, srcs):
                ins = pe.transpose(d, src, ident[0:src.shape[0], 0:src.shape[0]])
            out(ins, name)

        def project_first(t, p):
            R = rows(t)
            pe.wait_ge(S["x_normed"], t + 1)
            for j, before in ((0, "z_copied"), (1, "dq_copied")):
                after(pe, before, t)
                turn([ps[:, j, n * R:(n + 1) * R] for n in range(4)],
                     [x[p][0:R, kd * P:(kd + 1) * P] for kd in range(4 * j, 4 * j + 4)], f"xT_ready{j}")
            for j, cts, before in ((0, range(0, 4), "kv_copied"), (1, range(4, 6), "xbc_copied1")):
                pe.wait_ge(S[f"xT_copied{j}"], t + 1)
                if j == 0:
                    pe.wait_ge(S["xT_copied1"], t + 1)
                after(pe, before, t)
                for n, ct in enumerate(cts):
                    product(ps[:, 2 + j, n * R:(n + 1) * R],
                            [w_in[:, kd, C_XBC + ct * P:C_XBC + (ct + 1) * P] for kd in range(KD)],
                            [xT[:, kd, 0:R] for kd in range(KD)], f"xbc_ready{j}" if ct == cts[-1] else None)
            product(ps[0:R, 0, :], [xT[:, kd, 0:R] for kd in range(KD)], [w_in[:, kd, 0:SW] for kd in range(KD)], "z_ready")

        def project_rest(t):
            R = rows(t)
            for b, lo, n, name in ((1, C_DT, N_DQ, "dq_ready"), (2, C_KV, N_KV, "kv_ready")):
                if b == 2:
                    pe.wait_ge(S["xbc_copied0"], t + 1)
                product(ps[0:R, b, 0:n], [xT[:, kd, 0:R] for kd in range(KD)],
                        [w_in[:, kd, lo:lo + n] for kd in range(KD)], name)

        def iteration(t, p, after_it):
            R = rows(t)
            C = META if R == ODD else P
            if after_it:
                project_first(t + 1, 1 - p)
            pe.wait_ge(S["cl_normed"], t + 1)
            after(pe, "kT_copied1", t)
            turn([ps[:, 4, n * R:(n + 1) * R] for n in range(4)],
                 [cq[0:R, n * P:(n + 1) * P] for n in range(3)] + [lat[0:R, 0:P]], "clT_ready0")
            pe.wait_ge(S["conv_silu"], t + 1)
            after(pe, "qT_copied1", t)
            turn([ps[0:R, 6, n * P:(n + 1) * P] for n in range(4)], [conv[:, n, 0:R] for n in range(4)], "xs_ready")
            nb = 2 if R == ODD else 1
            after(pe, "kT_copied0", t)
            turn([ps[:, 5, 0:R]], [lat[0:R, P:2 * P]], "clT_ready1")
            turn([ps[0:R, 5, (1 + n) * P:(2 + n) * P] for n in range(nb)], [conv[:, 4 + n, 0:R] for n in range(nb)], "bT_ready")
            pe.wait_ge(S["dt_done"], t + 1)
            after(pe, "qT_copied0", t)
            product(ps[0:C, 7, 0:SH], [upper[0:C, 0:C]], [dts[0:C, DTA, :]], "acs_ready")
            pe.wait_ge(S["ud_ready"], t + 1)
            pe.wait_ge(S["xs_copied"], t + 1)
            pe.wait_ge(S["xdt_ready"], t + 1)
            pe.wait_ge(S["acs_copied"], t + 1)
            for b in range(2):
                product(ps[:, 6 + b, 0:4 * C], [ones[0:C, :]], [ud[0:C, 4 * b:4 * b + 4, 0:C]], "bc_ready" if b else None)
            pe.wait_ge(S["cz_ready"], t + 1)
            pe.wait_ge(S["bn_copied"], t + 1)
            product(ps[0:C, 5, 2 * P:2 * P + 2 * C], [conv[:, 4, 0:C]], [cz[:, :, 0:C]], "cb_ready")
            if after_it:
                project_rest(t + 1)
            pe.wait_ge(S["clT_copied0"], t + 1)
            pe.wait_ge(S["clT_copied1"], t + 1)
            pe.wait_ge(S["cb_taken"], t + 1)
            for b in range(2):
                w = 4 * QK
                product(ps[0:R, 4 + b, 0:w], [clT[:, n, 0:R] for n in range(3)],
                        [w_uq[:, n, b * w:(b + 1) * w] for n in range(3)], "q_ready" if b else None)
            pe.wait_ge(S["seg_done"], t + 1)
            pe.wait_ge(S["last_exp"], t + 1)
            for b in range(2):
                product(ps[0:R, 6 + b, :], [clT[:, 3 + n, 0:R] for n in range(2)],
                        [w_ukv[:, n, b * 512:(b + 1) * 512] for n in range(2)], "kvu_ready" if b else None)
            pe.wait_ge(S["att_ready"], t + 1)
            pe.wait_ge(S["q_copied"], t + 1)
            for h in range(SH):
                product(ps[0:C, 4, h * SP_:(h + 1) * SP_], [seg[0:C, h, 0:C]], [xdt[0:C, h * SP_:(h + 1) * SP_]],
                        "yd_ready" if h == SH - 1 else None)
            after(pe, "state_done", t)
            for g in range(SG):
                product(ps[0:C, 5, 256 * g:256 * (g + 1)], [cz[:, g, 0:C]], [state[:, :]], "yo_ready" if g else None)
            pe.wait_ge(S["xw_ready"], t + 1)
            pe.wait_ge(S["yd_taken"], t + 1)
            product(ps[:, 4, :], [bn[0:C, 0:P]], [xw[0:C, :]], "st_ready")
            pe.wait_ge(S["q_normed"], t + 1)
            pe.wait_ge(S["kn_taken"], t + 1)
            pe.wait_ge(S["v_copied"], t + 1)
            for j, b in ((0, 7), (1, 6)):
                turn([ps[0:QK, b, n * R:(n + 1) * R] for n in range(4)],
                     [q[0:R, 4 * j + n, :] for n in range(4)], f"qT_ready{j}")
            pe.wait_ge(S["k_normed"], t + 1)
            for j, b, before in ((0, 5, "yo_taken"), (1, 4, "state_done")):
                pe.wait_ge(S[before], t + 1)
                turn([ps[0:QK, b, n * R:(n + 1) * R] for n in range(4)],
                     [k[0:R, 4 * j + n, :] for n in range(4)], f"kT_ready{j}")

        pe.wait_ge(S["consts"], 1)
        pe.wait_ge(smalls, 16 * N_SMALLS)
        turn([ps[:, 4, n * 3 * NS:(n + 1) * 3 * NS] for n in range(CT)],
             [sconv[:, n * P:(n + 1) * P] for n in range(CT)], "sconv_ready")
        pe.wait_ge(S["folded"], KD)
        project_first(0, 0)
        project_rest(0)
        pe.wait_ge(S["xbc_copied1"], 1)
        turn([ps[0:ODD, 6 + n // 4, n % 4 * P:(n % 4 + 1) * P] for n in range(CT)],
             [raw[0][:, n, 3:3 + ODD] for n in range(CT)], "rawn_ready")
        pe.wait_ge(S["rawn_copied"], 1)
        pe.wait_ge(S["sconv_copied"], 1)
        pe.wait_ge(S["up_folded"], 1)
        iteration(0, 0, True)
        with pe.Fori(0, 3) as i:
            iteration(i * 2 + 1, 1, True)
            iteration(i * 2 + 2, 0, True)
        iteration(7, 1, True)
        iteration(8, 0, False)
        pe.wait_ge(S["qT_copied1"], NT + 1)
        turn([ps[0:3, 6 + n // 4, n % 4 * P:(n % 4 + 1) * P] for n in range(CT)],
             [raw[0][:, n, P:P + 3] for n in range(CT)], "rawl_ready")
        pe.wait_ge(S["kT_copied0"], NT + 1)
        turn([ps[:, 5, n * P:(n + 1) * P] for n in range(2)], [state[:, n * P:(n + 1) * P] for n in range(2)], "stout_ready")

    ctx.close()
    nc.clear_and_free_semaphores(sems)
    nc.all_engine_barrier()


def attention_block(nc, s, att):
    ctx = ExitStack()
    sb = lambda name, shape: ctx.enter_context(nc.sbuf_tensor("a_" + name, shape, F32))
    sem = lambda name: ctx.enter_context(nc.semaphore("a_" + name))
    PAIRS = H // 2
    order = [(i + 1, P, META + i * P) for i in reversed(range(NT))]
    N = len(order)
    groups = []
    for n, (tile, _, _) in enumerate(order):
        blocks = list(range(tile + 1))
        groups.append([blocks[b:b + 2] for b in range(0, len(blocks), 2)])
    first_group = [sum(len(g) for g in groups[:n]) for n in range(N + 1)]
    G = first_group[N]

    ps = ctx.enter_context(nc.psum_tensor("a_ps", [P, 8, 512], F32))
    flat = ps[:, :, :].rearrange("p b c -> p (b c)")
    q = [sb(f"q{i}", [QK, 2, T]) for i in range(2)]
    k = [sb(f"k{i}", [QK, 2, T]) for i in range(2)]
    v = [sb(f"v{i}", [P, NT + 1, 2 * VD]) for i in range(2)]
    prob = [[sb(f"prob{i}{h}", [P, T]) for h in range(2)] for i in range(2)]
    pt = [sb(f"pt{i}", [P, 2, 2, P]) for i in range(2)]
    oT = [sb(f"oT{i}", [P, P]) for i in range(2)]
    st = [[sb(f"st{i}{h}", [P, 4]) for h in range(2)] for i in range(2)]
    mask = sb("mask", [P, P])
    ident = sb("ident", [P, P])
    credit = sb("credit", [P, 3])

    loaded = [sem(f"loaded{i}") for i in range(2)]
    consts, scores_ready, max_ready, exp_done, pt_ready = [
        sem(n) for n in ("consts", "scores_ready", "max_ready", "exp_done", "pt_ready")]
    pt_copied = [sem("pt_copied_by_dve"), sem("pt_copied_by_act")]
    o_ready, oT_copied, back_ready, att_done = [sem(n) for n in ("o_ready", "oT_copied", "back_ready", "att_done")]
    dve_steps = Steps(sem("dve_steps"), "attention dve")
    pool_steps = Steps(sem("pool_steps"), "attention pool")
    block = ctx.enter_context(nc.Block())

    def o_bank(n):
        return 5 if n % 2 else 2

    def width(n):
        tile, R, at = order[n]
        return at + R

    @block.sync
    def _(sp):
        for u in range(PAIRS):
            p = u % 2
            if u >= 2:
                sp.wait_ge(o_ready, (u - 1) * N)
            cols = slice(u * 2 * VD, (u + 1) * 2 * VD)
            for dst, src in (
                (q[p][:, :, :], s["qT"][2 * u:2 * u + 2, :, 0:T].rearrange("h d t -> d h t")),
                (k[p][:, :, :], s["kT"][2 * u:2 * u + 2, :, 0:T].rearrange("h d t -> d h t")),
                (v[p][0:META, 0, :], s["v"][0:META, cols]),
                (v[p][:, 1:NT + 1, :], s["v"][META:T, cols].rearrange("(j p) c -> p j c", p=P)),
            ):
                sp.dma_start(dst, src).then_inc(loaded[p], 16)

    @block.gpsimd
    def _(pool):
        pool_steps(pool, pool.memset(ident[:, :], 0.0))
        pool.affine_select(out=ident[:, :], in_=ident[:, :], compare_op=ALU.not_equal, fill=1.0,
                           base=0, pattern=[[-1, P]], channel_multiplier=1)
        pool_steps(pool, pool.memset(mask[:, :], 0.0))
        pool.memset(credit[:, 0:1], 0.0).then_inc(att_done, 1)
        pool.memset(credit[:, 1:2], 0.0).then_inc(pt_copied[0], 1)
        pool.memset(credit[:, 2:3], 0.0).then_inc(pt_copied[1], 1)
        pool.affine_select(out=mask[:, :], in_=mask[:, :], compare_op=ALU.is_ge, fill=NEG,
                           base=0, pattern=[[-1, P]], channel_multiplier=1).then_inc(consts, 1)

    def copy_groups(eng, i, par, n, mine, copied):
        R = order[n][1]
        for g, blocks in enumerate(groups[n]):
            gg = par * G + first_group[n] + g
            if gg % 2 != mine:
                continue
            eng.wait_ge(pt_ready, i * 2 * G + gg + 1)
            src = ps[:, 6 + gg % 2, :].rearrange("p (b h r) -> p b h r", b=2, r=P)[:, :, :, 0:R]
            dst = pt[gg % 2][:, :, :, 0:R]
            pieces = [(META, 0, 1)] + [(P, 1, 2)] * (len(blocks) - 1) if blocks[0] == 0 else [(P, 0, len(blocks))]
            for rows_, lo, hi in pieces:
                if mine == 0:
                    ins = eng.tensor_copy(dst[0:rows_, lo:hi], src[0:rows_, lo:hi])
                else:
                    ins = eng.activation(dst[0:rows_, lo:hi], src[0:rows_, lo:hi], ACT.Copy)
            ins.then_inc(copied, 1)

    @block.vector
    def _(dve):
        def maximum(u, n):
            tile, R, at = order[n]
            for h in range(2):
                t = st[n % 2][h]
                dve.wait_ge(scores_ready, u * 2 * N + 2 * n + h + 1)
                own = flat[0:R, 1536 * h + at:1536 * h + at + R]
                dve_steps(dve, dve.tensor_tensor(out=own, in0=own, in1=mask[0:R, 0:R], op=ALU.add))
                dve_steps(dve, dve.tensor_reduce(t[0:R, 0:1], flat[0:R, 1536 * h:1536 * h + at + R], AXX, ALU.max))
                dve.tensor_scalar(t[0:R, 1:2], t[0:R, 0:1], -SCALE, None, ALU.mult).then_inc(max_ready, 1)

        def finish(u, n):
            tile, R, at = order[n]
            for h in range(2):
                ins = dve.reciprocal(st[n % 2][h][0:R, 3:4], st[n % 2][h][0:R, 2:3])
            dve_steps(dve, ins)
            dve.wait_ge(back_ready, u * N + n + 1)
            for h in range(2):
                ins = dve.tensor_scalar(att[0:R, tile, ds(u * 2 * VD + h * VD, VD)],
                                        ps[0:R, o_bank(n), P + h * VD:P + (h + 1) * VD],
                                        st[n % 2][h][0:R, 3:4], None, ALU.mult)
            ins.then_inc(att_done, 1)

        dve.wait_ge(consts, 1)
        with dve.Fori(0, PAIRS // 2) as i:
            dve_steps.begin(i, 2 * N * 5)
            for par in range(2):
                for n in range(N + 2):
                    if n >= 2:
                        finish(i * 2 + par, n - 2)
                    if n < N:
                        maximum(i * 2 + par, n)
                    if 1 <= n <= N:
                        copy_groups(dve, i, par, n - 1, 0, pt_copied[0])
            dve_steps.end(PAIRS // 2)

    @block.scalar
    def _(act):
        with act.Fori(0, PAIRS // 2) as i:
            for par in range(2):
                u = i * 2 + par
                for n in range(N + 1):
                    if n < N:
                        tile, R, at = order[n]
                        for h in range(2):
                            t = st[n % 2][h]
                            act.wait_ge(max_ready, u * 2 * N + 2 * n + h + 1)
                            act.activation(prob[n % 2][h][0:R, 0:at + R], flat[0:R, 1536 * h:1536 * h + at + R], ACT.Exp,
                                           bias=t[0:R, 1:2], scale=SCALE, accum_out=t[0:R, 2:3]).then_inc(exp_done, 1)
                    if n >= 1:
                        copy_groups(act, i, par, n - 1, 1, pt_copied[1])
                        R = order[n - 1][1]
                        act.wait_ge(o_ready, u * N + n)
                        act.activation(oT[(n - 1) % 2][:, 0:R], ps[:, o_bank(n - 1), 0:R], ACT.Copy).then_inc(oT_copied, 1)

    @block.tensor
    def _(pe):
        def scores(i, par, n):
            u = i * 2 + par
            tile, R, at = order[n]
            L = at + R
            if n == 0:
                pe.wait_ge(loaded[par], (i + 1) * 64)
                pe.wait_ge(att_done, u * N + 1)
            for h in range(2):
                if n > 0:
                    pe.wait_ge(exp_done, u * 2 * N + 2 * (n - 1) + h + 1)
                for c in range(0, L, 512):
                    w = min(512, L - c)
                    ins = pe.matmul(ps[0:R, 3 * h + c // 512, 0:w], q[par][:, h, at:at + R], k[par][:, h, c:c + w],
                                    start=True, stop=True)
                ins.then_inc(scores_ready, 1)

        def turn(i, par, n, g):
            gg = par * G + first_group[n] + g
            pe.wait_ge(pt_copied[gg % 2], i * G + gg // 2 + 1)
            for b, blk in enumerate(groups[n][g]):
                lo, w = (0, META) if blk == 0 else (META + (blk - 1) * P, P)
                for h in range(2):
                    c = (b * 2 + h) * P
                    ins = pe.transpose(ps[0:w, 6 + gg % 2, c:c + P], prob[n % 2][h][:, lo:lo + w], ident[:, :])
            ins.then_inc(pt_ready, 1)

        def weigh(i, par, n, g):
            R = order[n][1]
            gg = par * G + first_group[n] + g
            pe.wait_ge(pt_copied[gg % 2], i * G + gg // 2 + 2)
            for b, blk in enumerate(groups[n][g]):
                w = META if blk == 0 else P
                for h in range(2):
                    ins = pe.matmul(ps[h * VD:(h + 1) * VD, o_bank(n), 0:R], v[par][0:w, blk, h * VD:(h + 1) * VD],
                                    pt[gg % 2][0:w, b, h, 0:R], start=(blk == 0), stop=(blk == groups[n][-1][-1]))
            if g == len(groups[n]) - 1:
                ins.then_inc(o_ready, 1)

        def values(i, par, n):
            u = i * 2 + par
            pe.wait_ge(exp_done, u * 2 * N + 2 * n + 2)
            if n >= 2:
                pe.wait_ge(att_done, u * N + n)
            turn(i, par, n, 0)
            for g in range(len(groups[n])):
                if g + 1 < len(groups[n]):
                    turn(i, par, n, g + 1)
                weigh(i, par, n, g)

        def back(i, par, n):
            u = i * 2 + par
            R = order[n][1]
            pe.wait_ge(oT_copied, u * N + n + 1)
            pe.transpose(ps[0:R, o_bank(n), P:2 * P], oT[n % 2][:, 0:R], ident[:, :]).then_inc(back_ready, 1)

        def pair(i, par):
            for n in range(N + 2):
                if n < N:
                    scores(i, par, n)
                if n >= 2:
                    back(i, par, n - 2)
                if 1 <= n <= N:
                    values(i, par, n - 1)

        pe.wait_ge(consts, 1)
        with pe.Fori(0, PAIRS // 2) as i:
            pair(i, 0)
            pair(i, 1)

    ctx.close()


def samples_block(nc, a, s, att):
    ctx = ExitStack()
    sb = lambda name, shape, dt=F32: ctx.enter_context(nc.sbuf_tensor("s_b_" + name, shape, dt))
    sem = lambda name: ctx.enter_context(nc.semaphore("s_" + name))
    GP = 4
    NG = NPG // GP
    HP = 32
    BH = NS * SH

    ps = ctx.enter_context(nc.psum_tensor("s_ps", [P, 8, 512], F32))
    ids = sb("ids", [1, NS * NPG], I32)
    latn = [sb(f"latn{i}", [P, NPG, LATW]) for i in range(2)]
    latT = [sb(f"latT{i}", [P, 3, GP, P]) for i in range(2)]
    wk = sb("wk", [P, 2, H * NOPE])
    wv = sb("wv", [P, 2, H * VD])
    wkT = sb("wkT", [NOPE, H, 2, P])
    qn = sb("qn", [NOPE, H, NS])
    qr = sb("qr", [ROPE, H, NS])
    qabs = sb("qabs", [P, 3, NS, HP])
    qab = [sb(f"qab{i}", [P, 3, HP]) for i in range(2)]
    ksq = [sb(f"ksq{i}", [P, H * NOPE]) for i in range(2)]
    krsq = sb("krsq", [P, NPG, ROPE])
    krs = sb("krs", [P, NPG])
    ssq = [sb(f"ssq{i}", [P, NPG, H]) for i in range(2)]
    rs = sb("rs", [P, NPG, H])
    sraw = [sb(f"sraw{i}", [P, NPG, H]) for i in range(2)]
    scs = [sb(f"scs{i}", [P, P]) for i in range(2)]
    mxp = sb("mxp", [P, H])
    mxa = sb("mxa", [P, H])
    waited = sb("waited", [P, 1])
    prob = sb("prob", [P, NPG, HP])
    lp = sb("lp", [P, H])
    ol = sb("ol", [P, KL])
    oLT = sb("oLT", [P, 2, H, NS])
    m_all = sb("m_all", [1, NS * H])
    l_all = sb("l_all", [1, NS * H])
    ident = sb("ident", [P, P])
    ones = sb("ones", [P, 1])
    sel = sb("sel", [P, H])
    mhalf = sb("mhalf", [P, 2])
    eps = sb("eps", [P, 2])
    q1, k1 = sb("q1", [NS, H, QK]), sb("k1", [NS, H, QK])
    gq, gk = sb("gq", [NS, QK]), sb("gk", [NS, QK])
    v1 = sb("v1", [NS, H * VD])
    mg = sb("mg", [NS, 10, H])
    M_, L_, SNEW, MT, A_, E_, LT, RL, AR, ER = range(10)
    oup = sb("oup", [NS, H * VD])
    h0 = sb("h0", [BH, SP_, SN])
    u0 = sb("u0", [BH, SP_, SN])
    xb, Bs, Cs = sb("xb", [BH, SP_]), sb("Bs", [BH, SN]), sb("Cs", [BH, SN])
    xd = sb("xd", [BH, SP_])
    sy = sb("sy", [BH, SP_])
    dt1, dta, dec, dsk = sb("dt1", [BH, 1]), sb("dta", [BH, 1]), sb("dec", [BH, 1]), sb("dsk", [BH, 1])
    yn, zn, yj = sb("yn", [NS, SW]), sb("zn", [NS, SW]), sb("yj", [NS, SW])
    ysm = sb("ysm", [NS, 4])

    lat_loaded = [[sem(f"lat_loaded{i}{g}") for g in range(NG)] for i in range(2)]
    ids_loaded, w_loaded, ssd_loaded, new_loaded, y_stored, y_loaded = [
        sem(n) for n in "ids_loaded w_loaded ssd_loaded new_loaded y_stored y_loaded".split()]
    ml_moved, stored = sem("ml_moved"), sem("stored")
    names = """consts ln_done wkT_ready wkT_copied qabs_ready qabs_copied qrope_copied qab_ready ta_ready tb_ready tc_ready ta_copied
    tb_copied tc_copied k_ready sq_done red_done sc_ready sc_copied scT_ready sraw_done krsq_done ssq_done rs_ready
    f2_done mxa_ready f3_done prob_ready lp_ready o_ready ol_copied oT_ready oT_copied up_ready up_copied
    new_prod new_sum merge_in merge_exp att_done
    dec_done xd_done u_done h1_done hc_done sy_done y_gated y_squared y_rstd y_normed m_saved""".split()
    S = {n: sem(n) for n in names}
    pool_steps, dve_steps = Steps(sem("pool_steps"), "samples pool"), Steps(sem("dve_steps"), "samples dve")
    N_W, N_SSD, N_NEW = 4, 1 + 1 + 8 + 2 + 8 + 1, 3 + 6
    block = ctx.enter_context(nc.Block())

    def out(ins, name):
        ins.then_inc(S[name], 1)

    def after(eng, name, n):
        if not (isinstance(n, int) and n <= 0):
            eng.wait_ge(S[name], n)

    @block.sync
    def _(sp):
        sp.dma_start(ids[:, :], a["page_table"].rearrange("b n -> (b n)").unsqueeze(0)).then_inc(ids_loaded, 16)
        sp.wait_ge(ids_loaded, 16)

        def load_pages(b, p):
            if not (isinstance(b, int) and b < 2):
                sp.wait_ge(S["o_ready"], b)
                sp.wait_ge(ids_loaded, 16)
            for pg in range(NPG):
                with sp.register(f"page{'_first' if isinstance(b, int) else ''}{p}_{pg}") as reg:
                    sp.reg_load(reg, ids[0:1, ds(b * NPG + pg, 1)])
                    page = sp.snap(reg, min_val=0, max_val=a["cache_kv_latent"].shape[1] - 1)
                    sem_ = lat_loaded[p][pg // GP]
                    sp.dma_start(latn[p][:, pg, 0:KL],
                                 a["cache_kv_latent"][0, ds(page, 1), :, :].rearrange("o t d -> (o t) d")).then_inc(sem_, 16)
                    sp.dma_start(latn[p][:, pg, KL:LATW],
                                 a["cache_k_rope"][0, ds(page, 1), :, :].rearrange("o t d -> (o t) d")).then_inc(sem_, 16)

        load_pages(0, 0)
        load_pages(1, 1)
        with sp.Fori(1, NS // 2) as i:
            load_pages(i * 2, 0)
            load_pages(i * 2 + 1, 1)
        sp.wait_ge(S["y_normed"], 1)
        sp.dma_start(s["ys"][T:TOK, :], yn[:, :]).then_inc(stored, 16)
        sp.wait_ge(S["m_saved"], NS)
        sp.wait_ge(S["ol_copied"], NS)
        sp.dma_start(mg[:, M_, :], m_all[0:1, :].rearrange("o (b h) -> o b h", b=NS)).then_inc(ml_moved, 16)
        sp.dma_start(mg[:, L_, :], l_all[0:1, :].rearrange("o (b h) -> o b h", b=NS)).then_inc(ml_moved, 16)
        sp.wait_ge(S["att_done"], 1)
        sp.dma_start(att[0:NS, 0, :], oup[:, :]).then_inc(stored, 16)
        sp.wait_ge(stored, 32)

    def group_of(b, g):
        return b * NG + g

    def following(b, g):
        return (b, g + 1) if g + 1 < NG else (b + 1, 0)

    @block.scalar
    def _(act):
        ukv = a["w_ukv"][0].rearrange("(c p) (h x) -> p c h x", p=P, x=NOPE + VD)
        for c in range(2):
            act.dma_start(by_head(wk[:, c, :], NOPE), ukv[:, c, :, 0:NOPE]).then_inc(w_loaded, 16)
        act.dma_start(qn[:, :, :], s["qT"][:, 0:NOPE, T:TOK].rearrange("h d b -> d h b")).then_inc(w_loaded, 16)
        act.dma_start(qr[:, :, :], s["qT"][:, NOPE:QK, T:TOK].rearrange("h d b -> d h b")).then_inc(w_loaded, 16)
        act.dma_start(h0[:, :, :], a["state_ssm"][0].rearrange("b h p n -> (b h) p n")).then_inc(ssd_loaded, 16)
        act.dma_start(xb[:, :], s["s_x"].rearrange("b (h p) -> (b h) p", p=SP_)).then_inc(ssd_loaded, 16)
        for r in range(4):
            for dst, lo in ((Bs, 0), (Cs, P)):
                act.dma_start(dst[r:BH:4, :], s["s_bc"][:, lo:lo + P].rearrange("b (g n) -> b g n", n=SN)).then_inc(ssd_loaded, 16)
        act.dma_start(dt1[:, :], s["s_dt"].rearrange("b h -> (b h)").unsqueeze(1)).then_inc(ssd_loaded, 16)
        act.dma_start(dta[:, :], s["s_dta"].rearrange("b h -> (b h)").unsqueeze(1)).then_inc(ssd_loaded, 16)
        for b in range(NS):
            act.dma_start(dsk[b * SH:(b + 1) * SH, :], a["d_skip"].rearrange("o h -> h o")).then_inc(ssd_loaded, 16)
        act.dma_start(zn[:, :], s["s_z"]).then_inc(ssd_loaded, 16)
        act.wait_ge(w_loaded, 16 * N_W)
        for j in range(4):
            act.wait_ge(S["wkT_ready"], j + 1)
            out(act.activation(wkT[:, 2 * j:2 * j + 2, :, :].rearrange("p h c l -> p (h c l)"), ps[0:NOPE, j, :], ACT.Copy), "wkT_copied")
        act.wait_ge(S["consts"], 1)
        out(act.activation(qabs[0:ROPE, 2, :, 0:H], qr[:, :, :].rearrange("p h b -> p b h"), ACT.Copy), "qrope_copied")

        def copy_turned(b, g):
            act.wait_ge(S["ta_ready"], group_of(b, g) + 1)
            out(act.activation(latT[g % 2][:, 0:2, 0:2, :], ps[:, 0, :].rearrange("p (c j t) -> p c j t", c=2, t=P), ACT.Copy),
                "ta_copied")

        def slot(b, p, g, ahead, behind):
            gg = group_of(b, g)
            if ahead:
                copy_turned(*following(b, g))
            for j in range(GP):
                n = gg * GP + j
                act.wait_ge(S["k_ready"], n + 1)
                if not (isinstance(b, int) and b == 0 and g == 0 and j < 2):
                    act.wait_ge(S["red_done"], n - 1)
                out(act.activation(ksq[j % 2][:, :], ps[:, 3 + j % 2, :], ACT.Square, scale=QK ** -0.5), "sq_done")
            act.wait_ge(S["sc_ready"], gg + 1)
            out(act.activation(scs[g % 2][:, :], ps[:, 5, 0:P], ACT.Copy), "sc_copied")
            if behind and g == 0:
                rstd(b - 1, 1 - p)
            if behind and g == 2:
                act.wait_ge(S["f3_done"], b)
                act.wait_ge(S["o_ready"], b)
                out(act.activation(prob[:, :, 0:H], sraw[1 - p][:, :, :], ACT.Exp, scale=SCALE), "prob_ready")
            if behind and g == 4:
                save_ol(b - 1)

        def rstd(b, p):
            act.wait_ge(S["ssq_done"], b + 1)
            out(act.activation(rs[:, :, :], ssq[p][:, :, :], ACT.Ln), "ln_done")
            act.wait_ge(S["ln_done"], b + 1)
            out(act.activation(rs[:, :, :], rs[:, :, :], ACT.Exp, scale=-0.5), "rs_ready")

        def save_ol(b):
            act.wait_ge(S["o_ready"], b + 2)
            act.wait_ge(S["oT_ready"], b + 1)
            act.activation(ol[:, :], ps[:, 7, 0:KL], ACT.Copy)
            out(act.activation(l_all[:, ds(b * H, H)], ps[0:1, 7, KL:KL + H], ACT.Copy), "ol_copied")

        copy_turned(0, 0)
        for g in range(NG):
            slot(0, 0, g, True, False)
            if g == 1:
                act.wait_ge(ssd_loaded, 16 * N_SSD)
                out(act.activation(dec[:, :], dta[:, :], ACT.Exp), "dec_done")
        act.dma_start(wv[:, 0, :].rearrange("p (h x) -> p h x", x=VD), ukv[:, 0, :, NOPE:]).then_inc(new_loaded, 16)
        act.dma_start(wv[:, 1, :].rearrange("p (h x) -> p h x", x=VD), ukv[:, 1, :, NOPE:]).then_inc(new_loaded, 16)
        act.dma_start(q1[:, :, :], s["s_q"]).then_inc(new_loaded, 16)
        act.dma_start(k1[:, :, :], s["s_k"]).then_inc(new_loaded, 16)
        act.dma_start(v1[:, :], s["v"][T:TOK, :]).then_inc(new_loaded, 16)
        for dst, n in ((gq, "q"), (gk, "k")):
            act.dma_start(dst[:, 0:NOPE], a[n + "_head_g_nope"].to_broadcast([NS, NOPE])).then_inc(new_loaded, 16)
            for j in range(2):
                act.dma_start(dst[:, NOPE + j * HALF:NOPE + (j + 1) * HALF],
                              a[n + "_head_g_rope"].to_broadcast([NS, HALF])).then_inc(new_loaded, 16)
        with act.Fori(0, 3) as i:
            for p, b in ((1, i * 2 + 1), (0, i * 2 + 2)):
                for g in range(NG):
                    slot(b, p, g, True, True)
        for g in range(NG):
            slot(NS - 1, 1, g, g + 1 < NG, True)
            if g == 1:
                act.wait_ge(S["y_gated"], 1)
                for gr in range(SG):
                    w = SW // SG
                    ins = act.activation(yj[:, gr * w:(gr + 1) * w], yn[:, gr * w:(gr + 1) * w], ACT.Square,
                                         scale=w ** -0.5, accum_out=ysm[:, gr:gr + 1])
                out(ins, "y_squared")
        rstd(NS - 1, 1)
        act.wait_ge(S["f3_done"], NS)
        act.wait_ge(S["o_ready"], NS)
        out(act.activation(prob[:, :, 0:H], sraw[1][:, :, :], ACT.Exp, scale=SCALE), "prob_ready")
        save_ol(NS - 1)
        act.wait_ge(S["merge_in"], 1)
        out(act.activation(mg[:, A_:E_ + 1, :], mg[:, A_:E_ + 1, :], ACT.Exp, scale=SCALE), "merge_exp")

    @block.gpsimd
    def _(pool):
        pool_steps(pool, pool.memset(ident[:, :], 0.0))
        pool.affine_select(out=ident[:, :], in_=ident[:, :], compare_op=ALU.not_equal, fill=1.0,
                           base=0, pattern=[[-1, P]], channel_multiplier=1)
        pool_steps(pool, pool.memset(sel[:, :], 0.0))
        for j in range(4):
            pool_steps(pool, pool.affine_select(out=sel[:, :], in_=sel[:, :], compare_op=ALU.not_equal, fill=1.0,
                                                base=-HP * j, pattern=[[-1, H]], channel_multiplier=1))
        pool.memset(ones[:, :], 1.0).then_inc(S["o_ready"], 1)
        pool.memset(mhalf[:, :], -0.5).then_inc(S["oT_ready"], 1)
        pool.memset(eps[:, :], EPS).then_inc(S["oT_copied"], 1)
        pool.memset(qabs[:, :, :, :], 0.0)
        pool.memset(prob[:, :, :], 0.0)
        pool.memset(latT[0][:, 2, :, :], 0.0)
        out(pool.memset(latT[1][:, 2, :, :], 0.0), "consts")

        def rope_squares(b, p):
            for g in range(NG):
                pool.wait_ge(lat_loaded[p][g], (b - p + 2) * (GP * 16))
            after(pool, "ssq_done", b)
            out(pool.tensor_tensor(out=krsq[:, :, :], in0=latn[p][:, :, KL:LATW], in1=latn[p][:, :, KL:LATW],
                                   op=ALU.mult), "krsq_done")

        def maxima(b):
            pool.wait_ge(S["f2_done"], b + 1)
            pool.tensor_tensor(out=waited[:, :], in0=eps[:, 0:1], in1=eps[:, 0:1], op=ALU.mult)
            out(pool.partition_all_reduce(mxa[:, :], mxp[:, :], P, RMAX), "mxa_ready")

        rope_squares(0, 0)
        pool.wait_ge(ssd_loaded, 16 * N_SSD)
        pool_steps(pool, pool.tensor_tensor(out=xd[:, :], in0=xb[:, :], in1=dt1[:, :].to_broadcast([BH, SP_]), op=ALU.mult))
        out(pool.tensor_tensor(out=u0[:, :, :], in0=bc(xd[:, :], SN, 2), in1=bc(Bs[:, :], SP_, 1), op=ALU.mult), "u_done")
        pool.wait_ge(S["h1_done"], 1)
        out(pool.tensor_tensor(out=u0[:, :, :], in0=h0[:, :, :], in1=bc(Cs[:, :], SP_, 1), op=ALU.mult), "hc_done")
        pool.dma_start(a["ssm_sample"][0].rearrange("b h p n -> (b h) p n"), h0[:, :, :]).then_inc(y_stored, 16)
        pool.wait_ge(S["sy_done"], 1)
        pool.wait_ge(y_stored, 16)
        pool.dma_start(s["s_y"].rearrange("b (h p) -> (b h) p", p=SP_), sy[:, :]).then_inc(y_stored, 16)
        pool.wait_ge(y_stored, 32)
        pool.dma_start(yn[:, :], s["s_y"]).then_inc(y_loaded, 16)
        maxima(0)
        with pool.Fori(0, 3) as i:
            rope_squares(i * 2 + 1, 1)
            maxima(i * 2 + 1)
            rope_squares(i * 2 + 2, 0)
            maxima(i * 2 + 2)
        rope_squares(NS - 1, 1)
        pool.wait_ge(S["y_squared"], 1)
        pool_steps(pool, pool.tensor_tensor(out=ysm[:, 0:2], in0=ysm[:, 0:2], in1=eps[0:NS, 0:2], op=ALU.add))
        out(pool.tensor_tensor(out=ysm[:, 2:4], in0=ysm[:, 0:2], in1=mhalf[0:NS, 0:2], op=ALU.pow), "y_rstd")
        maxima(NS - 1)

    @block.vector
    def _(dve):
        def copy_turned(b, g):
            gg = group_of(b, g)
            dve.wait_ge(S["tb_ready"], gg + 1)
            out(dve.tensor_copy(latT[g % 2][:, 0:2, 2:4, :], ps[:, 1, :].rearrange("p (c j t) -> p c j t", c=2, t=P)),
                "tb_copied")
            dve.wait_ge(S["tc_ready"], gg + 1)
            out(dve.tensor_copy(latT[g % 2][0:ROPE, 2, :, :].rearrange("p j t -> p (j t)"), ps[0:ROPE, 2, :]), "tc_copied")

        def take_query(b, p):
            after(dve, "sc_ready", (b - 1) * NG)
            out(dve.tensor_scalar(qab[p][:, :, :], qabs[:, :, ds(b, 1), :].rearrange("p c o h -> p c (o h)"),
                                  1.0, None, ALU.mult), "qab_ready")

        def keep_scores(b, p, g):
            gg = group_of(b, g)
            dve.wait_ge(S["scT_ready"], gg + 1)
            out(dve.tensor_copy(sraw[p][:, GP * g:GP * (g + 1), :],
                                ps[:, 6, 0:P].rearrange("p (j h) -> p j h", h=HP)[:, :, 0:H]), "sraw_done")

        def finish(b, p, step):
            if step == 0:
                dve.wait_ge(S["krsq_done"], b + 1)
                dve_steps(dve, dve.tensor_reduce(krs[:, :], krsq[:, :, :], AXX, ALU.add))
                dve.wait_ge(S["red_done"], (b + 1) * NPG)
                dve_steps(dve, dve.scalar_tensor_tensor(out=ssq[p][:, :, :], in0=bc(krs[:, :], H, 2), scalar=1.0 / QK,
                                             in1=ssq[p][:, :, :], op0=ALU.mult, op1=ALU.add))
                out(dve.tensor_scalar(ssq[p][:, :, :], ssq[p][:, :, :], EPS, None, ALU.add), "ssq_done")
            if step == 1:
                dve.wait_ge(S["rs_ready"], b + 1)
                dve_steps(dve, dve.tensor_tensor(out=ssq[p][:, :, :], in0=ssq[p][:, :, :], in1=rs[:, :, :], op=ALU.mult))
                dve_steps(dve, dve.tensor_tensor(out=ssq[p][:, :, :], in0=ssq[p][:, :, :], in1=rs[:, :, :], op=ALU.mult))
                dve_steps(dve, dve.tensor_scalar(ssq[p][:, :, :], ssq[p][:, :, :], -0.5, 1.5, ALU.mult, ALU.add))
                dve_steps(dve, dve.tensor_tensor(out=rs[:, :, :], in0=ssq[p][:, :, :], in1=rs[:, :, :], op=ALU.mult))
                dve.wait_ge(S["sraw_done"], (b + 1) * NG)
                dve_steps(dve, dve.tensor_tensor(out=sraw[p][:, :, :], in0=sraw[p][:, :, :], in1=rs[:, :, :], op=ALU.mult))
                out(dve.tensor_reduce(mxp[:, :], sraw[p][:, :, :].rearrange("p n h -> p h n"), AXX, ALU.max), "f2_done")
            if step == 2:
                dve.wait_ge(S["mxa_ready"], b + 1)
                out(dve.tensor_tensor(out=sraw[p][:, :, :], in0=sraw[p][:, :, :], in1=bc(mxa[:, :], NPG, 1),
                                      op=ALU.subtract), "f3_done")
                out(dve.tensor_scalar(m_all[:, ds(b * H, H)], mxa[0:1, :], 1.0, None, ALU.mult), "m_saved")
            if step == 3:
                dve.wait_ge(S["prob_ready"], b + 1)
                out(dve.tensor_reduce(lp[:, :], prob[:, :, 0:H].rearrange("p n h -> p h n"), AXX, ALU.add), "lp_ready")

        def keep_output(b):
            dve.wait_ge(S["oT_ready"], b + 2)
            out(dve.tensor_scalar(oLT[:, :, :, ds(b, 1)].rearrange("p c h o -> p (c h o)"), ps[:, 7, 0:2 * H],
                                  1.0, None, ALU.mult), "oT_copied")

        def slot(b, p, g, ahead, behind):
            gg = group_of(b, g)
            if ahead:
                copy_turned(*following(b, g))
            if g == 0 and behind:
                keep_scores(b - 1, 1 - p, NG - 1)
            for j in range(GP):
                dve.wait_ge(S["sq_done"], gg * GP + j + 1)
                out(dve.tensor_reduce(ssq[p][:, GP * g + j, :], by_head(ksq[j % 2][:, :], NOPE), AXX, ALU.add), "red_done")
            if g > 0:
                keep_scores(b, p, g - 1)
            if behind:
                if g < 2:
                    finish(b - 1, 1 - p, g)
                if g == 2:
                    finish(b - 1, 1 - p, 2)
                if g == 3:
                    finish(b - 1, 1 - p, 3)
            if g == 6 and not (isinstance(b, int) and b == NS - 1):
                take_query(b + 1, 1 - p)

        dve.wait_ge(S["qabs_ready"], 1)
        out(dve.tensor_copy(qabs[:, 0:2, :, 0:H], ps[:, 4, 0:2 * H * NS].rearrange("p (c h b) -> p c b h", c=2, h=H)), "qabs_copied")
        dve.wait_ge(S["qabs_copied"], 1)
        dve.wait_ge(S["qrope_copied"], 1)
        take_query(0, 0)
        dve.wait_ge(S["consts"], 1)
        copy_turned(0, 0)
        for g in range(NG):
            slot(0, 0, g, True, False)
            if g == 4:
                dve.wait_ge(S["u_done"], 1)
                dve.wait_ge(S["dec_done"], 1)
                out(dve.scalar_tensor_tensor(out=h0[:, :, :], in0=h0[:, :, :], scalar=dec[:, 0:1], in1=u0[:, :, :],
                                             op0=ALU.mult, op1=ALU.add), "h1_done")
            if g == 7:
                dve.wait_ge(S["hc_done"], 1)
                dve_steps(dve, dve.tensor_reduce(sy[:, :], u0[:, :, :], AXX, ALU.add))
                out(dve.scalar_tensor_tensor(out=sy[:, :], in0=xb[:, :], scalar=dsk[:, 0:1], in1=sy[:, :],
                                             op0=ALU.mult, op1=ALU.add), "sy_done")
        with dve.Fori(0, 3) as i:
            dve_steps.begin(i, 14)
            for p, b in ((1, i * 2 + 1), (0, i * 2 + 2)):
                for g in range(NG):
                    slot(b, p, g, True, True)
                    if g == 5:
                        keep_output(b - 1)
            dve_steps.end(3)
        for g in range(NG):
            slot(NS - 1, 1, g, g + 1 < NG, True)
            if g == 5:
                keep_output(NS - 2)
            if g == 0:
                dve.wait_ge(y_loaded, 16)
                out(dve.tensor_tensor(out=yn[:, :], in0=yn[:, :], in1=zn[:, :], op=ALU.mult), "y_gated")
            if g == 4:
                dve.wait_ge(S["y_rstd"], 1)
                for gr in range(SG):
                    w = SW // SG
                    ins = dve.tensor_scalar(yn[:, gr * w:(gr + 1) * w], yn[:, gr * w:(gr + 1) * w],
                                            ysm[:, 2 + gr:3 + gr], None, ALU.mult)
                out(ins, "y_normed")
        keep_scores(NS - 1, 1, NG - 1)
        for step in range(4):
            finish(NS - 1, 1, step)
        dve.wait_ge(new_loaded, 16 * (N_NEW + 2))
        dve_steps(dve, dve.tensor_tensor(out=gq[:, :], in0=gq[:, :], in1=gk[:, :], op=ALU.mult))
        dve_steps(dve, dve.tensor_tensor(out=k1[:, :, :], in0=k1[:, :, :], in1=bc(gq[:, :], H, 1), op=ALU.mult))
        dve_steps(dve, dve.tensor_tensor(out=q1[:, :, :], in0=q1[:, :, :], in1=k1[:, :, :], op=ALU.mult))
        dve_steps(dve, dve.tensor_reduce(mg[:, SNEW, :], q1[:, :, :], AXX, ALU.add))
        keep_output(NS - 1)
        dve.wait_ge(ml_moved, 32)
        dve_steps(dve, dve.tensor_tensor(out=mg[:, MT, :], in0=mg[:, M_, :], in1=mg[:, SNEW, :], op=ALU.max))
        dve.tensor_tensor(out=mg[:, A_, :], in0=mg[:, M_, :], in1=mg[:, MT, :], op=ALU.subtract)
        out(dve.tensor_tensor(out=mg[:, E_, :], in0=mg[:, SNEW, :], in1=mg[:, MT, :], op=ALU.subtract), "merge_in")
        dve.wait_ge(S["merge_exp"], 1)
        dve_steps(dve, dve.tensor_tensor(out=mg[:, LT, :], in0=mg[:, L_, :], in1=mg[:, A_, :], op=ALU.mult))
        dve_steps(dve, dve.tensor_tensor(out=mg[:, LT, :], in0=mg[:, LT, :], in1=mg[:, E_, :], op=ALU.add))
        dve_steps(dve, dve.reciprocal(mg[:, RL, :], mg[:, LT, :]))
        dve.tensor_tensor(out=mg[:, AR, :], in0=mg[:, A_, :], in1=mg[:, RL, :], op=ALU.mult)
        dve_steps(dve, dve.tensor_tensor(out=mg[:, ER, :], in0=mg[:, E_, :], in1=mg[:, RL, :], op=ALU.mult))
        dve.tensor_tensor(out=by_head(v1[:, :], VD), in0=by_head(v1[:, :], VD), in1=bc(mg[:, ER, :], VD, 2), op=ALU.mult)
        dve.wait_ge(S["up_ready"], 1)
        dve_steps(dve, dve.tensor_tensor(out=by_head(oup[:, :], VD), in0=by_head(ps[0:NS, 0, :], VD),
                                         in1=bc(mg[:, AR, :], VD, 2), op=ALU.mult))
        out(dve.tensor_tensor(out=oup[:, :], in0=oup[:, :], in1=v1[:, :], op=ALU.add), "att_done")

    @block.tensor
    def _(pe):
        pe.wait_ge(S["consts"], 1)
        pe.wait_ge(w_loaded, 16 * N_W)
        for j in range(4):
            for n in range(4):
                h, c = 2 * j + n // 2, n % 2
                ins = pe.transpose(ps[0:NOPE, j, n * P:(n + 1) * P], wk[:, c, h * NOPE:(h + 1) * NOPE], ident[:, :])
            out(ins, "wkT_ready")
        pe.wait_ge(S["wkT_copied"], 4)
        for c in range(2):
            for h in range(H):
                at = (c * H + h) * NS
                ins = pe.matmul(ps[:, 4, at:at + NS], wkT[:, h, c, :], qn[:, h, :], start=True, stop=True)
        out(ins, "qabs_ready")

        def turn(b, p, g):
            gg = group_of(b, g)
            pe.wait_ge(lat_loaded[p][g], (b - p + 2) * (GP * 16))
            page = lambda j, lo, hi: latn[p][:, GP * g + j, lo:hi]
            for bank, name in ((0, "ta"), (1, "tb")):
                after(pe, name + "_copied", gg)
                for c in range(2):
                    for j in range(2):
                        at = (c * 2 + j) * P
                        ins = pe.transpose(ps[:, bank, at:at + P], page(2 * bank + j, c * P, (c + 1) * P), ident[:, :])
                out(ins, name + "_ready")
            after(pe, "tc_copied", gg)
            for j in range(GP):
                ins = pe.transpose(ps[0:ROPE, 2, j * P:(j + 1) * P], page(j, KL, LATW), ident[:, :])
            out(ins, "tc_ready")

        def scores_back(b, g):
            gg = group_of(b, g)
            pe.wait_ge(S["sc_copied"], gg + 1)
            after(pe, "sraw_done", gg)
            out(pe.transpose(ps[:, 6, 0:P], scs[g % 2][:, :], ident[:, :]), "scT_ready")

        def weigh(b, p):
            pe.wait_ge(S["lp_ready"], b + 1)
            pe.wait_ge(S["oT_copied"], b + 1)
            for pg in range(NPG):
                j = pg % 4
                pe.matmul(ps[HP * j:HP * (j + 1), 7, 0:KL], prob[:, pg, :], latn[p][:, pg, 0:KL],
                          start=(pg < 4), stop=(pg >= NPG - 4))
            out(pe.matmul(ps[0:1, 7, KL:KL + H], ones[:, :], lp[:, :], start=True, stop=True), "o_ready")

        def gather_output(b):
            pe.wait_ge(S["ol_copied"], b + 1)
            for c in range(2):
                ins = pe.matmul(ps[:, 7, c * H:(c + 1) * H], ol[:, c * P:(c + 1) * P], sel[:, :], start=True, stop=True)
            out(ins, "oT_ready")

        def slot(b, p, g, ahead, behind):
            gg = group_of(b, g)
            if ahead:
                nb, ng = following(b, g)
                turn(nb, p if ng else 1 - p, ng)
            pe.wait_ge(S["ta_copied"], gg + 1)
            pe.wait_ge(S["tb_copied"], gg + 1)
            for j in range(GP):
                n = gg * GP + j
                if not (isinstance(b, int) and b == 0 and g == 0 and j < 2):
                    pe.wait_ge(S["sq_done"], n - 1)
                for c in range(2):
                    ins = pe.matmul(ps[:, 3 + j % 2, :], latT[g % 2][:, c, j, :], wk[:, c, :], start=(c == 0), stop=(c == 1))
                out(ins, "k_ready")
            pe.wait_ge(S["tc_copied"], gg + 1)
            after(pe, "sc_copied", gg)
            if g == 0:
                pe.wait_ge(S["qab_ready"], b + 1)
            for c in range(3):
                for j in range(GP):
                    ins = pe.matmul(ps[HP * j:HP * (j + 1), 5, 0:P], qab[p][:, c, :], latT[g % 2][:, c, j, :],
                                    start=(c == 0), stop=(c == 2))
            out(ins, "sc_ready")
            if g == 0 and behind:
                scores_back(b - 1, NG - 1)
            if g > 0:
                scores_back(b, g - 1)
            if behind and g == 4:
                weigh(b - 1, 1 - p)
            if behind and g == 5:
                gather_output(b - 1)

        pe.wait_ge(S["qabs_copied"], 1)
        turn(0, 0, 0)
        for g in range(NG):
            slot(0, 0, g, True, False)
        with pe.Fori(0, 3) as i:
            for p, b in ((1, i * 2 + 1), (0, i * 2 + 2)):
                for g in range(NG):
                    slot(b, p, g, True, True)
        for g in range(NG):
            slot(NS - 1, 1, g, g + 1 < NG, True)
        scores_back(NS - 1, NG - 1)
        weigh(NS - 1, 1)
        gather_output(NS - 1)
        pe.wait_ge(new_loaded, 16 * (N_NEW + 2))
        pe.wait_ge(S["oT_copied"], NS + 1)
        for h in range(H):
            for c in range(2):
                ins = pe.matmul(ps[0:NS, 0, h * VD:(h + 1) * VD], oLT[:, c, h, :], wv[:, c, h * VD:(h + 1) * VD],
                                start=(c == 0), stop=(c == 1))
        out(ins, "up_ready")

    ctx.close()


def mixing_block(nc, a, s, att, nT):
    ctx = ExitStack()
    sb = lambda name, shape, dt=F32: ctx.enter_context(nc.sbuf_tensor("m_" + name, shape, dt))
    sem = lambda name: ctx.enter_context(nc.semaphore("m_" + name))
    ps = ctx.enter_context(nc.psum_tensor("m_ps", [P, 8, 512], F32))
    MIX = SW + H * VD
    KM = MIX // P
    w_out = sb("w_out", [P, KM, D])
    mix_g = sb("mix_g", [P, KM])
    ffn_g = sb("ffn_g", [P, KD])
    ident = sb("ident", [P, P])
    mhalf = sb("mhalf", [P, NT + 1])
    eps = sb("eps", [P, NT + 1])
    att_ms = sb("att_ms", [P, NT + 1])
    att_rs = sb("att_rs", [P, NT + 1])
    junk = sb("junk", [P, D])
    ys = [sb(f"ys{i}", [P, SW]) for i in range(2)]
    h = [sb(f"h{i}", [P, D]) for i in range(2)]
    at = [sb(f"at{i}", [P, H * VD]) for i in range(2)]
    mixT = [sb(f"mixT{i}", [P, KM, P]) for i in range(2)]
    n = [sb(f"n{i}", [P, D]) for i in range(2)]
    st = [sb(f"st{i}", [P, 2]) for i in range(2)]

    w_loaded = [sem(f"w_loaded{k}") for k in range(KM)]
    gains_loaded, h_stored, att_steps = sem("gains_loaded"), sem("h_stored"), sem("att_steps")
    rows_loaded = [sem(f"rows_loaded{i}") for i in range(2)]
    names = """consts att_squared att_rstd att_normed at_ready ysT_ready atT_ready ysT_copied atT_copied o_ready h_done
    h_squared h_rstd n_ready nTa_ready nTb_ready nTa_copied nTb_copied""".split()
    S = {x: sem(x) for x in names}
    pool_steps = Steps(sem("pool_steps"), "mixing pool")
    block = ctx.enter_context(nc.Block())

    def out(ins, name):
        ins.then_inc(S[name], 1)

    def after(eng, name, count):
        if not (isinstance(count, int) and count <= 0):
            eng.wait_ge(S[name], count)

    def rows(t):
        return NS if isinstance(t, int) and t == 0 else P

    def loaded(t, p):
        return (t - p + 2) * 16

    def over_tiles(eng, slot):
        slot(0, 0)
        slot(1, 1)
        with eng.Fori(1, NT // 2) as i:
            slot(i * 2, 0)
            slot(i * 2 + 1, 1)
        slot(NT, 0)

    @block.sync
    def _(sp):
        def load(t, p):
            if isinstance(t, int) and t == 0:
                sp.dma_start(ys[0][0:NS, :], s["ys"][T:TOK, :]).then_inc(rows_loaded[0], 16)
                sp.dma_start(h[0][0:NS, :], a["x_sample"].rearrange("b s d -> (b s) d")).then_inc(rows_loaded[0], 16)
                return
            row = sp.snap((t - 1) * P)
            slot_row = sp.snap((t - 1) * P + META)
            sp.dma_start(ys[p][:, :], s["ys"][ds(slot_row, P), :]).then_inc(rows_loaded[p], 16)
            sp.dma_start(h[p][:, :], a["x_prompt"][0, ds(row, P), :]).then_inc(rows_loaded[p], 16)

        def store(t, p):
            if isinstance(t, int) and t == 0:
                sp.wait_ge(S["h_done"], 1)
                sp.dma_start(s["h"][SEQ:SEQ + NS, :], h[0][0:NS, :]).then_inc(h_stored, 16)
                return
            row = sp.snap((t - 1) * P)
            sp.wait_ge(S["h_done"], t + 1)
            sp.wait_ge(S["consts"], 1)
            sp.dma_start(s["h"][ds(row, P), :], h[p][:, :]).then_inc(h_stored, 16)

        def reload(t, p):
            sp.wait_ge(h_stored, t * 16 + 16)
            sp.wait_ge(S["n_ready"], t + 1)
            sp.wait_ge(S["consts"], 1)
            load(t + 2, p)

        load(0, 0)
        load(1, 1)
        for k in range(KM):
            sp.dma_start(w_out[:, k, :], a["w_out"][0, k * P:(k + 1) * P, :]).then_inc(w_loaded[k], 16)
        store(0, 0)
        reload(0, 0)
        with sp.Fori(0, NT // 2 - 1) as i:
            store(i * 2 + 1, 1)
            reload(i * 2 + 1, 1)
            store(i * 2 + 2, 0)
            reload(i * 2 + 2, 0)
        store(NT - 1, 1)
        store(NT, 0)
        sp.wait_ge(h_stored, (NT + 1) * 16)

    @block.gpsimd
    def _(pool):
        pool_steps(pool, pool.memset(ident[:, :], 0.0))
        pool_steps(pool, pool.affine_select(out=ident[:, :], in_=ident[:, :], compare_op=ALU.not_equal, fill=1.0,
                                            base=0, pattern=[[-1, P]], channel_multiplier=1))
        pool.memset(mhalf[:, :], -0.5).then_inc(S["nTb_ready"], 1)
        pool.memset(att_ms[:, :], 0.0)
        out(pool.memset(eps[:, :], EPS), "consts")
        pool.wait_ge(S["att_squared"], 1)
        pool_steps(pool, pool.tensor_tensor(out=att_ms[:, :], in0=att_ms[:, :], in1=eps[:, :], op=ALU.add))
        out(pool.tensor_tensor(out=att_rs[:, :], in0=att_ms[:, :], in1=mhalf[:, :], op=ALU.pow), "att_rstd")

        def slot(t, p):
            R = rows(t)
            pool.wait_ge(S["h_squared"], t + 1)
            pool_steps(pool, pool.tensor_tensor(out=st[p][0:R, 0:1], in0=st[p][0:R, 0:1], in1=eps[0:R, 0:1], op=ALU.add))
            out(pool.tensor_tensor(out=st[p][0:R, 1:2], in0=st[p][0:R, 0:1], in1=mhalf[0:R, 0:1], op=ALU.pow), "h_rstd")

        slot(0, 0)
        slot(1, 1)
        with pool.Fori(1, NT // 2) as i:
            pool_steps.begin(i, 2, first=1)
            slot(i * 2, 0)
            slot(i * 2 + 1, 1)
            pool_steps.end(NT // 2 - 1)
        slot(NT, 0)

    @block.scalar
    def _(act):
        for k in range(KM):
            src = a["ssd_norm_g"] if k < KM // 2 else a["mla_out_g"]
            c = k % (KM // 2) * P
            act.dma_start(mix_g[:, k:k + 1], src[0, c:c + P].unsqueeze(1)).then_inc(gains_loaded, 16)
        act.dma_start(ffn_g[:, :], a["ffn_norm_g"][0].rearrange("(k p) -> p k", p=P)).then_inc(gains_loaded, 16)
        act.wait_ge(S["consts"], 1)
        for t in range(NT + 1):
            R = rows(t)
            ins = act.activation(junk[0:R, 0:H * VD], att[0:R, t, :], ACT.Square, scale=(H * VD) ** -0.5,
                                 accum_out=att_ms[0:R, t:t + 1])
            if t < NT:
                ins.then_inc(att_steps, 1)
                act.wait_ge(att_steps, t + 1)
        out(ins, "att_squared")

        def slot(t, p):
            R = rows(t)
            act.wait_ge(S["h_done"], t + 1)
            after(act, "h_squared", t)
            after(act, "n_ready", t - 1)
            out(act.activation(junk[0:R, :], h[p][0:R, :], ACT.Square, scale=D ** -0.5, accum_out=st[p][0:R, 0:1]), "h_squared")

        act.wait_ge(S["att_squared"], 1)
        over_tiles(act, slot)

    @block.vector
    def _(dve):
        dve.wait_ge(S["att_rstd"], 1)
        for t in range(NT + 1):
            R = rows(t)
            ins = dve.tensor_scalar(att[0:R, t, :], att[0:R, t, :], att_rs[0:R, t:t + 1], None, ALU.mult)
        out(ins, "att_normed")
        dve.wait_ge(S["att_normed"], 1)

        def still(t, p):
            R = rows(t)
            after(dve, "atT_ready", t - 1)
            out(dve.tensor_scalar(at[p][0:R, :], att[0:R, ds(t, 1), :].rearrange("p o c -> p (o c)"), 1.0, None, ALU.mult),
                "at_ready")

        def keep_mix(t, p):
            R = rows(t)
            after(dve, "o_ready", t - 1)
            for j, name in enumerate(("ysT", "atT")):
                dve.wait_ge(S[name + "_ready"], t + 1)
                out(dve.tensor_tensor(out=mixT[p][:, 4 * j:4 * j + 4, 0:R],
                                      in0=ps[:, j, :].rearrange("p (k r) -> p k r", k=4)[:, :, 0:R],
                                      in1=bc(mix_g[:, 4 * j:4 * j + 4], R, 2), op=ALU.mult), name + "_copied")

        def residual(t, p):
            R = rows(t)
            dve.wait_ge(rows_loaded[p], loaded(t, p))
            dve.wait_ge(S["o_ready"], t + 1)
            hb = h[p][0:R, :].rearrange("p (c n) -> p c n", c=2)
            out(dve.tensor_tensor(out=hb, in0=ps[0:R, 2 + 2 * p:4 + 2 * p, :], in1=hb, op=ALU.add), "h_done")

        def normed(t, p):
            R = rows(t)
            dve.wait_ge(S["h_rstd"], t + 1)
            after(dve, "nTb_ready", t)
            out(dve.tensor_scalar(n[p][0:R, :], h[p][0:R, :], st[p][0:R, 1:2], None, ALU.mult), "n_ready")

        def keep_norms(t, p):
            R, col = (NS, SEQ) if isinstance(t, int) and t == 0 else (P, (t - 1) * P)
            for j, name in enumerate(("nTa", "nTb")):
                dve.wait_ge(S[name + "_ready"], t + 1 + j)
                out(dve.tensor_tensor(out=nT[:, 4 * j:4 * j + 4, ds(col, R)],
                                      in0=ps[:, 6 + j, :].rearrange("p (k r) -> p k r", k=4)[:, :, 0:R],
                                      in1=bc(ffn_g[:, 4 * j:4 * j + 4], R, 2), op=ALU.mult), name + "_copied")

        still(0, 0)
        still(1, 1)
        dve.wait_ge(gains_loaded, 16 * (KM + 1))
        keep_mix(0, 0)

        def slot(t, p):
            first, last = isinstance(t, int) and t == 0, isinstance(t, int) and t == NT
            if not first:
                normed(t - 1, 1 - p)
            if not last:
                keep_mix(t + 1, 1 - p)
            if not first:
                keep_norms(t - 1, 1 - p)
            if not (isinstance(t, int) and t >= NT - 1):
                still(t + 2, p)
            residual(t, p)

        slot(0, 0)
        slot(1, 1)
        with dve.Fori(1, NT // 2 - 1) as i:
            slot(i * 2, 0)
            slot(i * 2 + 1, 1)
        slot(NT - 2, 0)
        slot(NT - 1, 1)
        slot(NT, 0)
        normed(NT, 0)
        keep_norms(NT, 0)

    @block.tensor
    def _(pe):
        def turn_mix(t, p):
            R = rows(t)
            pe.wait_ge(rows_loaded[p], loaded(t, p))
            after(pe, "ysT_copied", t)
            for k in range(4):
                ins = pe.transpose(ps[:, 0, k * P:k * P + R], ys[p][0:R, k * P:(k + 1) * P], ident[0:R, 0:R])
            out(ins, "ysT_ready")
            pe.wait_ge(S["at_ready"], t + 1)
            after(pe, "atT_copied", t)
            for k in range(4):
                ins = pe.transpose(ps[:, 1, k * P:k * P + R], at[p][0:R, k * P:(k + 1) * P], ident[0:R, 0:R])
            out(ins, "atT_ready")

        def project(t, p):
            R = rows(t)
            pe.wait_ge(S["ysT_copied"], t + 1)
            pe.wait_ge(S["atT_copied"], t + 1)
            after(pe, "h_done", t - 1)
            for k in range(KM):
                if k == KM // 2:
                    if not (isinstance(t, int) and t == NT):
                        turn_mix(t + 1, 1 - p)
                    if not (isinstance(t, int) and t == 0):
                        turn_norms(t - 1, 1 - p)
                if isinstance(t, int) and t == 0:
                    pe.wait_ge(w_loaded[k], 16)
                for c in range(2):
                    ins = pe.matmul(ps[0:R, 2 + 2 * p + c, :], mixT[p][:, k, 0:R], w_out[:, k, c * 512:(c + 1) * 512],
                                    start=(k == 0), stop=(k == KM - 1))
            out(ins, "o_ready")

        def turn_norms(t, p):
            R = rows(t)
            pe.wait_ge(S["n_ready"], t + 1)
            for j, name in enumerate(("nTa", "nTb")):
                after(pe, name + "_copied", t)
                for k in range(4):
                    ins = pe.transpose(ps[:, 6 + j, k * P:k * P + R], n[p][0:R, (4 * j + k) * P:(4 * j + k + 1) * P],
                                       ident[0:R, 0:R])
                out(ins, name + "_ready")

        pe.wait_ge(S["consts"], 1)
        turn_mix(0, 0)
        over_tiles(pe, project)
        turn_norms(NT, 0)

    ctx.close()


def ffn_block(nc, a, s, nT):
    ctx = ExitStack()
    sb = lambda name, shape, dt=F32: ctx.enter_context(nc.sbuf_tensor("f_" + name, shape, dt))
    sem = lambda name: ctx.enter_context(nc.semaphore("f_" + name))
    KF = FF // P
    COLS = SEQ + NS
    NC = 3
    W = COLS // NC
    ps = ctx.enter_context(nc.psum_tensor("f_ps", [P, 8, 512], F32))
    hidT = sb("hidT", [P, KF, COLS])
    wg = [sb(f"wg{i}", [P, KD, P]) for i in range(2)]
    wu = [sb(f"wu{i}", [P, KD, P]) for i in range(2)]
    wd = [sb(f"wd{i}", [P, KF, P]) for i in range(2)]
    e = [sb(f"e{i}", [P, W]) for i in range(NC)]
    yT = sb("yT", [P, COLS])
    y = [sb(f"y{i}", [P, NT + 1, P]) for i in range(2)]
    ident = sb("ident", [P, P])

    up_loaded = [sem(f"up_loaded{i}") for i in range(2)]
    down_loaded = [sem(f"down_loaded{i}") for i in range(2)]
    h_loaded = [sem(f"h_loaded{i}") for i in range(2)]
    y_stored = [sem(f"y_stored{i}") for i in range(2)]
    names = "consts gate_ready up_ready exp_done hid_done down_ready yT_copied back0_ready back1_ready back2_ready y_done ident_step".split()
    S = {x: sem(x) for x in names}
    dve_steps = Steps(sem("dve_steps"), "ffn dve")
    block = ctx.enter_context(nc.Block())

    def out(ins, name):
        ins.then_inc(S[name], 1)

    def after(eng, name, count):
        if not (isinstance(count, int) and count <= 0):
            eng.wait_ge(S[name], count)

    @block.sync
    def _(sp):
        def load_up(f, p):
            col = f * P if isinstance(f, int) else sp.snap(f * P)
            if not (isinstance(f, int) and f < 2):
                sp.wait_ge(S["up_ready"], (f - 1) * NC)
                sp.wait_ge(S["consts"], 1)
            for dst, src in ((wg, "w_gate"), (wu, "w_up")):
                sp.dma_start(dst[p][:, :, :], a[src][0, :, ds(col, P)].rearrange("(k p) c -> p k c", p=P)).then_inc(up_loaded[p], 16)

        def load_down(d, p):
            col = d * P if isinstance(d, int) else sp.snap(d * P)
            if not (isinstance(d, int) and d < 2):
                sp.wait_ge(S["down_ready"], (d - 1) * NC)
                sp.wait_ge(S["consts"], 1)
            sp.dma_start(wd[p][:, :, :], a["w_down"][0, :, ds(col, P)].rearrange("(k p) c -> p k c", p=P)).then_inc(down_loaded[p], 16)
            if not (isinstance(d, int) and d < 2):
                sp.wait_ge(y_stored[p], (d - p) * 16)
                sp.wait_ge(S["consts"], 1)
            sp.dma_start(y[p][:, 0:NT, :], s["h"][0:SEQ, ds(col, P)].rearrange("(t p) c -> p t c", p=P)).then_inc(h_loaded[p], 16)
            sp.dma_start(y[p][0:NS, NT, :], s["h"][SEQ:SEQ + NS, ds(col, P)]).then_inc(h_loaded[p], 16)

        load_up(0, 0)
        load_up(1, 1)
        load_down(0, 0)
        load_down(1, 1)
        with sp.Fori(1, KF // 2) as i:
            load_up(i * 2, 0)
            load_up(i * 2 + 1, 1)
        with sp.Fori(1, KD // 2) as i:
            load_down(i * 2, 0)
            load_down(i * 2 + 1, 1)

    @block.gpsimd
    def _(pool):
        ident_step = S["ident_step"]
        pool.memset(ident[:, :], 0.0).then_inc(ident_step, 1)
        pool.wait_ge(ident_step, 1)
        pool.affine_select(out=ident[:, :], in_=ident[:, :], compare_op=ALU.not_equal, fill=1.0,
                           base=0, pattern=[[-1, P]], channel_multiplier=1).then_inc(S["consts"], 1)

    @block.scalar
    def _(act):
        with act.Fori(0, KF) as f:
            for c in range(NC):
                act.wait_ge(S["gate_ready"], f * NC + c + 1)
                out(act.activation(e[c][:, :], ps[:, 2 * c, 0:W], ACT.Exp, scale=-1.0), "exp_done")

        def keep(d, p):
            for c in range(NC):
                act.wait_ge(S["down_ready"], d * NC + c + 1)
                after(act, "back2_ready", d)
                out(act.activation(yT[:, c * W:(c + 1) * W], ps[:, 3 * p + c, 0:W], ACT.Copy), "yT_copied")

        def store(d, p):
            col = d * P if isinstance(d, int) else act.snap(d * P)
            act.wait_ge(S["y_done"], d * 3 + 3)
            act.wait_ge(S["consts"], 1)
            act.dma_start(a["y_prompt"][0, :, ds(col, P)].rearrange("(t p) c -> p t c", p=P), y[p][:, 0:NT, :]).then_inc(y_stored[p], 16)
            act.dma_start(a["y_sample"][:, 0, ds(col, P)], y[p][0:NS, NT, :]).then_inc(y_stored[p], 16)

        keep(0, 0)
        with act.Fori(0, KD // 2 - 1) as i:
            for p, d in ((1, i * 2 + 1), (0, i * 2 + 2)):
                keep(d, p)
                store(d - 1, 1 - p)
        keep(KD - 1, 1)
        store(KD - 2, 0)
        store(KD - 1, 1)
        for p in range(2):
            act.wait_ge(y_stored[p], KD // 2 * 32)

    @block.vector
    def _(dve):
        with dve.Fori(0, KF) as f:
            dve_steps.begin(f, 3 * NC)
            for c in range(NC):
                dve.wait_ge(S["exp_done"], f * NC + c + 1)
                dve_steps(dve, dve.tensor_scalar(e[c][:, :], e[c][:, :], 1.0, None, ALU.add))
                dve_steps(dve, dve.reciprocal(e[c][:, :], e[c][:, :]))
                dve_steps(dve, dve.tensor_tensor(out=e[c][:, :], in0=ps[:, 2 * c, 0:W], in1=e[c][:, :], op=ALU.mult))
                dve.wait_ge(S["up_ready"], f * NC + c + 1)
                out(dve.tensor_tensor(out=hidT[:, ds(f, 1), c * W:(c + 1) * W].rearrange("p o c -> p (o c)"),
                                      in0=ps[:, 2 * c + 1, 0:W], in1=e[c][:, :], op=ALU.mult), "hid_done")
            dve_steps.end(KF)

        def add_back(d, p):
            dve.wait_ge(h_loaded[p], (d - p + 2) * 16)
            for j, (t, w, R) in enumerate(((0, 4, P), (4, 4, P), (NT, 1, NS))):
                dve.wait_ge(S[f"back{j}_ready"], d + 1)
                dst = y[p][0:R, t:t + w, :]
                out(dve.tensor_tensor(out=dst, in0=ps[0:R, 6 + j % 2, 0:w * P].rearrange("p (t c) -> p t c", c=P),
                                      in1=dst, op=ALU.add), "y_done")

        add_back(0, 0)
        with dve.Fori(0, KD // 2 - 1) as i:
            add_back(i * 2 + 1, 1)
            add_back(i * 2 + 2, 0)
        add_back(KD - 1, 1)

    @block.tensor
    def _(pe):
        def hidden(f, p):
            first = isinstance(f, int) and f == 0
            pe.wait_ge(up_loaded[p], (f - p + 2) * 16)
            for c in range(NC):
                if not first:
                    pe.wait_ge(S["hid_done"], (f - 1) * NC + c + 1)
                for w, bank, name in ((wg, 2 * c, "gate_ready"), (wu, 2 * c + 1, "up_ready")):
                    for k in range(KD):
                        ins = pe.matmul(ps[:, bank, 0:W], w[p][:, k, :], nT[:, k, c * W:(c + 1) * W],
                                        start=(k == 0), stop=(k == KD - 1))
                    out(ins, name)

        hidden(0, 0)
        hidden(1, 1)
        with pe.Fori(1, KF // 2) as i:
            hidden(i * 2, 0)
            hidden(i * 2 + 1, 1)

        def down(d, p):
            pe.wait_ge(down_loaded[p], (d - p + 2) * 8)
            for c in range(NC):
                if not (isinstance(d, int) and d < 2):
                    pe.wait_ge(S["yT_copied"], (d - 2) * NC + c + 1)
                for k in range(KF):
                    ins = pe.matmul(ps[:, 3 * p + c, 0:W], wd[p][:, k, :], hidT[:, k, c * W:(c + 1) * W],
                                    start=(k == 0), stop=(k == KF - 1))
                out(ins, "down_ready")

        def turn_back(d, p):
            pe.wait_ge(S["yT_copied"], d * NC + NC)
            for j, (t0, tiles, R) in enumerate(((0, 4, P), (4, 4, P), (NT, 1, NS))):
                if j == 2:
                    pe.wait_ge(S["y_done"], d * 3 + 1)
                else:
                    after(pe, "y_done", d * 3 if j == 0 else d * 3 - 1)
                for t in range(tiles):
                    col = (t0 + t) * P
                    ins = pe.transpose(ps[0:R, 6 + j % 2, t * P:(t + 1) * P], yT[:, col:col + R], ident[:, :])
                out(ins, f"back{j}_ready")

        pe.wait_ge(S["consts"], 1)
        pe.wait_ge(S["hid_done"], KF * NC)
        down(0, 0)
        down(1, 1)
        turn_back(0, 0)
        with pe.Fori(1, KD // 2) as i:
            down(i * 2, 0)
            turn_back(i * 2 - 1, 1)
            down(i * 2 + 1, 1)
            turn_back(i * 2, 0)
        turn_back(KD - 1, 1)

    ctx.close()


def program(nc, a):
    d = lambda name, shape: nc.dram_tensor(name, shape, F32, kind="Internal").ap()
    s = {
        "ys": d("s_ys", (TOK, SW)), "v": d("s_v", (TOK, SW)), "qT": d("s_qT", (H, QK, TOK)), "kT": d("s_kT", (H, QK, TOK)),
        "s_z": d("s_z", (NS, SW)), "s_x": d("s_x", (NS, SW)), "s_bc": d("s_bc", (NS, 2 * P)),
        "h": d("s_h", (SEQ + NS, D)), "s_dt": d("s_dt", (NS, SH)), "s_dta": d("s_dta", (NS, SH)), "s_y": d("s_y", (NS, SW)), "s_q": d("s_q", (NS, H, QK)), "s_k": d("s_k", (NS, H, QK)),
    }
    with nc.allow_non_contiguous_dma(reason="small vectors into columns"):
        tiles_block(nc, a, s)
        with nc.sbuf_tensor("att", [P, NT + 1, H * VD], F32) as att:
            attention_block(nc, s, att)
            samples_block(nc, a, s, att)
            with nc.sbuf_tensor("nT", [P, KD, SEQ + NS], F32) as nT:
                mixing_block(nc, a, s, att, nT)
                ffn_block(nc, a, s, nT)
    return s


_OUTS = [
    ("y_prompt", (1, SEQ, D)), ("y_sample", (NS, 1, D)), ("kv_latent_prompt", (1, 1, T, KL)),
    ("k_rope_prompt", (1, 1, T, ROPE)), ("conv_prompt", (1, 1, 3, CONV)), ("ssm_prompt", (1, 1, SH, SP_, SN)),
    ("kv_latent_sample", (1, NS, 1, KL)), ("k_rope_sample", (1, NS, 1, ROPE)), ("conv_sample", (1, NS, 3, CONV)),
    ("ssm_sample", (1, NS, SH, SP_, SN)),
]


def rope_table(np):
    pos = np.zeros((P, NT + 1), np.float32)
    pos[0:META, 0] = np.arange(META)
    pos[META:ODD, 0] = NPG * PAGE
    pos[:, 1:] = META + np.arange(SEQ).reshape(NT, P).T
    inv = np.float32(10000.0) ** (-np.arange(HALF, dtype=np.float32) * np.float32(2.0 / ROPE))
    ang = (pos[:, :, None] * inv.astype(np.float32)).astype(np.float64)
    return np.concatenate([np.cos(ang), np.sin(ang)], axis=-1).astype(np.float32)


def kernel(**inputs):
    import numpy as np
    import concourse.bacc as bacc
    from concourse.bass_utils import run_bass_kernel_spmd

    nc = bacc.Bacc("TRN2", target_bir_lowering=False, num_devices=1)
    arrays = {"in_" + n: np.ascontiguousarray(v) for n, v in inputs.items()}
    arrays["in_rope_table"] = rope_table(np)
    a = {}
    for n, v in arrays.items():
        a[n[3:]] = nc.dram_tensor(n, v.shape, mybir.dt.from_np(v.dtype), kind="ExternalInput").ap()
    for n, shape in _OUTS:
        a[n] = nc.dram_tensor("out_" + n, shape, F32, kind="ExternalOutput").ap()
    program(nc, a)
    r = run_bass_kernel_spmd(nc, [arrays], core_ids=[0])
    return tuple(r.results[0]["out_" + n] for n, _ in _OUTS)
```

```python
from contextlib import ExitStack

import concourse.bass as bass
from concourse import mybir

F32 = mybir.dt.float32
F32R = mybir.dt.float32r
I32 = mybir.dt.int32
ALU = mybir.AluOpType
ACT = mybir.ActivationFunctionType
AXX = mybir.AxisListType.X
RMAX = bass.bass_isa.ReduceOp.max
ds = bass.ds

P = 128
D = 1024
KD = D // P
META = 16
SEQ = 1024
T = META + SEQ
NS = 8
TOK = T + NS
NT = SEQ // P
ODD = META + NS
SH, SP_, SN, SG = 8, 64, 64, 2
SW = SH * SP_
CONV = SW + 2 * SG * SN
CT = CONV // P
H, NOPE, ROPE, VD = 8, 64, 32, 64
HALF = ROPE // 2
QK = NOPE + ROPE
QL, KL = 384, 256
FF = 2816
IN = SW + CONV + SH + QL + KL + ROPE
C_XBC, C_DT, C_KV = SW, SW + CONV, SW + CONV + SH + QL
N_DQ, N_KV = SH + QL, KL + ROPE
PAGE, NPG = 128, 32
LATW = KL + ROPE
EPS = 1e-6
SCALE = QK ** -0.5
NEG = -1e30
N_SMALLS = 20
N_ODD_STORES = 7
POOL_TWO, ACT_TWO, DVE_TWO = 16, 2, 24


class Steps:

    def __init__(self, sem, name):
        self.sem, self.name, self.base, self.n, self.loop = sem, name, 0, 0, None

    def begin(self, i, per, first=0):
        self.loop, self.start = (i, per), self.n - first * per
        self.n, self.first = self.start, first

    def end(self, times):
        assert self.n - self.start == self.loop[1], (self.name, self.n - self.start)
        self.n = self.start + self.loop[1] * (self.first + times)
        self.loop = None

    def value(self):
        if self.loop is None:
            return self.n
        i, per = self.loop
        return i * per + self.n

    def __call__(self, eng, ins):
        ins.then_inc(self.sem, 1)
        self.n += 1
        eng.wait_ge(self.sem, self.value())


def bc(ap, n, axis):
    shape = list(ap.shape)
    shape.insert(axis, n)
    return ap.unsqueeze(axis).to_broadcast(shape)


def by_head(ap, width):
    return ap.rearrange("p (h d) -> p h d", d=width)



def tiles_block(nc, a, s):
    ctx = ExitStack()
    sb = lambda name, shape: ctx.enter_context(nc.sbuf_tensor("t_" + name, shape, F32))
    sems = []

    def sem(name):
        sems.append(nc.alloc_semaphore("t_" + name))
        return sems[-1]


    ps = ctx.enter_context(nc.psum_tensor("t_ps", [P, 8, 512], F32))
    w_in = sb("w_in", [P, KD, IN])
    w_uq = sb("w_uq", [P, QL // P, H * QK])
    w_ukv = sb("w_ukv", [P, KL // P, H * (NOPE + VD)])
    attn_g = sb("attn_g", [P, KD])
    qn_g = sb("qn_g", [P, QL // P])
    kvn_g = sb("kvn_g", [P, KL])
    conv_w = sb("conv_w", [P, CT, 4])
    conv_b = sb("conv_b", [P, CT])
    dt_b = sb("dt_b", [P, SH])
    neg_a = sb("neg_a", [P, SH])
    d_skip = sb("d_skip", [P, SH])
    gqk = sb("gqk", [QK, 1])
    gk = sb("gk", [QK, 1])
    cs = sb("cs", [P, NT + 1, 2 * HALF])
    ident = sb("ident", [P, P])
    upper = sb("upper", [P, P])
    ones = sb("ones", [P, P])
    mhalf = sb("mhalf", [P, 2 * H])
    eps = sb("eps", [P, 2 * H])
    cs_now = sb("cs_now", [P, 2 * HALF])
    state = sb("state", [P, 4 * SP_])
    stout = sb("stout", [P, 2, P])

    x = [sb(f"x{i}", [P, D]) for i in range(2)]
    xT = sb("xT", [P, KD, P])
    raw = [sb(f"raw{i}", [P, CT, 3 + P]) for i in range(2)]
    z = [sb(f"z{i}", [P, SW]) for i in range(2)]
    dq = [sb(f"dq{i}", [P, N_DQ]) for i in range(2)]
    kv = [sb(f"kv{i}", [P, N_KV]) for i in range(2)]
    junk = sb("junk", [P, D])
    junk_cl = sb("junk_cl", [P, QL + KL])
    junk_kr = sb("junk_kr", [P, ROPE])
    junk_y = sb("junk_y", [P, SW])
    stx = sb("stx", [P, 8])
    stc = sb("stc", [P, 4])
    sty = sb("sty", [P, 4])
    stq = sb("stq", [P, 5 * H])
    conv = sb("conv", [P, CT, P])
    ex = sb("ex", [P, CT, P])
    zex = sb("zex", [P, SW])
    xs = sb("xs", [P, SW])
    bn = sb("bn", [P, 2 * P])
    cz = sb("cz", [P, SG, P])
    gmask = sb("gmask", [P, SG, P])
    dts = sb("dts", [P, 14, SH])
    ud = sb("ud", [P, SH, P])
    seg = sb("seg", [P, SH, P])
    cbm = sb("cbm", [P, SG, P])
    xdt = sb("xdt", [P, SW])
    xw = sb("xw", [P, SW])
    dx = sb("dx", [P, SW])
    y = sb("y", [P, SW])
    ys = sb("ys", [P, SW])
    cq = sb("cq", [P, QL])
    lat = sb("lat", [P, KL])
    kr = sb("kr", [P, ROPE])
    krt = sb("krt", [P, 4, HALF])
    clT = sb("clT", [P, 5, P])
    q = sb("q", [P, H, QK])
    qsq = sb("qsq", [P, H, QK])
    k = sb("k", [P, H, QK])
    ksq = sb("ksq", [P, H, NOPE])
    v = sb("v", [P, SW])
    rp = sb("rp", [P, 4, H, HALF])
    qT = sb("qT", [QK, H, P])
    kT = sb("kT", [QK, H, P])
    sconv = sb("sconv", [3 * NS, CONV])
    sT = sb("sT", [P, CT, 3 * NS])
    rawn = sb("rawn", [ODD, CONV])
    rawl = sb("rawl", [3, CONV])

    V, AV, U, W, LN, W1, DT, DTA, ACS, EACS, DIN, DEC, DLAST = range(13)

    weights = [sem(f"weights{i}") for i in range(KD)]
    smalls = sem("smalls")
    gain_loaded = sem("gain_loaded")
    up_weights = sem("up_weights")
    names = """consts a_exp folded up_folded x_squared x_rstd x_normed xT_ready0 xT_ready1 xT_copied0 xT_copied1
    xbc_ready0 xbc_ready1 xbc_copied0 xbc_copied1 z_ready z_copied dq_ready dq_copied kv_ready kv_copied
    halo_done conv_done conv_exp conv_silu z_exp z_silu dt_in dt_exp dt_w dt_ln dt_done ud_ready
    cl_squared cl_rstd cl_normed clT_ready0 clT_ready1 clT_copied0 clT_copied1
    xs_ready bT_ready xs_copied bn_copied acs_ready acs_copied bc_ready bc_taken cb_ready cb_taken
    seg_done seg_exp last_exp decay_in decay_exp cz_ready att_ready xdt_ready xw_ready dx_ready
    yd_ready yo_ready st_ready yd_taken yo_taken st_taken state_done
    q_ready kvu_ready q_copied kn_squared v_copied kn_taken kr_done kr_squared q_roped q_squared qk_sums qk_rstd
    q_normed k_normed qT_ready0 qT_ready1 kT_ready0 kT_ready1 qT_copied0 qT_copied1 kT_copied0 kT_copied1
    y_done y_squared y_rstd y_normed
    sconv_ready sconv_copied rawn_ready rawn_copied rawl_ready rawl_copied stout_ready stout_copied""".split()
    S = {n: sem(n) for n in names}
    x_loaded = [sem(f"x_loaded{i}") for i in range(2)]
    sample_loaded = sem("sample_loaded")
    stored = {n: sem("stored_" + n) for n in "ys lat kr qT kT v odd".split()}
    last_stored = sem("last_stored")
    act_steps = Steps(sem("act_steps"), "act")
    dve_steps = Steps(sem("dve_steps"), "dve")
    pool_steps = Steps(sem("pool_steps"), "pool")

    def out(ins, name):
        ins.then_inc(S[name], 1)


    def rows(t):
        return ODD if isinstance(t, int) and t == 0 else P

    def after(eng, name, n):
        if not (isinstance(n, int) and n <= 0):
            eng.wait_ge(S[name], n)

    def free(eng, name, t):
        if not (isinstance(t, int) and t <= 0):
            eng.wait_ge(stored[name], t * 16 + 16)

    block = ctx.enter_context(nc.Block())

    @block.sync
    def _(sp):
        def data(name, n):
            sp.wait_ge(S[name], n)
            sp.wait_ge(S["consts"], 1)

        def load_x(t, c, p):
            if isinstance(t, int) and t == 0:
                sp.dma_start(x[0][0:META, :], a["meta_tokens"]).then_inc(x_loaded[0], 16)
                sp.dma_start(x[0][META:ODD, :], a["x_sample"].rearrange("b s d -> (b s) d")).then_inc(sample_loaded, 16)
                return
            row = sp.snap((t - 1) * P)
            if not (isinstance(t, int) and t == 1):
                data("xT_ready1", t - 1)
            sp.dma_start(x[p][:, :], a["x_prompt"][0, ds(row, P), :]).then_inc(x_loaded[p], 16)

        def store(t):
            if isinstance(t, int) and t == 0:
                pieces = [(0, META, 0, True), (META, ODD, T, False)]
            else:
                at = sp.snap(META + (t - 1) * P)
                pieces = [(0, P, at, True)]
            data("cl_normed", t + 1)
            for lo, hi, at, prompt in pieces:
                dst = a["kv_latent_prompt"][0, 0, ds(at, hi - lo), :] if prompt else a["kv_latent_sample"][0, :, 0, :]
                sp.dma_start(dst, lat[lo:hi, :]).then_inc(stored["lat"], 16)
            data("kr_done", t + 1)
            for lo, hi, at, prompt in pieces:
                dst = a["k_rope_prompt"][0, 0, ds(at, hi - lo), :] if prompt else a["k_rope_sample"][0, :, 0, :]
                sp.dma_start(dst, kr[lo:hi, :]).then_inc(stored["kr"], 16)
            data("v_copied", t + 1)
            for lo, hi, at, _ in pieces:
                sp.dma_start(s["v"][ds(at, hi - lo), :], v[lo:hi, :]).then_inc(stored["v"], 16)
            data("qT_copied1", t + 1)
            data("y_normed", t + 1)
            for lo, hi, at, _ in pieces[:1]:
                sp.dma_start(s["ys"][ds(at, hi - lo), :], ys[lo:hi, :]).then_inc(stored["ys"], 16)
            for lo, hi, at, _ in pieces:
                sp.dma_start(s["qT"][:, :, ds(at, hi - lo)].rearrange("h d t -> d h t"),
                             qT[:, :, lo:hi]).then_inc(stored["qT"], 16)
            data("kT_copied1", t + 1)
            for lo, hi, at, _ in pieces:
                sp.dma_start(s["kT"][:, :, ds(at, hi - lo)].rearrange("h d t -> d h t"),
                             kT[:, :, lo:hi]).then_inc(stored["kT"], 16)

        load_x(0, 0, 0)
        load_x(1, 0, 1)
        for kd in range(KD):
            sp.dma_start(w_in[:, kd, :], a["w_in"][0, kd * P:(kd + 1) * P, :]).then_inc(weights[kd], 16)
        sp.dma_start(w_uq[:, :, :], a["w_uq"][0].rearrange("(k p) n -> p k n", p=P)).then_inc(up_weights, 16)
        sp.dma_start(w_ukv[:, :, :], a["w_ukv"][0].rearrange("(k p) n -> p k n", p=P)).then_inc(up_weights, 16)
        load_x(2, 1, 0)
        sp.wait_ge(S["z_silu"], 1)
        sp.dma_start(s["s_z"], z[0][META:ODD, :]).then_inc(stored["odd"], 16)
        sp.wait_ge(S["xs_copied"], 1)
        sp.dma_start(s["s_x"], xs[META:ODD, :]).then_inc(stored["odd"], 16)
        sp.wait_ge(S["bn_copied"], 1)
        sp.dma_start(s["s_bc"], bn[META:ODD, :]).then_inc(stored["odd"], 16)
        sp.wait_ge(S["dt_done"], 1)
        sp.dma_start(s["s_dt"], dts[META:ODD, DT, :]).then_inc(stored["odd"], 16)
        sp.dma_start(s["s_dta"], dts[META:ODD, DTA, :]).then_inc(stored["odd"], 16)
        sp.wait_ge(S["rawn_copied"], 1)
        sp.dma_start(a["conv_sample"][0, :, 0:2, :], a["state_conv"][0, :, 1:3, :]).then_inc(last_stored, 16)
        sp.dma_start(a["conv_sample"][0, :, 2, :], rawn[META:ODD, :]).then_inc(last_stored, 16)
        sp.wait_ge(S["q_normed"], 1)
        sp.dma_start(s["s_q"], q[META:ODD, :, :]).then_inc(stored["odd"], 16)
        sp.wait_ge(S["k_normed"], 1)
        sp.wait_ge(S["kn_taken"], 1)
        sp.dma_start(s["s_k"], k[META:ODD, :, :]).then_inc(stored["odd"], 16)
        store(0)
        with sp.Fori(0, 3) as i:
            load_x(i * 2 + 3, i + 1, 1)
            store(i * 2 + 1)
            load_x(i * 2 + 4, i + 2, 0)
            store(i * 2 + 2)
        store(7)
        store(8)
        sp.wait_ge(S["rawl_copied"], 1)
        sp.dma_start(a["conv_prompt"][0, 0, :, :], rawl[:, :]).then_inc(last_stored, 16)
        sp.wait_ge(S["stout_copied"], 1)
        for b2 in range(2):
            for g in range(SG):
                h0 = g * 4 + b2 * 2
                sp.dma_start(a["ssm_prompt"][0, 0, h0:h0 + 2, :, :].rearrange("h p n -> (h p) n"),
                             stout[:, b2, g * SN:(g + 1) * SN]).then_inc(last_stored, 16)
        sp.wait_ge(last_stored, 16 * 7)
        sp.wait_ge(stored["odd"], 16 * N_ODD_STORES)
        sp.wait_ge(stored["ys"], 16 * (NT + 1))
        for n in ("lat", "kr", "qT", "kT", "v"):
            sp.wait_ge(stored[n], 16 * (NT + 2))

    @block.gpsimd
    def _(pool):
        def rstd(dst, src):
            pool_steps(pool, pool.tensor_tensor(out=src, in0=src, in1=eps[0:src.shape[0], 0:src.shape[1]], op=ALU.add))
            return pool.tensor_tensor(out=dst, in0=src, in1=mhalf[0:src.shape[0], 0:src.shape[1]], op=ALU.pow)

        def norm_x(t):
            R = rows(t)
            after(pool, "x_squared", t + 1)
            out(rstd(stx[0:R, 2:3], stx[0:R, 0:1]), "x_rstd")

        pool_steps(pool, pool.memset(ident[:, :], 0.0))
        pool_steps(pool, pool.affine_select(out=ident[:, :], in_=ident[:, :], compare_op=ALU.not_equal, fill=1.0,
                                            base=0, pattern=[[-1, P]], channel_multiplier=1))
        pool_steps(pool, pool.memset(upper[:, :], 1.0))
        pool.affine_select(out=upper[:, :], in_=upper[:, :], compare_op=ALU.is_ge, fill=0.0, base=0,
                           pattern=[[1, P]], channel_multiplier=-1)
        pool.memset(ones[:, :], 1.0)
        pool.memset(mhalf[:, :], -0.5)
        pool.memset(eps[:, :], EPS)
        pool_steps(pool, pool.memset(gmask[:, :, :], 0.0))
        pool_steps(pool, pool.memset(gmask[0:SN, 0, :], 1.0))
        pool_steps(pool, pool.memset(gmask[SN:P, 1, :], 1.0))
        pool.memset(state[:, :], 0.0)
        pool_steps(pool, pool.memset(raw[0][:, :, 0:3], 0.0))
        out(pool.memset(junk[:, :], 0.0), "consts")
        norm_x(0)
        norm_x(1)

        def rope(dst, src, tmp, t, R, heads):
            c, sn = cs_now[0:R, 0:HALF], cs_now[0:R, HALF:2 * HALF]
            if heads:
                c, sn = bc(c, H, 1), bc(sn, H, 1)
                x1, x2, d1, d2 = src[:, :, 0:HALF], src[:, :, HALF:ROPE], dst[:, :, 0:HALF], dst[:, :, HALF:ROPE]
            else:
                x1, x2, d1, d2 = src[:, 0:HALF], src[:, HALF:ROPE], dst[:, 0:HALF], dst[:, HALF:ROPE]
            pool.tensor_tensor(out=tmp[0], in0=x1, in1=c, op=ALU.mult)
            pool.tensor_tensor(out=tmp[1], in0=x2, in1=sn, op=ALU.mult)
            pool.tensor_tensor(out=tmp[2], in0=x1, in1=sn, op=ALU.mult)
            pool_steps(pool, pool.tensor_tensor(out=tmp[3], in0=x2, in1=c, op=ALU.mult))
            pool.tensor_tensor(out=d1, in0=tmp[0], in1=tmp[1], op=ALU.subtract)
            return pool.tensor_tensor(out=d2, in0=tmp[2], in1=tmp[3], op=ALU.add)

        def iteration(t, p, ahead):
            R = rows(t)
            C = META if R == ODD else P
            pool.wait_ge(S["cl_squared"], t + 1)
            out(rstd(stc[0:R, 2:4], stc[0:R, 0:2]), "cl_rstd")
            pool.wait_ge(S["conv_silu"], t + 1)
            out(pool.tensor_tensor(out=cz[:, :, 0:R], in0=bc(conv[:, CT - 1, 0:R], SG, 1), in1=gmask[:, :, 0:R],
                                   op=ALU.mult), "cz_ready")
            pool_steps(pool, pool.tensor_copy(cs_now[:, :], cs[:, ds(t, 1), :].rearrange("p o d -> p (o d)")))
            free(pool, "kr", t)
            pool.wait_ge(S["kv_copied"], t + 1)
            out(rope(kr[0:R, :], kv[p][0:R, KL:N_KV], [krt[0:R, j, :] for j in range(4)], t, R, False), "kr_done")
            pool.wait_ge(S["dt_done"], t + 1)
            out(pool.tensor_tensor(out=ud[0:C, :, 0:C], in0=bc(upper[0:C, 0:C], SH, 1),
                                   in1=bc(dts[0:C, DTA, :], C, 2), op=ALU.mult), "ud_ready")
            pool.wait_ge(S["xs_copied"], t + 1)
            out(pool.tensor_tensor(out=by_head(dx[0:C, :], SP_), in0=by_head(xs[0:C, :], SP_),
                                   in1=bc(d_skip[0:C, :], SP_, 2), op=ALU.mult), "dx_ready")
            pool.wait_ge(S["decay_exp"], t + 1)
            pool.wait_ge(S["xdt_ready"], t + 1)
            out(pool.tensor_tensor(out=by_head(xw[0:C, :], SP_), in0=by_head(xdt[0:C, :], SP_),
                                   in1=bc(dts[0:C, DEC, :], SP_, 2), op=ALU.mult), "xw_ready")
            pool.wait_ge(S["seg_exp"], t + 1)
            pool.wait_ge(S["cb_taken"], t + 1)
            for g in range(SG):
                ins = pool.tensor_tensor(out=seg[0:C, 4 * g:4 * g + 4, 0:C], in0=seg[0:C, 4 * g:4 * g + 4, 0:C],
                                         in1=bc(cbm[0:C, g, 0:C], 4, 1), op=ALU.mult)
            out(ins, "att_ready")
            if ahead:
                norm_x(t + 2)
            pool.wait_ge(S["q_copied"], t + 1)
            out(rope(q[0:R, :, NOPE:QK], q[0:R, :, NOPE:QK], [rp[0:R, j, :, :] for j in range(4)], t, R, True), "q_roped")
            pool.wait_ge(S["qk_sums"], t + 1)
            pool.wait_ge(S["kr_squared"], t + 1)
            pool_steps(pool, pool.tensor_tensor(out=stq[0:R, H:2 * H], in0=stq[0:R, H:2 * H],
                                                in1=stq[0:R, 4 * H:4 * H + 1].to_broadcast([R, H]), op=ALU.add))
            out(rstd(stq[0:R, 2 * H:4 * H], stq[0:R, 0:2 * H]), "qk_rstd")
            pool.wait_ge(S["qk_rstd"], t + 1)
            out(pool.tensor_tensor(out=q[0:R, :, :], in0=q[0:R, :, :], in1=bc(stq[0:R, 2 * H:3 * H], QK, 2),
                                   op=ALU.mult), "q_normed")
            out(pool.tensor_tensor(out=k[0:R, :, NOPE:QK], in0=bc(kr[0:R, :], H, 1),
                                   in1=bc(stq[0:R, 3 * H:4 * H], ROPE, 2), op=ALU.mult), "k_normed")
            pool.wait_ge(S["y_squared"], t + 1)
            out(rstd(sty[0:C, 2:4], sty[0:C, 0:2]), "y_rstd")

        iteration(0, 0, True)
        with pool.Fori(0, 3) as i:
            pool_steps.begin(i, POOL_TWO)
            iteration(i * 2 + 1, 1, True)
            iteration(i * 2 + 2, 0, True)
            pool_steps.end(3)
        iteration(7, 1, False)
        iteration(8, 0, False)

    @block.scalar
    def _(act):
        act.preload_act_table_set("natural_log_exp_and_others")
        def load_small(dst, src):
            act.dma_start(dst, src).then_inc(smalls, 16)

        act.dma_start(attn_g[:, :], a["attn_norm_g"].rearrange("o (k p) -> p (o k)", p=P)).then_inc(gain_loaded, 16)
        load_small(qn_g[:, :], a["q_norm_g"].rearrange("o (k p) -> p (o k)", p=P))
        load_small(kvn_g[:, :], a["kv_norm_g"].to_broadcast([P, KL]))
        load_small(neg_a[:, :], a["a_log"].to_broadcast([P, SH]))
        load_small(dt_b[:, :], a["dt_bias"].to_broadcast([P, SH]))
        load_small(d_skip[:, :], a["d_skip"].to_broadcast([P, SH]))
        for j in range(CT):
            load_small(conv_w[:, j, :], a["conv_w"][0, :, j * P:(j + 1) * P].rearrange("k p -> p k"))
        load_small(conv_b[:, :], a["conv_b"].rearrange("o (c p) -> p (o c)", p=P))
        for dst, name in ((gqk, "q"), (gk, "k")):
            load_small(dst[0:NOPE, :], a[name + "_head_g_nope"].rearrange("o d -> d o"))
            for j in range(2):
                load_small(dst[NOPE + j * HALF:NOPE + (j + 1) * HALF, :], a[name + "_head_g_rope"].rearrange("o d -> d o"))
        load_small(cs[:, :, :], a["rope_table"])
        load_small(sconv[:, :], a["state_conv"][0].rearrange("b k c -> (b k) c"))

        def copy(dst, src, name):
            out(act.activation(dst, src, ACT.Copy), name)

        def square_x(t, c, p):
            R = rows(t)
            act.wait_ge(x_loaded[p], 16 * (c + 1))
            if R == ODD:
                act.wait_ge(sample_loaded, 16)
                act.wait_ge(S["consts"], 1)
            after(act, "x_normed", t)
            out(act.activation(junk[0:R, :], x[p][0:R, :], ACT.Square, scale=D ** -0.5,
                               accum_out=stx[0:R, 0:1]), "x_squared")

        def copy_xT(t):
            R = rows(t)
            after(act, "kv_ready", t)
            for j in range(2):
                act.wait_ge(S[f"xT_ready{j}"], t + 1)
                copy(xT[:, 4 * j:4 * j + 4, 0:R], ps[:, j, 0:4 * R].rearrange("p (k r) -> p k r", r=R), f"xT_copied{j}")

        def copy_xbc(t, p):
            R = rows(t)
            after(act, "halo_done", t)
            act.wait_ge(S["xbc_ready0"], t + 1)
            copy(raw[p][:, 0:4, 3:3 + R], ps[:, 2, 0:4 * R].rearrange("p (k r) -> p k r", r=R), "xbc_copied0")
            act.wait_ge(S["xbc_ready1"], t + 1)
            copy(raw[p][:, 4:6, 3:3 + R], ps[:, 3, 0:2 * R].rearrange("p (k r) -> p k r", r=R), "xbc_copied1")
            act.wait_ge(S["z_ready"], t + 1)
            after(act, "y_done", t - 1)
            copy(z[p][0:R, :], ps[0:R, 0, :], "z_copied")

        def copy_rest(t, p):
            R = rows(t)
            act.wait_ge(S["dq_ready"], t + 1)
            copy(dq[p][0:R, :], ps[0:R, 1, 0:N_DQ], "dq_copied")
            act.wait_ge(S["kv_ready"], t + 1)
            copy(kv[p][0:R, :], ps[0:R, 2, 0:N_KV], "kv_copied")

        def exp_conv(t):
            R = rows(t)
            act.wait_ge(S["conv_done"], t + 1)
            out(act.activation(ex[:, :, 0:R], conv[:, :, 0:R], ACT.Exp, scale=-1.0), "conv_exp")

        square_x(0, 0, 0)
        square_x(1, 0, 1)
        copy_xT(0)
        act.wait_ge(smalls, 16 * N_SMALLS)
        out(act.activation(neg_a[:, :], neg_a[:, :], ACT.Exp), "a_exp")
        act.wait_ge(S["rawn_ready"], 1)
        act.activation(rawn[:, 0:4 * P], ps[0:ODD, 4, :], ACT.Copy)
        copy(rawn[:, 4 * P:], ps[0:ODD, 5, 0:2 * P], "rawn_copied")
        act.wait_ge(S["z_ready"], 1)
        copy(z[0][0:ODD, :], ps[0:ODD, 0, :], "z_copied")
        copy_rest(0, 0)
        act.wait_ge(S["sconv_ready"], 1)
        copy(sT[:, :, :], ps[:, 3, 0:CT * 3 * NS].rearrange("p (c r) -> p c r", c=CT), "sconv_copied")
        act.wait_ge(S["xbc_ready0"], 1)
        copy(raw[0][:, 0:4, 3:3 + ODD], ps[:, 6, 0:4 * ODD].rearrange("p (k r) -> p k r", r=ODD), "xbc_copied0")
        act.wait_ge(S["xbc_ready1"], 1)
        copy(raw[0][:, 4:6, 3:3 + ODD], ps[:, 7, 0:2 * ODD].rearrange("p (k r) -> p k r", r=ODD), "xbc_copied1")
        copy_xT(1)

        def iteration(t, c, p, ahead, after_it):
            R = rows(t)
            C = META if R == ODD else P
            act.wait_ge(S["dt_in"], t + 1)
            act_steps(act, act.activation(dts[0:R, AV, :], dts[0:R, V, :], ACT.Abs))
            out(act.activation(dts[0:R, U, :], dts[0:R, AV, :], ACT.Exp, scale=-1.0), "dt_exp")
            act.activation(junk_cl[0:R, 0:QL], dq[p][0:R, SH:N_DQ], ACT.Square, scale=QL ** -0.5, accum_out=stc[0:R, 0:1])
            out(act.activation(junk_cl[0:R, QL:QL + KL], kv[p][0:R, 0:KL], ACT.Square, scale=KL ** -0.5,
                               accum_out=stc[0:R, 1:2]), "cl_squared")
            out(act.activation(zex[0:R, :], z[p][0:R, :], ACT.Exp, scale=-1.0), "z_exp")
            act.wait_ge(S["dt_w"], t + 1)
            out(act.activation(dts[0:R, LN, :], dts[0:R, W, :], ACT.Ln), "dt_ln")
            if after_it:
                copy_xbc(t + 1, 1 - p)
            act.wait_ge(S["clT_ready0"], t + 1)
            copy(clT[:, 0:4, 0:R], ps[:, 4, 0:4 * R].rearrange("p (k r) -> p k r", r=R), "clT_copied0")
            act.wait_ge(S["xs_ready"], t + 1)
            copy(xs[0:R, :], ps[0:R, 6, :], "xs_copied")
            act.wait_ge(S["bT_ready"], t + 1)
            copy(clT[:, 4, 0:R], ps[:, 5, 0:R], "clT_copied1")
            nb = 2 if R == ODD else 1
            copy(bn[0:R, 0:nb * P], ps[0:R, 5, P:(1 + nb) * P], "bn_copied")
            act.wait_ge(S["acs_ready"], t + 1)
            act.activation(dts[0:C, EACS, :], ps[0:C, 7, 0:SH], ACT.Exp)
            copy(dts[0:C, ACS, :], ps[0:C, 7, 0:SH], "acs_copied")
            act.wait_ge(S["bc_ready"], t + 1)
            last = ps[:, 6:8, 0:4 * C].rearrange("p b (h i) -> p b h i", i=C)[:, :, :, C - 1]
            out(act.activation(dts[:, DLAST, :].rearrange("p (b h) -> p b h", b=2), last, ACT.Exp), "last_exp")
            act.wait_ge(S["decay_in"], t + 1)
            out(act.activation(dts[0:C, DEC, :], dts[0:C, DIN, :], ACT.Exp), "decay_exp")
            act.wait_ge(S["seg_done"], t + 1)
            out(act.activation(seg[0:C, :, 0:C], seg[0:C, :, 0:C], ACT.Exp), "seg_exp")
            if ahead:
                square_x(t + 2, c + 1, p)
            if after_it:
                copy_rest(t + 1, 1 - p)
                exp_conv(t + 1)
            act.wait_ge(S["q_ready"], t + 1)
            copy(q[0:R, :, :].rearrange("p (b h) d -> p b (h d)", b=2), ps[0:R, 4:6, 0:4 * QK], "q_copied")
            act.wait_ge(S["kvu_ready"], t + 1)
            up = ps[0:R, 6:8, :].rearrange("p b (h d) -> p b h d", d=NOPE + VD)
            out(act.activation(ksq[0:R, :, :].rearrange("p (b h) d -> p b h d", b=2), up[:, :, :, 0:NOPE],
                               ACT.Square, scale=QK ** -0.5), "kn_squared")
            free(act, "v", t)
            copy(v[0:R, :].rearrange("p (b h d) -> p b h d", b=2, d=VD), up[:, :, :, NOPE:NOPE + VD], "v_copied")
            act.wait_ge(S["kr_done"], t + 1)
            out(act.activation(junk_kr[0:R, :], kr[0:R, :], ACT.Square, scale=QK ** -0.5,
                               accum_out=stq[0:R, 4 * H:4 * H + 1]), "kr_squared")
            act.wait_ge(S["q_roped"], t + 1)
            out(act.activation(qsq[0:R, :, :], q[0:R, :, :], ACT.Square, scale=QK ** -0.5), "q_squared")
            if ahead:
                copy_xT(t + 2)
            act.wait_ge(S["y_done"], t + 1)
            for g in range(SG):
                w = SW // SG
                ins = act.activation(junk_y[0:C, g * w:(g + 1) * w], y[0:C, g * w:(g + 1) * w], ACT.Square,
                                     scale=w ** -0.5, accum_out=sty[0:C, g:g + 1])
            out(ins, "y_squared")
            free(act, "kT", t)
            for j, b in ((0, 5), (1, 4)):
                act.wait_ge(S[f"kT_ready{j}"], t + 1)
                copy(kT[:, 4 * j:4 * j + 4, 0:R], ps[0:QK, b, 0:4 * R].rearrange("p (h r) -> p h r", r=R), f"kT_copied{j}")

        exp_conv(0)
        iteration(0, 0, 0, True, True)
        act.wait_ge(stored["odd"], 16 * N_ODD_STORES)
        with act.Fori(0, 3) as i:
            act_steps.begin(i, ACT_TWO)
            iteration(i * 2 + 1, i, 1, True, True)
            iteration(i * 2 + 2, i + 1, 0, True, True)
            act_steps.end(3)
        iteration(7, 3, 1, False, True)
        iteration(8, 4, 0, False, False)
        act.wait_ge(S["rawl_ready"], 1)
        act.activation(rawl[:, 0:4 * P], ps[0:3, 6, :], ACT.Copy)
        copy(rawl[:, 4 * P:], ps[0:3, 7, 0:2 * P], "rawl_copied")
        act.wait_ge(S["stout_ready"], 1)
        copy(stout[:, :, :], ps[:, 5, 0:2 * P].rearrange("p (b n) -> p b n", b=2), "stout_copied")

    @block.vector
    def _(dve):
        def add_one_reciprocal(ap):
            dve_steps(dve, dve.tensor_scalar(ap, ap, 1.0, None, ALU.add))
            dve_steps(dve, dve.reciprocal(ap, ap))

        def norm_x(t, p):
            R = rows(t)
            dve.wait_ge(S["x_rstd"], t + 1)
            out(dve.tensor_scalar(x[p][0:R, :], x[p][0:R, :], stx[0:R, 2:3], None, ALU.mult), "x_normed")

        norm_x(0, 0)
        dve.wait_ge(gain_loaded, 16)
        for kd in range(KD):
            dve.wait_ge(weights[kd], 16)
            out(dve.tensor_scalar(w_in[:, kd, :], w_in[:, kd, :], attn_g[:, kd:kd + 1], None, ALU.mult), "folded")
        norm_x(1, 1)
        dve.wait_ge(smalls, 16 * N_SMALLS)
        dve.wait_ge(up_weights, 32)
        for kd in range(QL // P):
            ins = dve.tensor_scalar(w_uq[:, kd, :], w_uq[:, kd, :], qn_g[:, kd:kd + 1], None, ALU.mult)
        out(ins, "up_folded")
        dve_steps(dve, dve.tensor_tensor(out=gqk[:, :], in0=gqk[:, :], in1=gk[:, :], op=ALU.mult))
        dve.wait_ge(S["sconv_copied"], 1)
        dve.wait_ge(S["a_exp"], 1)
        dve.wait_ge(S["consts"], 1)

        def convolve(t, p):
            R = rows(t)
            odd = R == ODD
            C = META if odd else P
            if not odd:
                out(dve.tensor_copy(raw[p][:, :, 0:3], raw[1 - p][:, :, P:P + 3]), "halo_done")
                dve.wait_ge(S["halo_done"], t + 1)
            dve.wait_ge(S["xbc_copied1"], t + 1)
            for kk in range(4):
                for j in range(CT):
                    parts = [(0, C, raw[p][:, j, kk:kk + C])]
                    if odd:
                        own = raw[p][:, j, 3 + META:3 + ODD] if kk == 3 else sT[:, j, :].rearrange("p (b k) -> p b k", k=3)[:, :, kk]
                        parts.append((META, ODD, own))
                    for lo, hi, src in parts:
                        o = conv[:, j, lo:hi]
                        if kk == 0:
                            ins = dve.tensor_scalar(o, src, conv_w[:, j, 0:1], conv_b[:, j:j + 1], ALU.mult, ALU.add)
                        else:
                            ins = dve.scalar_tensor_tensor(out=o, in0=src, scalar=conv_w[:, j, kk:kk + 1], in1=o,
                                                           op0=ALU.mult, op1=ALU.add)
                if kk < 3:
                    dve_steps(dve, ins)
            out(ins, "conv_done")
            if odd:
                out(dve.tensor_copy(raw[0][:, :, P:P + 3], raw[0][:, :, META:META + 3]), "halo_done")

        def iteration(t, p, ahead, after_it):
            R = rows(t)
            odd = R == ODD
            C = META if odd else P
            dve.wait_ge(S["dq_copied"], t + 1)
            out(dve.tensor_tensor(out=dts[0:R, V, :], in0=dq[p][0:R, 0:SH], in1=dt_b[0:R, :], op=ALU.add), "dt_in")
            dve.wait_ge(S["dt_exp"], t + 1)
            dve_steps(dve, dve.tensor_scalar(dts[0:R, W, :], dts[0:R, U, :], 1.0, None, ALU.add))
            out(dve.scalar_tensor_tensor(out=dts[0:R, W1, :], in0=dts[0:R, W, :], scalar=-1.0, in1=dts[0:R, U, :],
                                         op0=ALU.add, op1=ALU.subtract), "dt_w")
            dve.wait_ge(S["conv_exp"], t + 1)
            add_one_reciprocal(ex[:, :, 0:R])
            out(dve.tensor_tensor(out=conv[:, :, 0:R], in0=conv[:, :, 0:R], in1=ex[:, :, 0:R], op=ALU.mult), "conv_silu")
            dve.wait_ge(S["cl_rstd"], t + 1)
            free(dve, "lat", t)
            dve.tensor_scalar(cq[0:R, :], dq[p][0:R, SH:N_DQ], stc[0:R, 2:3], None, ALU.mult)
            out(dve.scalar_tensor_tensor(out=lat[0:R, :], in0=kv[p][0:R, 0:KL], scalar=stc[0:R, 3:4], in1=kvn_g[0:R, :],
                                         op0=ALU.mult, op1=ALU.mult), "cl_normed")
            dve.wait_ge(S["dt_ln"], t + 1)
            dve.wait_ge(S["dt_w"], t + 1)
            dve.tensor_tensor(out=dts[0:R, LN, :], in0=dts[0:R, LN, :], in1=dts[0:R, W1, :], op=ALU.subtract)
            dve_steps(dve, dve.tensor_scalar(dts[0:R, V, :], dts[0:R, V, :], 0.0, None, ALU.max))
            dve_steps(dve, dve.tensor_tensor(out=dts[0:R, DT, :], in0=dts[0:R, V, :], in1=dts[0:R, LN, :], op=ALU.add))
            out(dve.scalar_tensor_tensor(out=dts[0:R, DTA, :], in0=dts[0:R, DT, :], scalar=-1.0, in1=neg_a[0:R, :],
                                         op0=ALU.mult, op1=ALU.mult), "dt_done")
            dve.wait_ge(S["xs_copied"], t + 1)
            out(dve.tensor_tensor(out=by_head(xdt[0:C, :], SP_), in0=by_head(ps[0:C, 6, :], SP_),
                                  in1=bc(dts[0:C, DT, :], SP_, 2), op=ALU.mult), "xdt_ready")
            dve.wait_ge(S["last_exp"], t + 1)
            every = ps[0:C, 6:8, 0:4 * C].rearrange("p b (h i) -> p b h i", i=C)
            out(dve.tensor_tensor(out=dts[0:C, DIN, :].rearrange("p (b h) -> p b h", b=2), in0=every[:, :, :, C - 1],
                                  in1=dts[0:C, ACS, :].rearrange("p (b h) -> p b h", b=2), op=ALU.subtract), "decay_in")
            for h in range(SH):
                ins = dve.tensor_scalar(seg[0:C, h, 0:C], every[:, h // 4, h % 4, :], dts[0:C, ACS, h:h + 1], 0.0,
                                        ALU.subtract, ALU.min)
            out(ins, "seg_done")
            dve.wait_ge(S["cb_ready"], t + 1)
            out(dve.tensor_tensor(out=cbm[0:C, :, 0:C], in0=ps[0:C, 5, 2 * P:2 * P + 2 * C].rearrange("p (g i) -> p g i", g=SG),
                                  in1=bc(upper[0:C, 0:C], SG, 1), op=ALU.mult), "cb_taken")
            dve.wait_ge(S["z_exp"], t + 1)
            add_one_reciprocal(zex[0:R, :])
            out(dve.tensor_tensor(out=z[p][0:R, :], in0=z[p][0:R, :], in1=zex[0:R, :], op=ALU.mult), "z_silu")
            if ahead:
                norm_x(t + 2, p)
            if after_it:
                convolve(t + 1, 1 - p)
            dve.wait_ge(S["kn_squared"], t + 1)
            dve.tensor_reduce(stq[0:R, H:2 * H], ksq[0:R, :, :], AXX, ALU.add)
            dve.wait_ge(S["q_squared"], t + 1)
            out(dve.tensor_reduce(stq[0:R, 0:H], qsq[0:R, :, :], AXX, ALU.add), "qk_sums")
            dve.wait_ge(S["yo_ready"], t + 1)
            out(dve.tensor_tensor(out=by_head(y[0:C, :], SP_), in0=by_head(ps[0:C, 5, :], SP_),
                                  in1=bc(dts[0:C, EACS, :], SP_, 2), op=ALU.mult), "yo_taken")
            dve.wait_ge(S["yo_taken"], t + 1)
            dve.wait_ge(S["yd_ready"], t + 1)
            out(dve.tensor_tensor(out=y[0:C, :], in0=y[0:C, :], in1=ps[0:C, 4, :], op=ALU.add), "yd_taken")
            dve.wait_ge(S["yd_taken"], t + 1)
            dve.wait_ge(S["dx_ready"], t + 1)
            dve_steps(dve, dve.tensor_tensor(out=y[0:C, :], in0=y[0:C, :], in1=dx[0:C, :], op=ALU.add))
            out(dve.tensor_tensor(out=y[0:C, :], in0=y[0:C, :], in1=z[p][0:C, :], op=ALU.mult), "y_done")
            dve.wait_ge(S["qk_rstd"], t + 1)
            dve.wait_ge(S["v_copied"], t + 1)
            out(dve.tensor_tensor(out=k[0:R, :, 0:NOPE].rearrange("p (b h) d -> p b h d", b=2),
                                  in0=ps[0:R, 6:8, :].rearrange("p b (h d) -> p b h d", d=NOPE + VD)[:, :, :, 0:NOPE],
                                  in1=bc(stq[0:R, 3 * H:4 * H].rearrange("p (b h) -> p b h", b=2), NOPE, 3),
                                  op=ALU.mult), "kn_taken")
            dve.wait_ge(S["st_ready"], t + 1)
            dve.wait_ge(S["last_exp"], t + 1)
            half = [slice(0, SN), slice(SN, P)]
            for g in range(SG):
                ins = dve.tensor_tensor(out=by_head(state[half[g], :], SP_), in0=by_head(state[half[g], :], SP_),
                                        in1=bc(dts[half[g], DLAST, 4 * g:4 * g + 4], SP_, 2), op=ALU.mult)
            dve_steps(dve, ins)
            for g in range(SG):
                ins = dve.tensor_tensor(out=state[half[g], :], in0=state[half[g], :],
                                        in1=ps[half[g], 4, 256 * g:256 * (g + 1)], op=ALU.add)
            out(ins, "state_done")
            free(dve, "qT", t)
            for j, b in ((0, 7), (1, 6)):
                dve.wait_ge(S[f"qT_ready{j}"], t + 1)
                out(dve.tensor_scalar(qT[:, 4 * j:4 * j + 4, 0:R], ps[0:QK, b, 0:4 * R].rearrange("p (h r) -> p h r", r=R),
                                      gqk[:, 0:1], None, ALU.mult), f"qT_copied{j}")
            dve.wait_ge(S["y_rstd"], t + 1)
            if not odd:
                dve.wait_ge(stored["ys"], t * 16)
            for g in range(SG):
                w = SW // SG
                ins = dve.tensor_scalar(ys[0:C, g * w:(g + 1) * w], y[0:C, g * w:(g + 1) * w], sty[0:C, 2 + g:3 + g],
                                        None, ALU.mult)
            out(ins, "y_normed")

        convolve(0, 0)
        iteration(0, 0, True, True)
        dve.wait_ge(stored["odd"], 16 * N_ODD_STORES)
        with dve.Fori(0, 3) as i:
            dve_steps.begin(i, DVE_TWO)
            iteration(i * 2 + 1, 1, True, True)
            iteration(i * 2 + 2, 0, True, True)
            dve_steps.end(3)
        iteration(7, 1, False, True)
        iteration(8, 0, False, False)

    @block.tensor
    def _(pe):
        def product(dst, lhsT, rhs, name):
            for n, (l, r) in enumerate(zip(lhsT, rhs)):
                ins = pe.matmul(dst, l, r, start=(n == 0), stop=(n == len(lhsT) - 1))
            if name:
                out(ins, name)

        def turn(dst, srcs, name):
            for d, src in zip(dst, srcs):
                ins = pe.transpose(d, src, ident[0:src.shape[0], 0:src.shape[0]])
            out(ins, name)

        def turn_x(t, p):
            R = rows(t)
            pe.wait_ge(S["x_normed"], t + 1)
            for j, before in ((0, "z_copied"), (1, "dq_copied")):
                after(pe, before, t)
                turn([ps[:, j, n * R:(n + 1) * R] for n in range(4)],
                     [x[p][0:R, kd * P:(kd + 1) * P] for kd in range(4 * j, 4 * j + 4)], f"xT_ready{j}")

        def project_xbc(t, j, cts, before):
            R = rows(t)
            pe.wait_ge(S["xT_copied0"], t + 1)
            pe.wait_ge(S["xT_copied1"], t + 1)
            after(pe, before, t)
            for n, ct in enumerate(cts):
                product(ps[:, 2 + j, n * R:(n + 1) * R],
                        [w_in[:, kd, C_XBC + ct * P:C_XBC + (ct + 1) * P] for kd in range(KD)],
                        [xT[:, kd, 0:R] for kd in range(KD)], f"xbc_ready{j}" if ct == cts[-1] else None)

        def project_x(t):
            project_xbc(t, 0, range(0, 4), "kv_copied")

        def project_bcz(t):
            R = rows(t)
            project_xbc(t, 1, range(4, 6), "xbc_copied1")
            product(ps[0:R, 0, :], [xT[:, kd, 0:R] for kd in range(KD)], [w_in[:, kd, 0:SW] for kd in range(KD)], "z_ready")

        def project_rest(t):
            R = rows(t)
            for b, lo, n, name in ((1, C_DT, N_DQ, "dq_ready"), (2, C_KV, N_KV, "kv_ready")):
                if b == 2:
                    pe.wait_ge(S["xbc_copied0"], t + 1)
                product(ps[0:R, b, 0:n], [xT[:, kd, 0:R] for kd in range(KD)],
                        [w_in[:, kd, lo:lo + n] for kd in range(KD)], name)

        def iteration(t, p, ahead, after_it):
            R = rows(t)
            C = META if R == ODD else P
            if after_it:
                project_bcz(t + 1)
            pe.wait_ge(S["cl_normed"], t + 1)
            after(pe, "kT_copied1", t)
            turn([ps[:, 4, n * R:(n + 1) * R] for n in range(4)],
                 [cq[0:R, n * P:(n + 1) * P] for n in range(3)] + [lat[0:R, 0:P]], "clT_ready0")
            pe.wait_ge(S["conv_silu"], t + 1)
            after(pe, "qT_copied1", t)
            turn([ps[0:R, 6, n * P:(n + 1) * P] for n in range(4)], [conv[:, n, 0:R] for n in range(4)], "xs_ready")
            nb = 2 if R == ODD else 1
            after(pe, "kT_copied0", t)
            turn([ps[:, 5, 0:R]], [lat[0:R, P:2 * P]], "clT_ready1")
            turn([ps[0:R, 5, (1 + n) * P:(2 + n) * P] for n in range(nb)], [conv[:, 4 + n, 0:R] for n in range(nb)], "bT_ready")
            pe.wait_ge(S["dt_done"], t + 1)
            after(pe, "qT_copied0", t)
            product(ps[0:C, 7, 0:SH], [upper[0:C, 0:C]], [dts[0:C, DTA, :]], "acs_ready")
            pe.wait_ge(S["ud_ready"], t + 1)
            pe.wait_ge(S["xs_copied"], t + 1)
            pe.wait_ge(S["xdt_ready"], t + 1)
            pe.wait_ge(S["acs_copied"], t + 1)
            for b in range(2):
                product(ps[:, 6 + b, 0:4 * C], [ones[0:C, :]], [ud[0:C, 4 * b:4 * b + 4, 0:C]], "bc_ready" if b else None)
            pe.wait_ge(S["cz_ready"], t + 1)
            pe.wait_ge(S["bn_copied"], t + 1)
            product(ps[0:C, 5, 2 * P:2 * P + 2 * C], [conv[:, 4, 0:C]], [cz[:, :, 0:C]], "cb_ready")
            if after_it:
                project_rest(t + 1)
            pe.wait_ge(S["clT_copied0"], t + 1)
            pe.wait_ge(S["clT_copied1"], t + 1)
            pe.wait_ge(S["cb_taken"], t + 1)
            for b in range(2):
                w = 4 * QK
                product(ps[0:R, 4 + b, 0:w], [clT[:, n, 0:R] for n in range(3)],
                        [w_uq[:, n, b * w:(b + 1) * w] for n in range(3)], "q_ready" if b else None)
            pe.wait_ge(S["seg_done"], t + 1)
            pe.wait_ge(S["last_exp"], t + 1)
            for b in range(2):
                product(ps[0:R, 6 + b, :], [clT[:, 3 + n, 0:R] for n in range(2)],
                        [w_ukv[:, n, b * 512:(b + 1) * 512] for n in range(2)], "kvu_ready" if b else None)
            if ahead:
                turn_x(t + 2, p)
            pe.wait_ge(S["att_ready"], t + 1)
            pe.wait_ge(S["q_copied"], t + 1)
            for h in range(SH):
                product(ps[0:C, 4, h * SP_:(h + 1) * SP_], [seg[0:C, h, 0:C]], [xdt[0:C, h * SP_:(h + 1) * SP_]],
                        "yd_ready" if h == SH - 1 else None)
            after(pe, "state_done", t)
            for g in range(SG):
                product(ps[0:C, 5, 256 * g:256 * (g + 1)], [cz[:, g, 0:C]], [state[:, :]], "yo_ready" if g else None)
            pe.wait_ge(S["xw_ready"], t + 1)
            pe.wait_ge(S["yd_taken"], t + 1)
            product(ps[:, 4, :], [bn[0:C, 0:P]], [xw[0:C, :]], "st_ready")
            if ahead:
                project_x(t + 2)
            pe.wait_ge(S["q_normed"], t + 1)
            pe.wait_ge(S["kn_taken"], t + 1)
            pe.wait_ge(S["v_copied"], t + 1)
            for j, b in ((0, 7), (1, 6)):
                turn([ps[0:QK, b, n * R:(n + 1) * R] for n in range(4)],
                     [q[0:R, 4 * j + n, :] for n in range(4)], f"qT_ready{j}")
            pe.wait_ge(S["k_normed"], t + 1)
            for j, b, before in ((0, 5, "yo_taken"), (1, 4, "state_done")):
                pe.wait_ge(S[before], t + 1)
                turn([ps[0:QK, b, n * R:(n + 1) * R] for n in range(4)],
                     [k[0:R, 4 * j + n, :] for n in range(4)], f"kT_ready{j}")

        pe.wait_ge(S["consts"], 1)
        turn_x(0, 0)
        pe.wait_ge(S["xT_copied0"], 1)
        pe.wait_ge(S["xT_copied1"], 1)
        for kd in range(KD):
            pe.wait_ge(S["folded"], kd + 1)
            for bank, lo, n, name in ((4, C_XBC, 4 * P, None), (5, C_XBC + 4 * P, 2 * P, "rawn_ready"), (0, 0, SW, "z_ready"),
                                      (1, C_DT, N_DQ, "dq_ready"), (2, C_KV, N_KV, "kv_ready")):
                ins = pe.matmul(ps[0:ODD, bank, 0:n], xT[:, kd, 0:ODD], w_in[:, kd, lo:lo + n],
                                start=(kd == 0), stop=(kd == KD - 1))
                if kd == KD - 1 and name:
                    out(ins, name)
        pe.wait_ge(smalls, 16 * N_SMALLS)
        turn([ps[:, 3, n * 3 * NS:(n + 1) * 3 * NS] for n in range(CT)],
             [sconv[:, n * P:(n + 1) * P] for n in range(CT)], "sconv_ready")
        pe.wait_ge(S["rawn_copied"], 1)
        turn([ps[:, 6, n * ODD:(n + 1) * ODD] for n in range(4)], [rawn[:, n * P:(n + 1) * P] for n in range(4)], "xbc_ready0")
        turn([ps[:, 7, n * ODD:(n + 1) * ODD] for n in range(2)], [rawn[:, n * P:(n + 1) * P] for n in range(4, CT)],
             "xbc_ready1")
        pe.wait_ge(S["xbc_copied1"], 1)
        pe.wait_ge(S["sconv_copied"], 1)
        pe.wait_ge(S["up_folded"], 1)
        turn_x(1, 1)
        project_x(1)
        iteration(0, 0, True, True)
        with pe.Fori(0, 3) as i:
            iteration(i * 2 + 1, 1, True, True)
            iteration(i * 2 + 2, 0, True, True)
        iteration(7, 1, False, True)
        iteration(8, 0, False, False)
        pe.wait_ge(S["qT_copied1"], NT + 1)
        turn([ps[0:3, 6 + n // 4, n % 4 * P:(n % 4 + 1) * P] for n in range(CT)],
             [raw[0][:, n, P:P + 3] for n in range(CT)], "rawl_ready")
        pe.wait_ge(S["kT_copied0"], NT + 1)
        turn([ps[:, 5, n * P:(n + 1) * P] for n in range(2)], [state[:, n * P:(n + 1) * P] for n in range(2)], "stout_ready")

    ctx.close()
    nc.clear_and_free_semaphores(sems)
    nc.all_engine_barrier()


GP = 4
NG = NPG // GP


class Pages:

    def __init__(self, nc, ctx, a, s):
        sb = lambda name, shape, dt=F32: ctx.enter_context(nc.sbuf_tensor("p_" + name, shape, dt))
        sem = lambda name: ctx.enter_context(nc.semaphore("p_" + name))
        self.a, self.s = a, s
        self.ids = sb("ids", [1, NS * NPG], I32)
        self.latn = [sb(f"latn{i}", [P, NPG, LATW]) for i in range(2)]
        self.wk = sb("wk", [P, 2, H * NOPE])
        self.qn = sb("qn", [NOPE, H, NS])
        self.qr = sb("qr", [ROPE, H, NS])
        self.ids_loaded, self.w_loaded = sem("ids_loaded"), sem("w_loaded")
        self.lat_loaded = [[sem(f"lat_loaded{i}{g}") for g in range(NG)] for i in range(2)]

    def load_ids_and_weights(self, sp):
        sp.dma_start(self.ids[:, :], self.a["page_table"].rearrange("b n -> (b n)").unsqueeze(0)).then_inc(self.ids_loaded, 16)
        ukv = self.a["w_ukv"][0].rearrange("(c p) (h x) -> p c h x", p=P, x=NOPE + VD)
        for c in range(2):
            sp.dma_start(by_head(self.wk[:, c, :], NOPE), ukv[:, c, :, 0:NOPE]).then_inc(self.w_loaded, 16)
        sp.dma_start(self.qn[:, :, :], self.s["qT"][:, 0:NOPE, T:TOK].rearrange("h d b -> d h b")).then_inc(self.w_loaded, 16)
        sp.dma_start(self.qr[:, :, :], self.s["qT"][:, NOPE:QK, T:TOK].rearrange("h d b -> d h b")).then_inc(self.w_loaded, 16)
        sp.wait_ge(self.ids_loaded, 16)

    def load(self, sp, b, p):
        for pg in range(NPG):
            with sp.register(f"page{'_first' if isinstance(b, int) else ''}{p}_{pg}") as reg:
                sp.reg_load(reg, self.ids[0:1, ds(b * NPG + pg, 1)])
                page = sp.snap(reg, min_val=0, max_val=self.a["cache_kv_latent"].shape[1] - 1)
                for cols, src in ((slice(0, KL), "cache_kv_latent"), (slice(KL, LATW), "cache_k_rope")):
                    sp.dma_start(self.latn[p][:, pg, cols],
                                 self.a[src][0, ds(page, 1), :, :].rearrange("o t d -> (o t) d")).then_inc(
                                     self.lat_loaded[p][pg // GP], 16)


def attention_block(nc, s, pages):
    ctx = ExitStack()
    sb = lambda name, shape: ctx.enter_context(nc.sbuf_tensor("a_" + name, shape, F32))
    sem = lambda name: ctx.enter_context(nc.semaphore("a_" + name))
    PAIRS = H // 2
    order = [(i + 1, P, META + i * P) for i in reversed(range(NT))]
    N = len(order)
    groups = []
    for n, (tile, _, _) in enumerate(order):
        blocks = list(range(tile + 1))
        groups.append([blocks[b:b + 2] for b in range(0, len(blocks), 2)])
    first_group = [sum(len(g) for g in groups[:n]) for n in range(N + 1)]
    G = first_group[N]

    ps = ctx.enter_context(nc.psum_tensor("a_ps", [P, 8, 512], F32))
    flat = ps[:, :, :].rearrange("p b c -> p (b c)")
    q = [sb(f"q{i}", [QK, 2, T]) for i in range(2)]
    k = [sb(f"k{i}", [QK, 2, T]) for i in range(2)]
    v = [sb(f"v{i}", [P, NT + 1, 2 * VD]) for i in range(2)]
    prob = [[sb(f"prob{i}{h}", [P, T]) for h in range(2)] for i in range(2)]
    pt = [sb(f"pt{i}", [P, 2, 2, P]) for i in range(2)]
    oT = [sb(f"oT{i}", [P, P]) for i in range(2)]
    st = [[sb(f"st{i}{h}", [P, 4]) for h in range(2)] for i in range(4)]
    att = sb("att", [P, NT, H * VD])
    mask = sb("mask", [P, P])
    ident = sb("ident", [P, P])
    credit = sb("credit", [P, 3])

    loaded = [sem(f"loaded{i}") for i in range(2)]
    consts, scores_ready, max_ready, exp_done, pt_ready = [
        sem(n) for n in ("consts", "scores_ready", "max_ready", "exp_done", "pt_ready")]
    att_stored = sem("att_stored")
    pt_copied = [sem("pt_copied_by_dve"), sem("pt_copied_by_act")]
    o_ready, oT_copied, back_ready, att_done = [sem(n) for n in ("o_ready", "oT_copied", "back_ready", "att_done")]
    dve_steps = Steps(sem("dve_steps"), "attention dve")
    pool_steps = Steps(sem("pool_steps"), "attention pool")
    block = ctx.enter_context(nc.Block())

    def o_bank(n):
        return 5 if n % 2 else 2

    def width(n):
        tile, R, at = order[n]
        return at + R

    @block.sync
    def _(sp):
        def store(u):
            cols = slice(u * 2 * VD, (u + 1) * 2 * VD)
            sp.wait_ge(att_done, (u + 1) * N + 1)
            sp.dma_start(s["att"][0:SEQ, cols].rearrange("(t p) c -> p t c", p=P), att[:, :, cols]).then_inc(att_stored, 16)

        for u in range(PAIRS):
            p = u % 2
            if u >= 2:
                sp.wait_ge(o_ready, (u - 1) * N)
            cols = slice(u * 2 * VD, (u + 1) * 2 * VD)
            for dst, src in (
                (q[p][:, :, :], s["qT"][2 * u:2 * u + 2, :, 0:T].rearrange("h d t -> d h t")),
                (k[p][:, :, :], s["kT"][2 * u:2 * u + 2, :, 0:T].rearrange("h d t -> d h t")),
                (v[p][0:META, 0, :], s["v"][0:META, cols]),
                (v[p][:, 1:NT + 1, :], s["v"][META:T, cols].rearrange("(j p) c -> p j c", p=P)),
            ):
                sp.dma_start(dst, src).then_inc(loaded[p], 16)
            if u == 1:
                pages.load_ids_and_weights(sp)
                pages.load(sp, 0, 0)
            if u == PAIRS - 1:
                pages.load(sp, 1, 1)
            if u >= 1:
                store(u - 1)
        store(PAIRS - 1)
        sp.wait_ge(att_stored, PAIRS * 16)

    @block.gpsimd
    def _(pool):
        pool_steps(pool, pool.memset(ident[:, :], 0.0))
        pool.affine_select(out=ident[:, :], in_=ident[:, :], compare_op=ALU.not_equal, fill=1.0,
                           base=0, pattern=[[-1, P]], channel_multiplier=1)
        pool_steps(pool, pool.memset(mask[:, :], 0.0))
        pool.memset(credit[:, 0:1], 0.0).then_inc(att_done, 1)
        pool.memset(credit[:, 1:2], 0.0).then_inc(pt_copied[0], 1)
        pool.memset(credit[:, 2:3], 0.0).then_inc(pt_copied[1], 1)
        pool.affine_select(out=mask[:, :], in_=mask[:, :], compare_op=ALU.is_ge, fill=NEG,
                           base=0, pattern=[[-1, P]], channel_multiplier=1).then_inc(consts, 1)

    def copy_groups(eng, i, par, n, mine, copied, which):
        R = order[n][1]
        for g, blocks in enumerate(groups[n]):
            gg = par * G + first_group[n] + g
            if gg % 2 != mine or g not in which:
                continue
            eng.wait_ge(pt_ready, i * 2 * G + gg + 1)
            src = ps[:, 6 + gg % 2, :].rearrange("p (b h r) -> p b h r", b=2, r=P)[:, :, :, 0:R]
            dst = pt[gg % 2][:, :, :, 0:R]
            pieces = [(META, 0, 1)] + [(P, 1, 2)] * (len(blocks) - 1) if blocks[0] == 0 else [(P, 0, len(blocks))]
            for rows_, lo, hi in pieces:
                if mine == 0:
                    ins = eng.tensor_copy(dst[0:rows_, lo:hi], src[0:rows_, lo:hi])
                else:
                    ins = eng.activation(dst[0:rows_, lo:hi], src[0:rows_, lo:hi], ACT.Copy)
            ins.then_inc(copied, 1)

    EARLY, LATE = range(0, 2), range(2, NT)

    @block.vector
    def _(dve):
        def maximum(u, n):
            tile, R, at = order[n]
            for h in range(2):
                t = st[n % 4][h]
                dve.wait_ge(scores_ready, u * 2 * N + 2 * n + h + 1)
                own = flat[0:R, 1536 * h + at:1536 * h + at + R]
                dve_steps(dve, dve.tensor_tensor(out=own, in0=own, in1=mask[0:R, 0:R], op=ALU.add))
                dve_steps(dve, dve.tensor_reduce(t[0:R, 0:1], flat[0:R, 1536 * h:1536 * h + at + R], AXX, ALU.max))
                dve.tensor_scalar(t[0:R, 1:2], t[0:R, 0:1], -SCALE, None, ALU.mult).then_inc(max_ready, 1)

        def finish(u, n):
            tile, R, at = order[n]
            for h in range(2):
                ins = dve.reciprocal(st[n % 4][h][0:R, 3:4], st[n % 4][h][0:R, 2:3])
            dve_steps(dve, ins)
            dve.wait_ge(back_ready, u * N + n + 1)
            for h in range(2):
                ins = dve.tensor_scalar(att[0:R, tile - 1, ds(u * 2 * VD + h * VD, VD)],
                                        ps[0:R, o_bank(n), P + h * VD:P + (h + 1) * VD],
                                        st[n % 4][h][0:R, 3:4], None, ALU.mult)
            ins.then_inc(att_done, 1)

        dve.wait_ge(consts, 1)
        with dve.Fori(0, PAIRS // 2) as i:
            dve_steps.begin(i, 2 * N * 5)
            for par in range(2):
                for n in range(N + 2):
                    if 1 <= n <= N:
                        copy_groups(dve, i, par, n - 1, 0, pt_copied[0], EARLY)
                    if n < N:
                        maximum(i * 2 + par, n)
                    if n >= 2:
                        finish(i * 2 + par, n - 2)
                    if 1 <= n <= N:
                        copy_groups(dve, i, par, n - 1, 0, pt_copied[0], LATE)
            dve_steps.end(PAIRS // 2)

    @block.scalar
    def _(act):
        with act.Fori(0, PAIRS // 2) as i:
            for par in range(2):
                u = i * 2 + par
                for n in range(N + 1):
                    if n >= 1:
                        copy_groups(act, i, par, n - 1, 1, pt_copied[1], EARLY)
                    if n < N:
                        tile, R, at = order[n]
                        for h in range(2):
                            t = st[n % 4][h]
                            act.wait_ge(max_ready, u * 2 * N + 2 * n + h + 1)
                            act.activation(prob[n % 2][h][0:R, 0:at + R], flat[0:R, 1536 * h:1536 * h + at + R], ACT.Exp,
                                           bias=t[0:R, 1:2], scale=SCALE, accum_out=t[0:R, 2:3]).then_inc(exp_done, 1)
                    if n >= 1:
                        copy_groups(act, i, par, n - 1, 1, pt_copied[1], LATE)
                        R = order[n - 1][1]
                        act.wait_ge(o_ready, u * N + n)
                        act.activation(oT[(n - 1) % 2][:, 0:R], ps[:, o_bank(n - 1), 0:R], ACT.Copy).then_inc(oT_copied, 1)

    @block.tensor
    def _(pe):
        def scores(i, par, n):
            u = i * 2 + par
            tile, R, at = order[n]
            L = at + R
            if n == 0:
                pe.wait_ge(loaded[par], (i + 1) * 64)
                pe.wait_ge(att_done, u * N + 1)
            for h in range(2):
                if n > 0:
                    pe.wait_ge(exp_done, u * 2 * N + 2 * (n - 1) + h + 1)
                for c in range(0, L, 512):
                    w = min(512, L - c)
                    ins = pe.matmul(ps[0:R, 3 * h + c // 512, 0:w], q[par][:, h, at:at + R], k[par][:, h, c:c + w],
                                    start=True, stop=True)
                ins.then_inc(scores_ready, 1)

        def turn(i, par, n, g):
            gg = par * G + first_group[n] + g
            pe.wait_ge(pt_copied[gg % 2], i * G + gg // 2 + 1)
            for b, blk in enumerate(groups[n][g]):
                lo, w = (0, META) if blk == 0 else (META + (blk - 1) * P, P)
                for h in range(2):
                    c = (b * 2 + h) * P
                    ins = pe.transpose(ps[0:w, 6 + gg % 2, c:c + P], prob[n % 2][h][:, lo:lo + w], ident[:, :])
            ins.then_inc(pt_ready, 1)

        def weigh(i, par, n, g):
            R = order[n][1]
            gg = par * G + first_group[n] + g
            pe.wait_ge(pt_copied[gg % 2], i * G + gg // 2 + 2)
            for b, blk in enumerate(groups[n][g]):
                w = META if blk == 0 else P
                for h in range(2):
                    ins = pe.matmul(ps[h * VD:(h + 1) * VD, o_bank(n), 0:R], v[par][0:w, blk, h * VD:(h + 1) * VD],
                                    pt[gg % 2][0:w, b, h, 0:R], start=(blk == 0), stop=(blk == groups[n][-1][-1]))
            if g == len(groups[n]) - 1:
                ins.then_inc(o_ready, 1)

        def turn_early(i, par, n):
            u = i * 2 + par
            pe.wait_ge(exp_done, u * 2 * N + 2 * n + 2)
            for g in EARLY[:len(groups[n])]:
                turn(i, par, n, g)

        def values(i, par, n):
            u = i * 2 + par
            if n >= 2:
                pe.wait_ge(att_done, u * N + n)
            for g in range(len(groups[n])):
                weigh(i, par, n, g)
                if g + 2 < len(groups[n]):
                    turn(i, par, n, g + 2)

        def back(i, par, n):
            u = i * 2 + par
            R = order[n][1]
            pe.wait_ge(oT_copied, u * N + n + 1)
            pe.transpose(ps[0:R, o_bank(n), P:2 * P], oT[n % 2][:, 0:R], ident[:, :]).then_inc(back_ready, 1)

        def pair(i, par):
            for n in range(N + 2):
                if 1 <= n <= N:
                    turn_early(i, par, n - 1)
                if n >= 2:
                    back(i, par, n - 2)
                if n < N:
                    scores(i, par, n)
                if 1 <= n <= N:
                    values(i, par, n - 1)

        pe.wait_ge(consts, 1)
        with pe.Fori(0, PAIRS // 2) as i:
            pair(i, 0)
            pair(i, 1)

    ctx.close()


def samples_block(nc, a, s, pages):
    ctx = ExitStack()
    sb = lambda name, shape, dt=F32: ctx.enter_context(nc.sbuf_tensor("s_b_" + name, shape, dt))
    sem = lambda name: ctx.enter_context(nc.semaphore("s_" + name))
    HP = 32
    BH = NS * SH

    ps = ctx.enter_context(nc.psum_tensor("s_ps", [P, 8, 512], F32))
    latn, lat_loaded, w_loaded, ids_loaded = pages.latn, pages.lat_loaded, pages.w_loaded, pages.ids_loaded
    wk, qn, qr = pages.wk, pages.qn, pages.qr
    latT = [sb(f"latT{i}", [P, 3, GP, P]) for i in range(2)]
    latT_hi = [sb(f"latT_hi{i}", [P, 2, GP, P], F32R) for i in range(2)]
    latT_lo = [sb(f"latT_lo{i}", [P, 2, GP, P], F32R) for i in range(2)]
    wk_hi = sb("wk_hi", [P, 2, H * NOPE], F32R)
    wk_lo = sb("wk_lo", [P, 2, H * NOPE], F32R)
    zero = sb("zero", [P, 1])
    wv = sb("wv", [P, 2, H * VD])
    wkT = sb("wkT", [NOPE, H, 2, P])
    qabs = sb("qabs", [P, 3, NS, HP])
    qab = [sb(f"qab{i}", [P, 3, HP]) for i in range(2)]
    ksq = [sb(f"ksq{i}", [P, H * NOPE]) for i in range(2)]
    krsq = sb("krsq", [P, NPG, ROPE])
    krs = sb("krs", [P, NPG])
    ssq = [sb(f"ssq{i}", [P, NPG, H]) for i in range(2)]
    rs = sb("rs", [P, NPG, H])
    sraw = [sb(f"sraw{i}", [P, NPG, H]) for i in range(2)]
    scs = [sb(f"scs{i}", [P, P]) for i in range(2)]
    mxp = sb("mxp", [P, H])
    mxa = sb("mxa", [P, H])
    waited = sb("waited", [P, 1])
    prob = sb("prob", [P, NPG, HP])
    lp = sb("lp", [P, H])
    ol = sb("ol", [P, KL])
    oLT = sb("oLT", [P, 2, H, NS])
    m_all = sb("m_all", [1, NS * H])
    l_all = sb("l_all", [1, NS * H])
    ident = sb("ident", [P, P])
    ones = sb("ones", [P, 1])
    sel = sb("sel", [P, H])
    mhalf = sb("mhalf", [P, 2])
    eps = sb("eps", [P, 2])
    q1, k1 = sb("q1", [NS, H, QK]), sb("k1", [NS, H, QK])
    gq, gk = sb("gq", [NS, QK]), sb("gk", [NS, QK])
    v1 = sb("v1", [NS, H * VD])
    mg = sb("mg", [NS, 10, H])
    M_, L_, SNEW, MT, A_, E_, LT, RL, AR, ER = range(10)
    oup = sb("oup", [NS, H * VD])
    h0 = sb("h0", [BH, SP_, SN])
    u0 = sb("u0", [BH, SP_, SN])
    xb, Bs, Cs = sb("xb", [BH, SP_]), sb("Bs", [BH, SN]), sb("Cs", [BH, SN])
    xd = sb("xd", [BH, SP_])
    sy = sb("sy", [BH, SP_])
    dt1, dta, dec, dsk = sb("dt1", [BH, 1]), sb("dta", [BH, 1]), sb("dec", [BH, 1]), sb("dsk", [BH, 1])
    yn, zn, yj = sb("yn", [NS, SW]), sb("zn", [NS, SW]), sb("yj", [NS, SW])
    ysm = sb("ysm", [NS, 4])

    ssd_loaded, new_loaded, y_stored, y_loaded = [sem(n) for n in "ssd_loaded new_loaded y_stored y_loaded".split()]
    ml_moved, stored = sem("ml_moved"), sem("stored")
    names = """consts wk_hi_done wk_lo_done hi_done lo_done ln_done wkT_ready wkT_copied qabs_ready qabs_copied qrope_copied qab_ready ta_ready tb_ready tc_ready ta_copied
    tb_copied tc_copied k_ready sq_done red_done sc_ready sc_copied scT_ready sraw_done krsq_done ssq_done rs_ready
    f2_done mxa_ready f3_done prob_ready lp_ready o_ready ol_copied oT_ready oT_copied up_ready up_copied
    new_prod new_sum merge_in merge_exp att_done
    dec_done xd_done u_done h1_done hc_done sy_done y_gated y_squared y_rstd y_normed m_saved""".split()
    S = {n: sem(n) for n in names}
    pool_steps, dve_steps = Steps(sem("pool_steps"), "samples pool"), Steps(sem("dve_steps"), "samples dve")
    N_W, N_SSD, N_NEW = 4, 1 + 1 + 8 + 2 + 8 + 1, 3 + 6
    block = ctx.enter_context(nc.Block())

    def out(ins, name):
        ins.then_inc(S[name], 1)

    def after(eng, name, n):
        if not (isinstance(n, int) and n <= 0):
            eng.wait_ge(S[name], n)

    @block.sync
    def _(sp):
        with sp.Fori(1, NS // 2) as i:
            for p in range(2):
                b = i * 2 + p
                sp.wait_ge(S["o_ready"], b)
                sp.wait_ge(ids_loaded, 16)
                pages.load(sp, b, p)
        sp.wait_ge(S["y_normed"], 1)
        sp.dma_start(s["ys"][T:TOK, :], yn[:, :]).then_inc(stored, 16)
        sp.wait_ge(S["m_saved"], NS)
        sp.wait_ge(S["ol_copied"], NS)
        sp.dma_start(mg[:, M_, :], m_all[0:1, :].rearrange("o (b h) -> o b h", b=NS)).then_inc(ml_moved, 16)
        sp.dma_start(mg[:, L_, :], l_all[0:1, :].rearrange("o (b h) -> o b h", b=NS)).then_inc(ml_moved, 16)
        sp.wait_ge(S["att_done"], 1)
        sp.dma_start(s["att"][SEQ:SEQ + NS, :], oup[:, :]).then_inc(stored, 16)
        sp.wait_ge(stored, 32)

    def group_of(b, g):
        return b * NG + g

    def following(b, g):
        return (b, g + 1) if g + 1 < NG else (b + 1, 0)

    @block.scalar
    def _(act):
        ukv = a["w_ukv"][0].rearrange("(c p) (h x) -> p c h x", p=P, x=NOPE + VD)
        act.dma_start(h0[:, :, :], a["state_ssm"][0].rearrange("b h p n -> (b h) p n")).then_inc(ssd_loaded, 16)
        act.dma_start(xb[:, :], s["s_x"].rearrange("b (h p) -> (b h) p", p=SP_)).then_inc(ssd_loaded, 16)
        for r in range(4):
            for dst, lo in ((Bs, 0), (Cs, P)):
                act.dma_start(dst[r:BH:4, :], s["s_bc"][:, lo:lo + P].rearrange("b (g n) -> b g n", n=SN)).then_inc(ssd_loaded, 16)
        act.dma_start(dt1[:, :], s["s_dt"].rearrange("b h -> (b h)").unsqueeze(1)).then_inc(ssd_loaded, 16)
        act.dma_start(dta[:, :], s["s_dta"].rearrange("b h -> (b h)").unsqueeze(1)).then_inc(ssd_loaded, 16)
        for b in range(NS):
            act.dma_start(dsk[b * SH:(b + 1) * SH, :], a["d_skip"].rearrange("o h -> h o")).then_inc(ssd_loaded, 16)
        act.dma_start(zn[:, :], s["s_z"]).then_inc(ssd_loaded, 16)
        act.wait_ge(w_loaded, 16 * N_W)
        out(act.activation(wk_hi[:, :, :], wk[:, :, :], ACT.Copy), "wk_hi_done")
        for j in range(4):
            act.wait_ge(S["wkT_ready"], j + 1)
            out(act.activation(wkT[:, 2 * j:2 * j + 2, :, :].rearrange("p h c l -> p (h c l)"), ps[0:NOPE, j, :], ACT.Copy), "wkT_copied")
        act.wait_ge(S["consts"], 1)
        out(act.activation(qabs[0:ROPE, 2, :, 0:H], qr[:, :, :].rearrange("p h b -> p b h"), ACT.Copy), "qrope_copied")

        def copy_turned(b, g):
            act.wait_ge(S["ta_ready"], group_of(b, g) + 1)
            out(act.activation(latT[g % 2][:, 0:2, 0:2, :], ps[:, 0, :].rearrange("p (c j t) -> p c j t", c=2, t=P), ACT.Copy),
                "ta_copied")

        def slot(b, p, g, ahead, behind):
            gg = group_of(b, g)
            if ahead:
                copy_turned(*following(b, g))
            for j in range(GP):
                n = gg * GP + j
                act.wait_ge(S["k_ready"], n + 1)
                if not (isinstance(b, int) and b == 0 and g == 0 and j < 2):
                    act.wait_ge(S["red_done"], n - 1)
                out(act.activation(ksq[j % 2][:, :], ps[:, 3 + j % 2, :], ACT.Square, scale=QK ** -0.5), "sq_done")
            act.wait_ge(S["sc_ready"], gg + 1)
            out(act.activation(scs[g % 2][:, :], ps[:, 5, 0:P], ACT.Copy), "sc_copied")
            if behind and g == 0:
                rstd(b - 1, 1 - p)
            if behind and g == 2:
                act.wait_ge(S["f3_done"], b)
                act.wait_ge(S["o_ready"], b)
                out(act.activation(prob[:, :, 0:H], sraw[1 - p][:, :, :], ACT.Exp, scale=SCALE), "prob_ready")
            if behind and g == 4:
                save_ol(b - 1)

        def rstd(b, p):
            act.wait_ge(S["ssq_done"], b + 1)
            out(act.activation(rs[:, :, :], ssq[p][:, :, :], ACT.Ln), "ln_done")
            act.wait_ge(S["ln_done"], b + 1)
            out(act.activation(rs[:, :, :], rs[:, :, :], ACT.Exp, scale=-0.5), "rs_ready")

        def save_ol(b):
            act.wait_ge(S["o_ready"], b + 2)
            act.wait_ge(S["oT_ready"], b + 1)
            act.activation(ol[:, :], ps[:, 7, 0:KL], ACT.Copy)
            out(act.activation(l_all[:, ds(b * H, H)], ps[0:1, 7, KL:KL + H], ACT.Copy), "ol_copied")

        copy_turned(0, 0)
        for g in range(NG):
            slot(0, 0, g, True, False)
            if g == 1:
                act.wait_ge(ssd_loaded, 16 * N_SSD)
                out(act.activation(dec[:, :], dta[:, :], ACT.Exp), "dec_done")
        act.dma_start(wv[:, 0, :].rearrange("p (h x) -> p h x", x=VD), ukv[:, 0, :, NOPE:]).then_inc(new_loaded, 16)
        act.dma_start(wv[:, 1, :].rearrange("p (h x) -> p h x", x=VD), ukv[:, 1, :, NOPE:]).then_inc(new_loaded, 16)
        act.dma_start(q1[:, :, :], s["s_q"]).then_inc(new_loaded, 16)
        act.dma_start(k1[:, :, :], s["s_k"]).then_inc(new_loaded, 16)
        act.dma_start(v1[:, :], s["v"][T:TOK, :]).then_inc(new_loaded, 16)
        for dst, n in ((gq, "q"), (gk, "k")):
            act.dma_start(dst[:, 0:NOPE], a[n + "_head_g_nope"].to_broadcast([NS, NOPE])).then_inc(new_loaded, 16)
            for j in range(2):
                act.dma_start(dst[:, NOPE + j * HALF:NOPE + (j + 1) * HALF],
                              a[n + "_head_g_rope"].to_broadcast([NS, HALF])).then_inc(new_loaded, 16)
        with act.Fori(0, 3) as i:
            for p, b in ((1, i * 2 + 1), (0, i * 2 + 2)):
                for g in range(NG):
                    slot(b, p, g, True, True)
        for g in range(NG):
            slot(NS - 1, 1, g, g + 1 < NG, True)
            if g == 3:
                act.wait_ge(S["y_gated"], 1)
                for gr in range(SG):
                    w = SW // SG
                    ins = act.activation(yj[:, gr * w:(gr + 1) * w], yn[:, gr * w:(gr + 1) * w], ACT.Square,
                                         scale=w ** -0.5, accum_out=ysm[:, gr:gr + 1])
                out(ins, "y_squared")
        rstd(NS - 1, 1)
        act.wait_ge(S["f3_done"], NS)
        act.wait_ge(S["o_ready"], NS)
        out(act.activation(prob[:, :, 0:H], sraw[1][:, :, :], ACT.Exp, scale=SCALE), "prob_ready")
        save_ol(NS - 1)
        act.wait_ge(S["merge_in"], 1)
        out(act.activation(mg[:, A_:E_ + 1, :], mg[:, A_:E_ + 1, :], ACT.Exp, scale=SCALE), "merge_exp")

    @block.gpsimd
    def _(pool):
        pool_steps(pool, pool.memset(ident[:, :], 0.0))
        pool.affine_select(out=ident[:, :], in_=ident[:, :], compare_op=ALU.not_equal, fill=1.0,
                           base=0, pattern=[[-1, P]], channel_multiplier=1)
        pool_steps(pool, pool.memset(sel[:, :], 0.0))
        for j in range(4):
            pool_steps(pool, pool.affine_select(out=sel[:, :], in_=sel[:, :], compare_op=ALU.not_equal, fill=1.0,
                                                base=-HP * j, pattern=[[-1, H]], channel_multiplier=1))
        pool.memset(ones[:, :], 1.0).then_inc(S["o_ready"], 1)
        pool.memset(mhalf[:, :], -0.5).then_inc(S["oT_ready"], 1)
        pool.memset(eps[:, :], EPS).then_inc(S["oT_copied"], 1)
        pool.memset(qabs[:, :, :, :], 0.0)
        pool.memset(prob[:, :, :], 0.0)
        pool.memset(latT[0][:, 2, :, :], 0.0)
        pool.memset(zero[:, :], 0.0)
        out(pool.memset(latT[1][:, 2, :, :], 0.0), "consts")

        def rope_squares(b, p):
            for g in range(NG):
                pool.wait_ge(lat_loaded[p][g], (b - p + 2) * (GP * 16))
            after(pool, "ssq_done", b)
            out(pool.tensor_tensor(out=krsq[:, :, :], in0=latn[p][:, :, KL:LATW], in1=latn[p][:, :, KL:LATW],
                                   op=ALU.mult), "krsq_done")

        def maxima(b):
            pool.wait_ge(S["f2_done"], b + 1)
            pool.tensor_tensor(out=waited[:, :], in0=eps[:, 0:1], in1=eps[:, 0:1], op=ALU.mult)
            out(pool.partition_all_reduce(mxa[:, :], mxp[:, :], P, RMAX), "mxa_ready")

        def split(b, g):
            gg = group_of(b, g)
            flat = lambda t: t[g % 2][:, 0:2, :, :].rearrange("p c j t -> p (c j t)")
            pool.wait_ge(S["ta_copied"], gg + 1)
            pool.wait_ge(S["tb_copied"], gg + 1)
            out(pool.tensor_tensor(out=flat(latT_hi), in0=flat(latT), in1=zero[:, :].to_broadcast([P, 2 * GP * P]),
                                   op=ALU.add), "hi_done")
            pool.wait_ge(S["hi_done"], gg + 1)
            out(pool.tensor_tensor(out=flat(latT_lo), in0=flat(latT), in1=flat(latT_hi).bitcast(F32), op=ALU.subtract),
                "lo_done")

        def slot(b, p, g, ahead, behind):
            if ahead:
                split(*following(b, g))
            if behind and g == 1:
                maxima(b - 1)
            if g == NG - 1:
                rope_squares(b, p)

        pool.wait_ge(S["wk_hi_done"], 1)
        out(pool.tensor_tensor(out=wk_lo[:, :, :], in0=wk[:, :, :], in1=wk_hi[:, :, :].bitcast(F32), op=ALU.subtract),
            "wk_lo_done")
        split(0, 0)
        for g in range(NG):
            slot(0, 0, g, True, False)
            if g == 2:
                pool.wait_ge(ssd_loaded, 16 * N_SSD)
                pool_steps(pool, pool.tensor_tensor(out=xd[:, :], in0=xb[:, :], in1=dt1[:, :].to_broadcast([BH, SP_]),
                                                    op=ALU.mult))
                out(pool.tensor_tensor(out=u0[:, :, :], in0=bc(xd[:, :], SN, 2), in1=bc(Bs[:, :], SP_, 1), op=ALU.mult),
                    "u_done")
            if g == 5:
                pool.wait_ge(S["h1_done"], 1)
                out(pool.tensor_tensor(out=u0[:, :, :], in0=h0[:, :, :], in1=bc(Cs[:, :], SP_, 1), op=ALU.mult), "hc_done")
        pool.dma_start(a["ssm_sample"][0].rearrange("b h p n -> (b h) p n"), h0[:, :, :]).then_inc(y_stored, 16)
        with pool.Fori(0, 3) as i:
            for p, b in ((1, i * 2 + 1), (0, i * 2 + 2)):
                for g in range(NG):
                    slot(b, p, g, True, True)
        pool.wait_ge(S["sy_done"], 1)
        pool.wait_ge(y_stored, 16)
        pool.dma_start(s["s_y"].rearrange("b (h p) -> (b h) p", p=SP_), sy[:, :]).then_inc(y_stored, 16)
        for g in range(NG):
            slot(NS - 1, 1, g, g + 1 < NG, True)
            if g == 0:
                pool.wait_ge(y_stored, 32)
                pool.dma_start(yn[:, :], s["s_y"]).then_inc(y_loaded, 16)
            if g == 3:
                pool.wait_ge(S["y_squared"], 1)
                pool_steps(pool, pool.tensor_tensor(out=ysm[:, 0:2], in0=ysm[:, 0:2], in1=eps[0:NS, 0:2], op=ALU.add))
                out(pool.tensor_tensor(out=ysm[:, 2:4], in0=ysm[:, 0:2], in1=mhalf[0:NS, 0:2], op=ALU.pow), "y_rstd")
        maxima(NS - 1)

    @block.vector
    def _(dve):
        def copy_turned(b, g):
            gg = group_of(b, g)
            dve.wait_ge(S["tb_ready"], gg + 1)
            out(dve.tensor_copy(latT[g % 2][:, 0:2, 2:4, :], ps[:, 1, :].rearrange("p (c j t) -> p c j t", c=2, t=P)),
                "tb_copied")
            dve.wait_ge(S["tc_ready"], gg + 1)
            out(dve.tensor_copy(latT[g % 2][0:ROPE, 2, :, :].rearrange("p j t -> p (j t)"), ps[0:ROPE, 2, :]), "tc_copied")

        def take_query(b, p):
            after(dve, "sc_ready", (b - 1) * NG)
            out(dve.tensor_scalar(qab[p][:, :, :], qabs[:, :, ds(b, 1), :].rearrange("p c o h -> p c (o h)"),
                                  1.0, None, ALU.mult), "qab_ready")

        def keep_scores(b, p, g):
            gg = group_of(b, g)
            dve.wait_ge(S["scT_ready"], gg + 1)
            out(dve.tensor_copy(sraw[p][:, GP * g:GP * (g + 1), :],
                                ps[:, 6, 0:P].rearrange("p (j h) -> p j h", h=HP)[:, :, 0:H]), "sraw_done")

        def finish(b, p, step):
            if step == 0:
                dve.wait_ge(S["krsq_done"], b + 1)
                dve_steps(dve, dve.tensor_reduce(krs[:, :], krsq[:, :, :], AXX, ALU.add))
                dve.wait_ge(S["red_done"], (b + 1) * NPG)
                dve_steps(dve, dve.scalar_tensor_tensor(out=ssq[p][:, :, :], in0=bc(krs[:, :], H, 2), scalar=1.0 / QK,
                                             in1=ssq[p][:, :, :], op0=ALU.mult, op1=ALU.add))
                out(dve.tensor_scalar(ssq[p][:, :, :], ssq[p][:, :, :], EPS, None, ALU.add), "ssq_done")
            if step == 1:
                dve.wait_ge(S["rs_ready"], b + 1)
                dve_steps(dve, dve.tensor_tensor(out=ssq[p][:, :, :], in0=ssq[p][:, :, :], in1=rs[:, :, :], op=ALU.mult))
                dve_steps(dve, dve.tensor_tensor(out=ssq[p][:, :, :], in0=ssq[p][:, :, :], in1=rs[:, :, :], op=ALU.mult))
                dve_steps(dve, dve.tensor_scalar(ssq[p][:, :, :], ssq[p][:, :, :], -0.5, 1.5, ALU.mult, ALU.add))
                dve_steps(dve, dve.tensor_tensor(out=rs[:, :, :], in0=ssq[p][:, :, :], in1=rs[:, :, :], op=ALU.mult))
                dve.wait_ge(S["sraw_done"], (b + 1) * NG)
                dve_steps(dve, dve.tensor_tensor(out=sraw[p][:, :, :], in0=sraw[p][:, :, :], in1=rs[:, :, :], op=ALU.mult))
                out(dve.tensor_reduce(mxp[:, :], sraw[p][:, :, :].rearrange("p n h -> p h n"), AXX, ALU.max), "f2_done")
            if step == 2:
                dve.wait_ge(S["mxa_ready"], b + 1)
                out(dve.tensor_tensor(out=sraw[p][:, :, :], in0=sraw[p][:, :, :], in1=bc(mxa[:, :], NPG, 1),
                                      op=ALU.subtract), "f3_done")
                out(dve.tensor_scalar(m_all[:, ds(b * H, H)], mxa[0:1, :], 1.0, None, ALU.mult), "m_saved")
            if step == 3:
                dve.wait_ge(S["prob_ready"], b + 1)
                out(dve.tensor_reduce(lp[:, :], prob[:, :, 0:H].rearrange("p n h -> p h n"), AXX, ALU.add), "lp_ready")

        def keep_output(b):
            dve.wait_ge(S["oT_ready"], b + 2)
            out(dve.tensor_scalar(oLT[:, :, :, ds(b, 1)].rearrange("p c h o -> p (c h o)"), ps[:, 7, 0:2 * H],
                                  1.0, None, ALU.mult), "oT_copied")

        def slot(b, p, g, ahead, behind):
            gg = group_of(b, g)
            if ahead:
                copy_turned(*following(b, g))
            if g == 0 and behind:
                keep_scores(b - 1, 1 - p, NG - 1)
            for j in range(GP):
                dve.wait_ge(S["sq_done"], gg * GP + j + 1)
                out(dve.tensor_reduce(ssq[p][:, GP * g + j, :], by_head(ksq[j % 2][:, :], NOPE), AXX, ALU.add), "red_done")
            if g > 0:
                keep_scores(b, p, g - 1)
            if behind:
                if g < 2:
                    finish(b - 1, 1 - p, g)
                if g == 2:
                    finish(b - 1, 1 - p, 2)
                if g == 3:
                    finish(b - 1, 1 - p, 3)
            if g == 6 and not (isinstance(b, int) and b == NS - 1):
                take_query(b + 1, 1 - p)

        dve.wait_ge(S["qabs_ready"], 1)
        out(dve.tensor_copy(qabs[:, 0:2, :, 0:H], ps[:, 4, 0:2 * H * NS].rearrange("p (c h b) -> p c b h", c=2, h=H)), "qabs_copied")
        dve.wait_ge(S["qabs_copied"], 1)
        dve.wait_ge(S["qrope_copied"], 1)
        take_query(0, 0)
        dve.wait_ge(S["consts"], 1)
        copy_turned(0, 0)
        for g in range(NG):
            slot(0, 0, g, True, False)
            if g == 4:
                dve.wait_ge(S["u_done"], 1)
                dve.wait_ge(S["dec_done"], 1)
                out(dve.scalar_tensor_tensor(out=h0[:, :, :], in0=h0[:, :, :], scalar=dec[:, 0:1], in1=u0[:, :, :],
                                             op0=ALU.mult, op1=ALU.add), "h1_done")
            if g == 7:
                dve.wait_ge(S["hc_done"], 1)
                dve_steps(dve, dve.tensor_reduce(sy[:, :], u0[:, :, :], AXX, ALU.add))
                out(dve.scalar_tensor_tensor(out=sy[:, :], in0=xb[:, :], scalar=dsk[:, 0:1], in1=sy[:, :],
                                             op0=ALU.mult, op1=ALU.add), "sy_done")
        with dve.Fori(0, 3) as i:
            dve_steps.begin(i, 14)
            for p, b in ((1, i * 2 + 1), (0, i * 2 + 2)):
                for g in range(NG):
                    slot(b, p, g, True, True)
                    if g == 5:
                        keep_output(b - 1)
            dve_steps.end(3)
        for g in range(NG):
            slot(NS - 1, 1, g, g + 1 < NG, True)
            if g == 5:
                keep_output(NS - 2)
            if g == 2:
                dve.wait_ge(y_loaded, 16)
                out(dve.tensor_tensor(out=yn[:, :], in0=yn[:, :], in1=zn[:, :], op=ALU.mult), "y_gated")
            if g == 5:
                dve.wait_ge(S["y_rstd"], 1)
                for gr in range(SG):
                    w = SW // SG
                    ins = dve.tensor_scalar(yn[:, gr * w:(gr + 1) * w], yn[:, gr * w:(gr + 1) * w],
                                            ysm[:, 2 + gr:3 + gr], None, ALU.mult)
                out(ins, "y_normed")
        keep_scores(NS - 1, 1, NG - 1)
        for step in range(4):
            finish(NS - 1, 1, step)
        dve.wait_ge(new_loaded, 16 * (N_NEW + 2))
        dve_steps(dve, dve.tensor_tensor(out=gq[:, :], in0=gq[:, :], in1=gk[:, :], op=ALU.mult))
        dve_steps(dve, dve.tensor_tensor(out=k1[:, :, :], in0=k1[:, :, :], in1=bc(gq[:, :], H, 1), op=ALU.mult))
        dve_steps(dve, dve.tensor_tensor(out=q1[:, :, :], in0=q1[:, :, :], in1=k1[:, :, :], op=ALU.mult))
        dve_steps(dve, dve.tensor_reduce(mg[:, SNEW, :], q1[:, :, :], AXX, ALU.add))
        keep_output(NS - 1)
        dve.wait_ge(ml_moved, 32)
        dve_steps(dve, dve.tensor_tensor(out=mg[:, MT, :], in0=mg[:, M_, :], in1=mg[:, SNEW, :], op=ALU.max))
        dve.tensor_tensor(out=mg[:, A_, :], in0=mg[:, M_, :], in1=mg[:, MT, :], op=ALU.subtract)
        out(dve.tensor_tensor(out=mg[:, E_, :], in0=mg[:, SNEW, :], in1=mg[:, MT, :], op=ALU.subtract), "merge_in")
        dve.wait_ge(S["merge_exp"], 1)
        dve_steps(dve, dve.tensor_tensor(out=mg[:, LT, :], in0=mg[:, L_, :], in1=mg[:, A_, :], op=ALU.mult))
        dve_steps(dve, dve.tensor_tensor(out=mg[:, LT, :], in0=mg[:, LT, :], in1=mg[:, E_, :], op=ALU.add))
        dve_steps(dve, dve.reciprocal(mg[:, RL, :], mg[:, LT, :]))
        dve.tensor_tensor(out=mg[:, AR, :], in0=mg[:, A_, :], in1=mg[:, RL, :], op=ALU.mult)
        dve_steps(dve, dve.tensor_tensor(out=mg[:, ER, :], in0=mg[:, E_, :], in1=mg[:, RL, :], op=ALU.mult))
        dve.tensor_tensor(out=by_head(v1[:, :], VD), in0=by_head(v1[:, :], VD), in1=bc(mg[:, ER, :], VD, 2), op=ALU.mult)
        dve.wait_ge(S["up_ready"], 1)
        dve_steps(dve, dve.tensor_tensor(out=by_head(oup[:, :], VD), in0=by_head(ps[0:NS, 0, :], VD),
                                         in1=bc(mg[:, AR, :], VD, 2), op=ALU.mult))
        out(dve.tensor_tensor(out=oup[:, :], in0=oup[:, :], in1=v1[:, :], op=ALU.add), "att_done")

    @block.tensor
    def _(pe):
        pe.wait_ge(S["consts"], 1)
        pe.wait_ge(w_loaded, 16 * N_W)
        for j in range(4):
            for n in range(4):
                h, c = 2 * j + n // 2, n % 2
                ins = pe.transpose(ps[0:NOPE, j, n * P:(n + 1) * P], wk[:, c, h * NOPE:(h + 1) * NOPE], ident[:, :])
            out(ins, "wkT_ready")
        pe.wait_ge(S["wkT_copied"], 4)
        for c in range(2):
            for h in range(H):
                at = (c * H + h) * NS
                ins = pe.matmul(ps[:, 4, at:at + NS], wkT[:, h, c, :], qn[:, h, :], start=True, stop=True)
        out(ins, "qabs_ready")

        def turn(b, p, g):
            gg = group_of(b, g)
            pe.wait_ge(lat_loaded[p][g], (b - p + 2) * (GP * 16))
            page = lambda j, lo, hi: latn[p][:, GP * g + j, lo:hi]
            for bank, name in ((0, "ta"), (1, "tb")):
                after(pe, name + "_copied", gg)
                for c in range(2):
                    for j in range(2):
                        at = (c * 2 + j) * P
                        ins = pe.transpose(ps[:, bank, at:at + P], page(2 * bank + j, c * P, (c + 1) * P), ident[:, :])
                out(ins, name + "_ready")
            after(pe, "tc_copied", gg)
            for j in range(GP):
                ins = pe.transpose(ps[0:ROPE, 2, j * P:(j + 1) * P], page(j, KL, LATW), ident[:, :])
            out(ins, "tc_ready")

        def scores_back(b, g):
            gg = group_of(b, g)
            pe.wait_ge(S["sc_copied"], gg + 1)
            after(pe, "sraw_done", gg)
            out(pe.transpose(ps[:, 6, 0:P], scs[g % 2][:, :], ident[:, :]), "scT_ready")

        def weigh(b, p):
            pe.wait_ge(S["lp_ready"], b + 1)
            pe.wait_ge(S["oT_copied"], b + 1)
            for pg in range(NPG):
                j = pg % 4
                pe.matmul(ps[HP * j:HP * (j + 1), 7, 0:KL], prob[:, pg, :], latn[p][:, pg, 0:KL],
                          start=(pg < 4), stop=(pg >= NPG - 4))
            out(pe.matmul(ps[0:1, 7, KL:KL + H], ones[:, :], lp[:, :], start=True, stop=True), "o_ready")

        def gather_output(b):
            pe.wait_ge(S["ol_copied"], b + 1)
            for c in range(2):
                ins = pe.matmul(ps[:, 7, c * H:(c + 1) * H], ol[:, c * P:(c + 1) * P], sel[:, :], start=True, stop=True)
            out(ins, "oT_ready")

        def slot(b, p, g, ahead, behind):
            gg = group_of(b, g)
            if ahead:
                nb, ng = following(b, g)
                turn(nb, p if ng else 1 - p, ng)
            pe.wait_ge(S["lo_done"], gg + 1)
            for j in range(GP):
                n = gg * GP + j
                if not (isinstance(b, int) and b == 0 and g == 0 and j < 2):
                    pe.wait_ge(S["sq_done"], n - 1)
                for c in range(2):
                    for l, w in ((latT_hi, wk_hi), (latT_hi, wk_lo), (latT_lo, wk_hi)):
                        ins = pe.matmul(ps[:, 3 + j % 2, :], l[g % 2][:, c, j, :], w[:, c, :],
                                        start=(c == 0 and l is latT_hi and w is wk_hi), stop=(c == 1 and l is latT_lo))
                out(ins, "k_ready")
            pe.wait_ge(S["tc_copied"], gg + 1)
            after(pe, "sc_copied", gg)
            if g == 0:
                pe.wait_ge(S["qab_ready"], b + 1)
            for c in range(3):
                for j in range(GP):
                    ins = pe.matmul(ps[HP * j:HP * (j + 1), 5, 0:P], qab[p][:, c, :], latT[g % 2][:, c, j, :],
                                    start=(c == 0), stop=(c == 2))
            out(ins, "sc_ready")
            if g == 0 and behind:
                scores_back(b - 1, NG - 1)
            if g > 0:
                scores_back(b, g - 1)
            if behind and g == 4:
                weigh(b - 1, 1 - p)
            if behind and g == 5:
                gather_output(b - 1)

        pe.wait_ge(S["qabs_copied"], 1)
        pe.wait_ge(S["wk_lo_done"], 1)
        turn(0, 0, 0)
        for g in range(NG):
            slot(0, 0, g, True, False)
        with pe.Fori(0, 3) as i:
            for p, b in ((1, i * 2 + 1), (0, i * 2 + 2)):
                for g in range(NG):
                    slot(b, p, g, True, True)
        for g in range(NG):
            slot(NS - 1, 1, g, g + 1 < NG, True)
        scores_back(NS - 1, NG - 1)
        weigh(NS - 1, 1)
        gather_output(NS - 1)
        pe.wait_ge(new_loaded, 16 * (N_NEW + 2))
        pe.wait_ge(S["oT_copied"], NS + 1)
        for h in range(H):
            for c in range(2):
                ins = pe.matmul(ps[0:NS, 0, h * VD:(h + 1) * VD], oLT[:, c, h, :], wv[:, c, h * VD:(h + 1) * VD],
                                start=(c == 0), stop=(c == 1))
        out(ins, "up_ready")

    ctx.close()


def mixing_block(nc, a, s, h, nT_hi, nT_lo):
    ctx = ExitStack()
    sb = lambda name, shape, dt=F32: ctx.enter_context(nc.sbuf_tensor("m_" + name, shape, dt))
    sem = lambda name: ctx.enter_context(nc.semaphore("m_" + name))
    ps = ctx.enter_context(nc.psum_tensor("m_ps", [P, 8, 512], F32))
    AW = H * VD
    KM = (SW + AW) // P
    wo_hi = sb("wo_hi", [P, KM, D], F32R)
    wo_lo = sb("wo_lo", [P, KM, D], F32R)
    mix_g = sb("mix_g", [P, KM])
    ffn_g = sb("ffn_g", [P, KD])
    ident = sb("ident", [P, P])
    mhalf = sb("mhalf", [P, 1])
    eps = sb("eps", [P, 1])
    idle = sb("idle", [P, 1])
    junk = sb("junk", [P, AW])
    ys = [sb(f"ys{i}", [P, SW]) for i in range(2)]
    at = [sb(f"at{i}", [P, AW]) for i in range(2)]
    mv = [sb(f"mv{i}", [P, KM // 2, P]) for i in range(2)]
    mix_hi = [sb(f"mix_hi{i}", [P, KM, P], F32R) for i in range(2)]
    mix_lo = [sb(f"mix_lo{i}", [P, KM, P], F32R) for i in range(2)]
    n = [sb(f"n{i}", [P, D]) for i in range(2)]
    nv = [sb(f"nv{i}", [P, KD // 2, P]) for i in range(2)]
    st = [sb(f"st{i}", [P, 2]) for i in range(2)]
    st_at = [sb(f"st_at{i}", [P, 2]) for i in range(2)]

    w_loaded = [sem(f"w_loaded{i}") for i in range(2)]
    mix_loaded = [sem(f"mix_loaded{i}") for i in range(2)]
    x_loaded = [sem(f"x_loaded{i}") for i in range(2)]
    gains_loaded = sem("gains_loaded")
    names = """consts w_hi w_lo at_squared at_rstd at_normed ysT_ready atT_ready mv0_ready mv1_ready mix_hi_done mix_lo_done
    o_ready h_done h_squared h_rstd n_ready nTa_ready nTb_ready nTa_copied nTb_copied""".split()
    S = {x: sem(x) for x in names}
    pool_steps, dve_steps = Steps(sem("pool_steps"), "mixing pool"), Steps(sem("dve_steps"), "mixing dve")
    block = ctx.enter_context(nc.Block())

    def out(ins, name):
        ins.then_inc(S[name], 1)

    def known(t):
        return isinstance(t, int)

    def after(eng, name, count):
        if not (known(count) and count <= 0):
            eng.wait_ge(S[name], count)

    def rows(t):
        return NS if known(t) and t == 0 else P

    def loaded(t, p):
        return (t - p + 2) * 16

    @block.sync
    def _(sp):
        def load_mix(t, p):
            R = rows(t)
            row = T if known(t) and t == 0 else sp.snap((t - 1) * P + META)
            att_row = SEQ if known(t) and t == 0 else sp.snap((t - 1) * P)
            if not (known(t) and t < 2):
                sp.wait_ge(S["atT_ready"], t - 1)
                sp.wait_ge(S["consts"], 1)
            sp.dma_start(ys[p][0:R, :], s["ys"][ds(row, R), :]).then_inc(mix_loaded[p], 16)
            sp.dma_start(at[p][0:R, :], s["att"][ds(att_row, R), :]).then_inc(mix_loaded[p], 16)

        load_mix(0, 0)
        for k in range(KM):
            if k >= 2:
                sp.wait_ge(S["w_lo"], k - 1)
            sp.dma_start(n[k % 2][:, :], a["w_out"][0, k * P:(k + 1) * P, :]).then_inc(w_loaded[k % 2], 16)
            if k == 1:
                load_mix(1, 1)
                sp.dma_start(h[0:NS, 0, :], a["x_sample"].rearrange("b s d -> (b s) d")).then_inc(x_loaded[0], 16)
        sp.dma_start(h[:, 1:NT + 1, :], a["x_prompt"][0].rearrange("(t p) d -> p t d", p=P)).then_inc(x_loaded[1], 16)
        load_mix(2, 0)
        with sp.Fori(1, NT // 2) as i:
            load_mix(i * 2 + 1, 1)
            load_mix(i * 2 + 2, 0)

    @block.gpsimd
    def _(pool):
        pool_steps(pool, pool.memset(ident[:, :], 0.0))
        pool.affine_select(out=ident[:, :], in_=ident[:, :], compare_op=ALU.not_equal, fill=1.0,
                           base=0, pattern=[[-1, P]], channel_multiplier=1)
        pool.memset(mhalf[:, :], -0.5).then_inc(S["nTb_ready"], 1)
        pool_steps(pool, pool.memset(eps[:, :], EPS))
        out(pool.memset(nv[0][:, 0, 0:1], 0.0), "consts")

        def rstd(buf, R):
            pool_steps(pool, pool.tensor_tensor(out=buf[0:R, 0:1], in0=buf[0:R, 0:1], in1=eps[0:R, :], op=ALU.add))
            return pool.tensor_tensor(out=buf[0:R, 1:2], in0=buf[0:R, 0:1], in1=mhalf[0:R, :], op=ALU.pow)

        def att_rstd(t, p):
            pool.wait_ge(S["at_squared"], t + 1)
            out(rstd(st_at[p], rows(t)), "at_rstd")

        def low_parts(t, p):
            R = rows(t)
            for j in range(2):
                pool.wait_ge(S["mix_hi_done"], t * 2 + j + 1)
                out(pool.tensor_tensor(out=mix_lo[p][:, 4 * j:4 * j + 4, 0:R], in0=mv[j][:, :, 0:R],
                                       in1=mix_hi[p][:, 4 * j:4 * j + 4, 0:R].bitcast(F32), op=ALU.subtract), "mix_lo_done")

        def slot(t, p):
            if not (known(t) and t == NT):
                low_parts(t + 1, 1 - p)
            if not (known(t) and t >= NT - 1):
                att_rstd(t + 2, p)
            pool.wait_ge(S["h_squared"], t + 1)
            out(rstd(st[p], rows(t)), "h_rstd")

        att_rstd(0, 0)
        for k in range(KM):
            pool.wait_ge(S["w_hi"], k + 1)
            out(pool.tensor_tensor(out=wo_lo[:, k, :], in0=n[k % 2][:, :], in1=wo_hi[:, k, :].bitcast(F32),
                                   op=ALU.subtract), "w_lo")
            if k == 1:
                low_parts(0, 0)
                att_rstd(1, 1)
        slot(0, 0)
        slot(1, 1)
        with pool.Fori(1, NT // 2 - 1) as i:
            pool_steps.begin(i, 4, first=1)
            slot(i * 2, 0)
            slot(i * 2 + 1, 1)
            pool_steps.end(NT // 2 - 2)
        slot(NT - 2, 0)
        slot(NT - 1, 1)
        slot(NT, 0)

    @block.scalar
    def _(act):
        for k in range(KM):
            src = a["ssd_norm_g"] if k < KM // 2 else a["mla_out_g"]
            c = k % (KM // 2) * P
            act.dma_start(mix_g[:, k:k + 1], src[0, c:c + P].unsqueeze(1)).then_inc(gains_loaded, 16)
        act.dma_start(ffn_g[:, :], a["ffn_norm_g"][0].rearrange("(k p) -> p k", p=P)).then_inc(gains_loaded, 16)

        def att_square(t, p):
            R = rows(t)
            after(act, "at_squared", t)
            act.wait_ge(mix_loaded[p], loaded(t, p))
            out(act.activation(junk[0:R, :], at[p][0:R, :], ACT.Square, scale=AW ** -0.5,
                               accum_out=st_at[p][0:R, 0:1]), "at_squared")

        def high_parts(t, p):
            R = rows(t)
            for j in range(2):
                act.wait_ge(S[f"mv{j}_ready"], t + 1)
                out(act.activation(mix_hi[p][:, 4 * j:4 * j + 4, 0:R], mv[j][:, :, 0:R], ACT.Copy), "mix_hi_done")

        def slot(t, p):
            R = rows(t)
            if not (known(t) and t == NT):
                high_parts(t + 1, 1 - p)
            if not (known(t) and t >= NT - 1):
                att_square(t + 2, p)
            after(act, "nTb_ready", t)
            act.wait_ge(S["h_done"], t + 1)
            if known(t):
                src = h[0:R, t, :]
            else:
                act.activation(idle[:, :], eps[:, :], ACT.Copy)
                src = h[:, ds(t, 1), :].rearrange("p o d -> p (o d)")
            out(act.activation(n[p][0:R, :], src, ACT.Square, scale=D ** -0.5, accum_out=st[p][0:R, 0:1]), "h_squared")

        att_square(0, 0)
        for k in range(KM):
            act.wait_ge(w_loaded[k % 2], (k // 2 + 1) * 16)
            out(act.activation(wo_hi[:, k, :], n[k % 2][:, :], ACT.Copy), "w_hi")
            if k == 1:
                high_parts(0, 0)
                att_square(1, 1)
        act.wait_ge(S["w_lo"], KM)
        act.wait_ge(S["consts"], 1)
        slot(0, 0)
        slot(1, 1)
        with act.Fori(1, NT // 2 - 1) as i:
            slot(i * 2, 0)
            slot(i * 2 + 1, 1)
        slot(NT - 2, 0)
        slot(NT - 1, 1)
        slot(NT, 0)

    @block.vector
    def _(dve):
        def scale_att(t, p):
            R = rows(t)
            dve.wait_ge(S["at_rstd"], t + 1)
            out(dve.tensor_scalar(at[p][0:R, :], at[p][0:R, :], st_at[p][0:R, 1:2], None, ALU.mult), "at_normed")

        def keep_mix(t, p):
            R = rows(t)
            after(dve, "o_ready", t - 1)
            for j, name in enumerate(("ysT", "atT")):
                dve.wait_ge(S[name + "_ready"], t + 1)
                if not (known(t) and t == 0):
                    dve.wait_ge(S["mix_lo_done"], t * 2 + j - 1)
                out(dve.tensor_tensor(out=mv[j][:, :, 0:R], in0=ps[:, j, :].rearrange("p (k r) -> p k r", k=4)[:, :, 0:R],
                                      in1=bc(mix_g[:, 4 * j:4 * j + 4], R, 2), op=ALU.mult), f"mv{j}_ready")

        def residual(t, p):
            R = rows(t)
            if known(t) and t < 2:
                dve.wait_ge(x_loaded[t], 16)
            dve.wait_ge(S["o_ready"], t + 1)
            rows_ = h[0:R, ds(t, 1), :].rearrange("p o (c n) -> p (o c) n", c=2)
            out(dve.tensor_tensor(out=rows_, in0=ps[0:R, 2 + 2 * p:4 + 2 * p, :], in1=rows_, op=ALU.add), "h_done")

        def normed(t, p):
            R = rows(t)
            dve.wait_ge(S["h_rstd"], t + 1)
            out(dve.tensor_scalar(n[p][0:R, :], h[0:R, ds(t, 1), :].rearrange("p o d -> p (o d)"), st[p][0:R, 1:2], None,
                                  ALU.mult), "n_ready")

        def keep_norms(t, p):
            R, col = (NS, SEQ) if known(t) and t == 0 else (P, (t - 1) * P)
            for j, name in enumerate(("nTa", "nTb")):
                dve.wait_ge(S[name + "_ready"], t + 1 + j)
                out(dve.tensor_tensor(out=nv[j][:, :, 0:R], in0=ps[:, 6 + j, :].rearrange("p (k r) -> p k r", k=4)[:, :, 0:R],
                                      in1=bc(ffn_g[:, 4 * j:4 * j + 4], R, 2), op=ALU.mult), name + "_copied")
            dve.wait_ge(S["nTb_copied"], t + 1)
            for j in range(2):
                ins = dve.tensor_scalar(nT_hi[:, 4 * j:4 * j + 4, ds(col, R)], nv[j][:, :, 0:R], 1.0, None, ALU.mult)
            dve_steps(dve, ins)
            for j in range(2):
                dve.tensor_tensor(out=nT_lo[:, 4 * j:4 * j + 4, ds(col, R)], in0=nv[j][:, :, 0:R],
                                  in1=nT_hi[:, 4 * j:4 * j + 4, ds(col, R)].bitcast(F32), op=ALU.subtract)

        def slot(t, p):
            first, last = known(t) and t == 0, known(t) and t == NT
            if not first:
                normed(t - 1, 1 - p)
            if not last:
                scale_att(t + 1, 1 - p)
                keep_mix(t + 1, 1 - p)
            if not first:
                keep_norms(t - 1, 1 - p)
            residual(t, p)

        scale_att(0, 0)
        dve.wait_ge(gains_loaded, 16 * (KM + 1))
        keep_mix(0, 0)
        slot(0, 0)
        slot(1, 1)
        with dve.Fori(1, NT // 2) as i:
            dve_steps.begin(i, 2, first=1)
            slot(i * 2, 0)
            slot(i * 2 + 1, 1)
            dve_steps.end(NT // 2 - 1)
        slot(NT, 0)
        normed(NT, 0)
        keep_norms(NT, 0)

    @block.tensor
    def _(pe):
        def turn_mix(t, p):
            R = rows(t)
            pe.wait_ge(mix_loaded[p], loaded(t, p))
            after(pe, "mv0_ready", t)
            for k in range(4):
                ins = pe.transpose(ps[:, 0, k * P:k * P + R], ys[p][0:R, k * P:(k + 1) * P], ident[0:R, 0:R])
            out(ins, "ysT_ready")
            pe.wait_ge(S["at_normed"], t + 1)
            after(pe, "mv1_ready", t)
            for k in range(4):
                ins = pe.transpose(ps[:, 1, k * P:k * P + R], at[p][0:R, k * P:(k + 1) * P], ident[0:R, 0:R])
            out(ins, "atT_ready")

        def turn_norms(t, p):
            R = rows(t)
            pe.wait_ge(S["n_ready"], t + 1)
            for j, name in enumerate(("nTa", "nTb")):
                after(pe, name + "_copied", t)
                for k in range(4):
                    ins = pe.transpose(ps[:, 6 + j, k * P:k * P + R], n[p][0:R, (4 * j + k) * P:(4 * j + k + 1) * P],
                                       ident[0:R, 0:R])
                out(ins, name + "_ready")

        def project(t, p):
            R = rows(t)
            pe.wait_ge(S["mix_lo_done"], t * 2 + 2)
            after(pe, "h_done", t - 1)
            for k in range(KM):
                if k == 2:
                    if not (known(t) and t == NT):
                        turn_mix(t + 1, 1 - p)
                    if not (known(t) and t == 0):
                        turn_norms(t - 1, 1 - p)
                if known(t) and t == 0:
                    pe.wait_ge(S["w_lo"], k + 1)
                for c in range(2):
                    cols = slice(c * 512, (c + 1) * 512)
                    for m, w in ((mix_hi, wo_hi), (mix_hi, wo_lo), (mix_lo, wo_hi)):
                        ins = pe.matmul(ps[0:R, 2 + 2 * p + c, :], m[p][:, k, 0:R], w[:, k, cols],
                                        start=(k == 0 and w is wo_hi and m is mix_hi),
                                        stop=(k == KM - 1 and m is mix_lo))
            out(ins, "o_ready")

        pe.wait_ge(S["consts"], 1)
        turn_mix(0, 0)
        project(0, 0)
        project(1, 1)
        with pe.Fori(1, NT // 2) as i:
            project(i * 2, 0)
            project(i * 2 + 1, 1)
        project(NT, 0)
        turn_norms(NT, 0)

    ctx.close()


def ffn_block(nc, a, h, nT_hi, nT_lo):
    ctx = ExitStack()
    sb = lambda name, shape, dt=F32: ctx.enter_context(nc.sbuf_tensor("f_" + name, shape, dt))
    sem = lambda name: ctx.enter_context(nc.semaphore("f_" + name))
    KF = FF // P
    PARTS = KF // 2
    COLS = SEQ + NS
    NC = 3
    W = COLS // NC
    TILES = NT + 1
    ps = ctx.enter_context(nc.psum_tensor("f_ps", [P, 8, 512], F32))
    start = sb("start", [P, 2])
    gu_raw = sb("gu_raw", [P, 2, KD, P])
    gu_hi = [sb(f"gu_hi{i}", [P, 2, KD, P], F32R) for i in range(2)]
    gu_lo = [sb(f"gu_lo{i}", [P, 2, KD, P], F32R) for i in range(2)]
    wd_raw = sb("wd_raw", [P, 2, D])
    wd_hi = sb("wd_hi", [P, 2, D], F32R)
    wd_lo = sb("wd_lo", [P, 2, D], F32R)
    e = [sb(f"e{i}", [P, W]) for i in range(NC)]
    hid_hi = [sb(f"hid_hi{i}", [P, 2, COLS], F32R) for i in range(2)]
    hid_lo = [sb(f"hid_lo{i}", [P, 2, COLS], F32R) for i in range(2)]

    gu_loaded, wd_loaded, y_stored = sem("gu_loaded"), sem("wd_loaded"), sem("y_stored")
    names = """gu_hi_done gu_lo_done wd_hi_done wd_lo_done gate_ready up_ready exp_done v_ready hid_hi_done hid_lo_done
    down_ready h_added""".split()
    S = {x: sem(x) for x in names}
    dve_steps = Steps(sem("dve_steps"), "ffn dve")
    block = ctx.enter_context(nc.Block())

    def out(ins, name):
        ins.then_inc(S[name], 1)

    def known(t):
        return isinstance(t, int)

    def parts_in_loop(eng, part, end, steps=None, per=0):
        part(0, 0)
        with eng.Fori(0, (end - 1) // 2) as i:
            if steps:
                steps.begin(i, per)
            part(i * 2 + 1, 1)
            part(i * 2 + 2, 0)
            if steps:
                steps.end((end - 1) // 2)

    @block.sync
    def _(sp):
        def load_up(f):
            col = f * P if known(f) else sp.snap(f * P)
            if not (known(f) and f == 0):
                sp.wait_ge(S["gu_lo_done"], f)
                sp.wait_ge(wd_loaded, 16)
            for j, w in enumerate(("w_gate", "w_up")):
                sp.dma_start(gu_raw[:, j, :, :], a[w][0, :, ds(col, P)].rearrange("(k p) c -> p k c", p=P)).then_inc(gu_loaded, 16)

        def load_down(i):
            row = i * 2 * P if known(i) else sp.snap(i * 2 * P)
            if not (known(i) and i == 0):
                sp.wait_ge(S["wd_lo_done"], i)
                sp.wait_ge(wd_loaded, 16)
            sp.dma_start(wd_raw[:, :, :], a["w_down"][0, ds(row, 2 * P), :].rearrange("(j p) d -> p j d", p=P)).then_inc(wd_loaded, 16)

        load_up(0)
        load_down(0)
        load_up(1)
        with sp.Fori(1, PARTS) as i:
            load_up(i * 2)
            load_down(i)
            load_up(i * 2 + 1)
        for t in range(TILES):
            sp.wait_ge(S["h_added"], (PARTS - 1) * TILES + t + 3)
            if t == 0:
                sp.dma_start(a["y_sample"][:, 0, :], h[0:NS, 0, :]).then_inc(y_stored, 16)
            else:
                sp.dma_start(a["y_prompt"][0, (t - 1) * P:t * P, :], h[:, t, :]).then_inc(y_stored, 16)
        sp.wait_ge(y_stored, 16 * TILES)

    @block.gpsimd
    def _(pool):
        def low_up(f, p):
            pool.wait_ge(S["gu_hi_done"], f + 1)
            out(pool.tensor_tensor(out=gu_lo[p][:, :, :, :], in0=gu_raw[:, :, :, :], in1=gu_hi[p][:, :, :, :].bitcast(F32),
                                   op=ALU.subtract), "gu_lo_done")

        def part(i, q):
            for fi in range(2):
                f = i * 2 + fi
                if not (known(f) and f == KF - 1):
                    low_up(f + 1, 1 - fi)
                if fi == 1:
                    pool.wait_ge(S["wd_hi_done"], i + 1)
                    out(pool.tensor_tensor(out=wd_lo[:, :, :], in0=wd_raw[:, :, :], in1=wd_hi[:, :, :].bitcast(F32),
                                           op=ALU.subtract), "wd_lo_done")
                for c in range(NC):
                    cols = slice(c * W, (c + 1) * W)
                    pool.wait_ge(S["hid_hi_done"], f * NC + c + 1)
                    out(pool.tensor_tensor(out=hid_lo[q][:, fi, cols], in0=e[c][:, :], in1=hid_hi[q][:, fi, cols].bitcast(F32),
                                           op=ALU.subtract), "hid_lo_done")

        pool.memset(start[:, 0:1], 0.0).then_inc(S["h_added"], 1)
        pool.memset(start[:, 1:2], 0.0).then_inc(S["h_added"], 1)
        low_up(0, 0)
        parts_in_loop(pool, part, PARTS - 2)
        part(PARTS - 2, 1)
        part(PARTS - 1, 0)

    @block.scalar
    def _(act):
        def high_up(f, p):
            act.wait_ge(gu_loaded, (f + 1) * 32)
            if not (known(f) and f < 2):
                act.wait_ge(S["up_ready"], (f - 1) * NC)
            out(act.activation(gu_hi[p][:, :, :, :], gu_raw[:, :, :, :], ACT.Copy), "gu_hi_done")

        def part(i, q):
            for fi in range(2):
                f = i * 2 + fi
                if not (known(f) and f == KF - 1):
                    high_up(f + 1, 1 - fi)
                for c in range(NC):
                    cols = slice(c * W, (c + 1) * W)
                    act.wait_ge(S["gate_ready"], f * NC + c + 1)
                    if not (known(f) and f == 0):
                        act.wait_ge(S["hid_lo_done"], f * NC + c - 2)
                    out(act.activation(e[c][:, :], ps[:, 2 * ((fi + c) % 2), 0:W], ACT.Exp, scale=-1.0), "exp_done")
                    if fi == 1 and c == 0:
                        act.wait_ge(wd_loaded, (i + 1) * 16)
                        if not (known(i) and i == 0):
                            act.wait_ge(S["down_ready"], i * TILES)
                        out(act.activation(wd_hi[:, :, :], wd_raw[:, :, :], ACT.Copy), "wd_hi_done")
                    act.wait_ge(S["v_ready"], f * NC + c + 1)
                    out(act.activation(hid_hi[q][:, fi, cols], e[c][:, :], ACT.Copy), "hid_hi_done")

        high_up(0, 0)
        parts_in_loop(act, part, PARTS - 2)
        part(PARTS - 2, 1)
        part(PARTS - 1, 0)

    @block.vector
    def _(dve):
        def add_down(i, q):
            for t in range(TILES):
                R = NS if t == 0 else P
                dve.wait_ge(S["down_ready"], i * TILES + t + 1)
                rows_ = h[0:R, t, :].rearrange("p (c n) -> p c n", c=2)
                bank = 4 + 2 * ((q + t) % 2)
                out(dve.tensor_tensor(out=rows_, in0=ps[0:R, bank:bank + 2, :], in1=rows_, op=ALU.add), "h_added")

        def part(i, q):
            for fi in range(2):
                f = i * 2 + fi
                if fi == 1 and not (known(i) and i == 0):
                    add_down(i - 1, 1 - q)
                for c in range(NC):
                    bank = 2 * ((fi + c) % 2)
                    dve.wait_ge(S["exp_done"], f * NC + c + 1)
                    dve_steps(dve, dve.tensor_scalar(e[c][:, :], e[c][:, :], 1.0, None, ALU.add))
                    dve_steps(dve, dve.reciprocal(e[c][:, :], e[c][:, :]))
                    dve_steps(dve, dve.tensor_tensor(out=e[c][:, :], in0=ps[:, bank, 0:W], in1=e[c][:, :], op=ALU.mult))
                    dve.wait_ge(S["up_ready"], f * NC + c + 1)
                    out(dve.tensor_tensor(out=e[c][:, :], in0=ps[:, bank + 1, 0:W], in1=e[c][:, :], op=ALU.mult), "v_ready")

        parts_in_loop(dve, part, PARTS, dve_steps, 4 * 3 * NC)
        add_down(PARTS - 1, 0)

    @block.tensor
    def _(pe):
        def hidden(f, fi):
            pe.wait_ge(S["gu_lo_done"], f + 1)
            for c in range(NC):
                cols = slice(c * W, (c + 1) * W)
                bank = 2 * ((fi + c) % 2)
                if not (known(f) and f * NC + c < 2):
                    pe.wait_ge(S["v_ready"], f * NC + c - 1)
                for j, name in enumerate(("gate_ready", "up_ready")):
                    for k in range(KD):
                        for w, x in ((gu_hi, nT_hi), (gu_hi, nT_lo), (gu_lo, nT_hi)):
                            ins = pe.matmul(ps[:, bank + j, 0:W], w[fi][:, j, k, :], x[:, k, cols],
                                            start=(k == 0 and w is gu_hi and x is nT_hi), stop=(k == KD - 1 and w is gu_lo))
                    out(ins, name)

        def down(i, q):
            pe.wait_ge(S["wd_lo_done"], i + 1)
            pe.wait_ge(S["hid_lo_done"], (i + 1) * 2 * NC)
            for t in range(TILES):
                R, col = (NS, SEQ) if t == 0 else (P, (t - 1) * P)
                bank = 4 + 2 * ((q + t) % 2)
                pe.wait_ge(S["h_added"], i * TILES + t + 1)
                for c in range(2):
                    cols = slice(c * 512, (c + 1) * 512)
                    for fi in range(2):
                        for x, w in ((hid_hi, wd_hi), (hid_hi, wd_lo), (hid_lo, wd_hi)):
                            ins = pe.matmul(ps[0:R, bank + c, :], x[q][:, fi, col:col + R], w[:, fi, cols],
                                            start=(fi == 0 and w is wd_hi and x is hid_hi), stop=(fi == 1 and x is hid_lo))
                out(ins, "down_ready")

        def part(i, q):
            hidden(i * 2, 0)
            if not (known(i) and i == 0):
                down(i - 1, 1 - q)
            hidden(i * 2 + 1, 1)

        parts_in_loop(pe, part, PARTS)
        down(PARTS - 1, 0)

    ctx.close()


def program(nc, a):
    d = lambda name, shape: nc.dram_tensor(name, shape, F32, kind="Internal").ap()
    s = {
        "ys": d("s_ys", (TOK, SW)), "v": d("s_v", (TOK, SW)), "qT": d("s_qT", (H, QK, TOK)), "kT": d("s_kT", (H, QK, TOK)),
        "s_z": d("s_z", (NS, SW)), "s_x": d("s_x", (NS, SW)), "s_bc": d("s_bc", (NS, 2 * P)),
        "att": d("s_att", (SEQ + NS, H * VD)), "s_dt": d("s_dt", (NS, SH)), "s_dta": d("s_dta", (NS, SH)), "s_y": d("s_y", (NS, SW)), "s_q": d("s_q", (NS, H, QK)), "s_k": d("s_k", (NS, H, QK)),
    }
    with nc.allow_non_contiguous_dma(reason="small vectors into columns"):
        tiles_block(nc, a, s)
        with ExitStack() as early:
            pages = Pages(nc, early, a, s)
            attention_block(nc, s, pages)
            samples_block(nc, a, s, pages)
        with (nc.sbuf_tensor("h", [P, NT + 1, D], F32) as h, nc.sbuf_tensor("nT_hi", [P, KD, SEQ + NS], F32R) as nT_hi,
              nc.sbuf_tensor("nT_lo", [P, KD, SEQ + NS], F32R) as nT_lo):
            mixing_block(nc, a, s, h, nT_hi, nT_lo)
            ffn_block(nc, a, h, nT_hi, nT_lo)
    return s


_OUTS = [
    ("y_prompt", (1, SEQ, D)), ("y_sample", (NS, 1, D)), ("kv_latent_prompt", (1, 1, T, KL)),
    ("k_rope_prompt", (1, 1, T, ROPE)), ("conv_prompt", (1, 1, 3, CONV)), ("ssm_prompt", (1, 1, SH, SP_, SN)),
    ("kv_latent_sample", (1, NS, 1, KL)), ("k_rope_sample", (1, NS, 1, ROPE)), ("conv_sample", (1, NS, 3, CONV)),
    ("ssm_sample", (1, NS, SH, SP_, SN)),
]


def rope_table(np):
    pos = np.zeros((P, NT + 1), np.float32)
    pos[0:META, 0] = np.arange(META)
    pos[META:ODD, 0] = NPG * PAGE
    pos[:, 1:] = META + np.arange(SEQ).reshape(NT, P).T
    inv = np.float32(10000.0) ** (-np.arange(HALF, dtype=np.float32) * np.float32(2.0 / ROPE))
    ang = (pos[:, :, None] * inv.astype(np.float32)).astype(np.float64)
    return np.concatenate([np.cos(ang), np.sin(ang)], axis=-1).astype(np.float32)


def kernel(**inputs):
    import numpy as np
    import concourse.bacc as bacc
    from concourse.bass_utils import run_bass_kernel_spmd

    nc = bacc.Bacc("TRN2", target_bir_lowering=False, num_devices=1)
    arrays = {"in_" + n: np.ascontiguousarray(v) for n, v in inputs.items()}
    arrays["in_rope_table"] = rope_table(np)
    a = {}
    for n, v in arrays.items():
        a[n[3:]] = nc.dram_tensor(n, v.shape, mybir.dt.from_np(v.dtype), kind="ExternalInput").ap()
    for n, shape in _OUTS:
        a[n] = nc.dram_tensor("out_" + n, shape, F32, kind="ExternalOutput").ap()
    program(nc, a)
    r = run_bass_kernel_spmd(nc, [arrays], core_ids=[0])
    return tuple(r.results[0]["out_" + n] for n, _ in _OUTS)
```
